# Optimizing a Trainium2 kernel written in Bass

```python
import math
import jax, jax.numpy as jnp
from jax import lax
import numpy as np

D_MODEL = 1024
BATCH = 1
SEQ = 1024
DEPTH = 1

PLE_DIM = 256
RMS_EPS = 1e-6

RWKV_HEADS = 8
RWKV_HEAD_DIM = 64
RWKV_WIDTH = RWKV_HEADS * RWKV_HEAD_DIM
DECAY_LORA = 64
AAA_LORA = 64
GATE_LORA = 128
GN_EPS = 64e-5
RWKV_COLS = 3 * RWKV_WIDTH + DECAY_LORA + AAA_LORA + GATE_LORA

DIFF_HEADS = 4
DIFF_HEAD_DIM = 64
DIFF_QK_WIDTH = DIFF_HEADS * 2 * DIFF_HEAD_DIM
DIFF_V_DIM = 2 * DIFF_HEAD_DIM
DIFF_V_WIDTH = DIFF_HEADS * DIFF_V_DIM
DIFF_COLS = 2 * DIFF_QK_WIDTH + DIFF_V_WIDTH
ROPE_THETA = 10000.0
Q_BLOCK = 128

GATE_COLS = 2 * D_MODEL
IN_COLS = RWKV_COLS + DIFF_COLS + GATE_COLS

N_GROUPS = 4
EXPERTS_PER_GROUP = 8
N_EXPERTS = N_GROUPS * EXPERTS_PER_GROUP
TOP_K = 2
EXPERT_FF = 512
ROW_BLOCK = 128


def rms_norm(x, gain, eps=RMS_EPS):
    xf = x.astype(jnp.float32)
    y = xf * lax.rsqrt(jnp.mean(xf * xf, axis=-1, keepdims=True) + eps)
    return (y * gain.astype(jnp.float32)).astype(x.dtype)

def rope_tables(seq, dim):
    inv = ROPE_THETA ** (-jnp.arange(0, dim, 2, dtype=jnp.float32) / dim)
    ang = jnp.arange(seq, dtype=jnp.float32)[:, None] * inv[None, :]
    ang = jnp.concatenate([ang, ang], axis=-1)
    return jnp.cos(ang), jnp.sin(ang)

def apply_rope(x, cos, sin):
    c = cos[:, None, None, :]
    s = sin[:, None, None, :]
    x1, x2 = jnp.split(x, 2, axis=-1)
    rot = jnp.concatenate([-x2, x1], axis=-1)
    return (x.astype(jnp.float32) * c + rot.astype(jnp.float32) * s).astype(x.dtype)

def wkv7_scan(r, decay, k, kk, a, v):
    b, s, h, n = r.shape

    def step(state, inp):
        r_t, w_t, k_t, kk_t, a_t, v_t = inp
        sa = jnp.einsum('bhvk,bhk->bhv', state, -kk_t)
        state = (state * w_t[:, :, None, :]
                 + sa[..., None] * (kk_t * a_t)[:, :, None, :]
                 + v_t[..., None] * k_t[:, :, None, :])
        return state, jnp.einsum('bhvk,bhk->bhv', state, r_t)

    s0 = jnp.zeros((b, h, n, n), jnp.float32)
    xs = (jnp.swapaxes(r, 0, 1), jnp.swapaxes(decay, 0, 1), jnp.swapaxes(k, 0, 1),
          jnp.swapaxes(kk, 0, 1), jnp.swapaxes(a, 0, 1), jnp.swapaxes(v, 0, 1))
    _, y = lax.scan(step, s0, xs)
    return jnp.swapaxes(y, 0, 1)

def rwkv7_branch(pr, mu, w0, w2, a0, a2, g2, k_k, k_a, r_k, ln_w, ln_b):
    b, s, _ = pr.shape
    f32 = jnp.float32
    prev = jnp.pad(pr[:, :-1], ((0, 0), (1, 0), (0, 0)))
    xs = pr + (prev - pr) * mu
    c0 = RWKV_WIDTH
    r, k, v, xw, xa, xg = jnp.split(
        xs, [c0, 2 * c0, 3 * c0, 3 * c0 + DECAY_LORA, 3 * c0 + DECAY_LORA + AAA_LORA], axis=-1)
    w_log = -jax.nn.softplus(-(w0 + jnp.tanh(xw) @ w2).astype(f32)) - 0.5
    decay = jnp.exp(-jnp.exp(w_log))
    a = jax.nn.sigmoid((a0 + xa @ a2).astype(f32))
    g = jax.nn.sigmoid(xg) @ g2

    def heads(t):
        return t.reshape(b, s, RWKV_HEADS, RWKV_HEAD_DIM).astype(f32)

    kk = heads(k * k_k)
    kk = kk / jnp.maximum(jnp.sqrt(jnp.sum(kk * kk, axis=-1, keepdims=True)), 1e-12)
    k_mod = k.astype(f32) * (1.0 + (a - 1.0) * k_a.astype(f32))
    r_h, k_h, v_h = heads(r), heads(k_mod), heads(v)
    y = wkv7_scan(r_h, heads(decay), k_h, kk, heads(a), v_h)
    mean = jnp.mean(y, axis=-1, keepdims=True)
    var = jnp.mean(jnp.square(y - mean), axis=-1, keepdims=True)
    y = ((y - mean) * lax.rsqrt(var + GN_EPS)).reshape(b, s, RWKV_WIDTH)
    y = y * ln_w.astype(f32) + ln_b.astype(f32)
    bonus = jnp.sum(r_h * k_h * r_k.astype(f32), axis=-1, keepdims=True) * v_h
    out = (y + bonus.reshape(b, s, RWKV_WIDTH)) * g.astype(f32)
    return out.astype(pr.dtype)

def diff_attention_branch(pd, q_gain, k_gain, lq1, lk1, lq2, lk2, subln_w, lam_init, cos, sin):
    b, s, _ = pd.shape
    f32 = jnp.float32
    q, k, v = jnp.split(pd, [DIFF_QK_WIDTH, 2 * DIFF_QK_WIDTH], axis=-1)
    q = apply_rope(rms_norm(q.reshape(b, s, DIFF_HEADS, 2, DIFF_HEAD_DIM), q_gain), cos, sin)
    k = apply_rope(rms_norm(k.reshape(b, s, DIFF_HEADS, 2, DIFF_HEAD_DIM), k_gain), cos, sin)
    q = q.transpose(0, 2, 3, 1, 4)
    k = k.transpose(0, 2, 3, 1, 4)
    v = v.reshape(b, s, DIFF_HEADS, DIFF_V_DIM).transpose(0, 2, 1, 3)
    lam = (jnp.exp(jnp.sum(lq1.astype(f32) * lk1.astype(f32)))
           - jnp.exp(jnp.sum(lq2.astype(f32) * lk2.astype(f32))) + lam_init)
    scale = DIFF_HEAD_DIM ** -0.5
    neg = jnp.finfo(f32).min
    blocks = []
    for i in range(s // Q_BLOCK):
        q0 = i * Q_BLOCK
        end = q0 + Q_BLOCK
        sc = jnp.einsum('bhcqd,bhckd->bhcqk', q[:, :, :, q0:end], k[:, :, :, :end]).astype(f32) * scale
        causal = jnp.arange(end)[None, :] <= (q0 + jnp.arange(Q_BLOCK))[:, None]
        prob = jax.nn.softmax(jnp.where(causal, sc, neg), axis=-1)
        attn = prob[:, :, 0] - lam * prob[:, :, 1]
        blocks.append(jnp.einsum('bhqk,bhkv->bhqv', attn.astype(v.dtype), v[:, :, :end]))
    o = jnp.concatenate(blocks, axis=2)
    o = rms_norm(o, subln_w) * (1.0 - lam_init)
    return o.transpose(0, 2, 1, 3).reshape(b, s, DIFF_V_WIDTH)

def hierarchical_moe(h, w_group, b_group, w_er, b_er, w_gate, w_up, w_down):
    b, s, d = h.shape
    t = b * s
    f32 = jnp.float32
    hf = h.reshape(t, d)
    g_prob = jax.nn.softmax((hf @ w_group).astype(f32) + b_group.astype(f32), axis=-1)
    g_top, g_idx = lax.top_k(g_prob, 1)
    e_logits = ((hf @ w_er).astype(f32) + b_er.astype(f32)).reshape(t, N_GROUPS, EXPERTS_PER_GROUP)
    sel = jnp.broadcast_to(g_idx[:, :, None], (t, 1, EXPERTS_PER_GROUP))
    e_logits = jnp.take_along_axis(e_logits, sel, axis=1)[:, 0]
    e_top, e_idx = lax.top_k(e_logits, TOP_K)
    weights = g_top * jax.nn.softmax(e_top, axis=-1)
    expert_id = g_idx * EXPERTS_PER_GROUP + e_idx

    n_assign = t * TOP_K
    eid = expert_id.reshape(n_assign).astype(jnp.int32)
    tid = jnp.repeat(jnp.arange(t, dtype=jnp.int32), TOP_K)
    wt = weights.reshape(n_assign)
    order = jnp.argsort(eid)
    se = eid[order]
    counts = jnp.bincount(eid, length=N_EXPERTS).astype(jnp.int32)
    starts = jnp.cumsum(counts) - counts
    pcounts = ((counts + ROW_BLOCK - 1) // ROW_BLOCK) * ROW_BLOCK
    pends = jnp.cumsum(pcounts)
    pstarts = pends - pcounts
    dest = pstarts[se] + (jnp.arange(n_assign, dtype=jnp.int32) - starts[se])
    rows = n_assign + N_EXPERTS * ROW_BLOCK
    n_blocks = rows // ROW_BLOCK
    buf_tok = jnp.full((rows,), t, jnp.int32).at[dest].set(tid[order])
    buf_w = jnp.zeros((rows,), wt.dtype).at[dest].set(wt[order])
    blk_e = jnp.minimum(jnp.searchsorted(pends, jnp.arange(n_blocks, dtype=jnp.int32) * ROW_BLOCK,
                                         side='right'), N_EXPERTS - 1)
    hpad = jnp.concatenate([hf, jnp.zeros((1, d), hf.dtype)], axis=0)
    xs = hpad[buf_tok].reshape(n_blocks, ROW_BLOCK, d)

    def expert_block(args):
        xb, e = args
        return (jax.nn.silu(xb @ w_gate[e]) * (xb @ w_up[e])) @ w_down[e]

    yb = lax.map(expert_block, (xs, blk_e)).reshape(rows, d)
    yb = yb * buf_w[:, None].astype(yb.dtype)
    out = jax.ops.segment_sum(yb, buf_tok, num_segments=t + 1)[:t]
    return out.reshape(b, s, d)

def first_inputs(seed: int = 0) -> dict:
    key = jax.random.key(seed)
    ks = iter(jax.random.split(key, 40))
    L = DEPTH
    f32 = jnp.float32

    def nrm(shape, scale):
        return scale * jax.random.normal(next(ks), shape, f32)

    def gain(shape, base=1.0):
        return base + 0.1 * jax.random.normal(next(ks), shape, f32)

    return {
        'x': nrm((BATCH, SEQ, D_MODEL), 1.0),
        'p': nrm((L, BATCH, SEQ, PLE_DIM), 1.0),
        'norm_mix': gain((L, D_MODEL)),
        'w_in': nrm((L, D_MODEL, IN_COLS), D_MODEL ** -0.5),
        'rwkv_mu': jax.random.uniform(next(ks), (L, RWKV_COLS), f32),
        'rwkv_w0': jax.random.uniform(next(ks), (L, RWKV_WIDTH), f32, -6.0, 0.0),
        'rwkv_w2': nrm((L, DECAY_LORA, RWKV_WIDTH), DECAY_LORA ** -0.5),
        'rwkv_a0': nrm((L, RWKV_WIDTH), 0.5),
        'rwkv_a2': nrm((L, AAA_LORA, RWKV_WIDTH), AAA_LORA ** -0.5),
        'rwkv_g2': nrm((L, GATE_LORA, RWKV_WIDTH), GATE_LORA ** -0.5),
        'rwkv_k_k': gain((L, RWKV_WIDTH), 0.85),
        'rwkv_k_a': gain((L, RWKV_WIDTH)),
        'rwkv_r_k': gain((L, RWKV_HEADS, RWKV_HEAD_DIM), 0.5),
        'rwkv_ln_w': gain((L, RWKV_WIDTH)),
        'rwkv_ln_b': nrm((L, RWKV_WIDTH), 0.02),
        'q_norm': gain((L, DIFF_HEAD_DIM)),
        'k_norm': gain((L, DIFF_HEAD_DIM)),
        'lambda_q1': nrm((L, DIFF_HEAD_DIM), 0.1),
        'lambda_k1': nrm((L, DIFF_HEAD_DIM), 0.1),
        'lambda_q2': nrm((L, DIFF_HEAD_DIM), 0.1),
        'lambda_k2': nrm((L, DIFF_HEAD_DIM), 0.1),
        'subln_w': gain((L, DIFF_V_DIM)),
        'w_branch_rwkv': nrm((L, RWKV_WIDTH, D_MODEL), RWKV_WIDTH ** -0.5),
        'w_branch_diff': nrm((L, DIFF_V_WIDTH, D_MODEL), DIFF_V_WIDTH ** -0.5),
        'w_out': nrm((L, D_MODEL, D_MODEL), D_MODEL ** -0.5),
        'norm_ffn': gain((L, D_MODEL)),
        'w_group': nrm((L, D_MODEL, N_GROUPS), D_MODEL ** -0.5),
        'b_group': nrm((L, N_GROUPS), 0.01),
        'w_expert_router': nrm((L, D_MODEL, N_EXPERTS), D_MODEL ** -0.5),
        'b_expert_router': nrm((L, N_EXPERTS), 0.01),
        'w_gate': nrm((L, N_EXPERTS, D_MODEL, EXPERT_FF), D_MODEL ** -0.5),
        'w_up': nrm((L, N_EXPERTS, D_MODEL, EXPERT_FF), D_MODEL ** -0.5),
        'w_down': nrm((L, N_EXPERTS, EXPERT_FF, D_MODEL), EXPERT_FF ** -0.5),
        'norm_ple': gain((L, D_MODEL)),
        'w_ple_gate': nrm((L, D_MODEL, D_MODEL), D_MODEL ** -0.5),
        'w_ple_proj': nrm((L, PLE_DIM, D_MODEL), PLE_DIM ** -0.5),
    }

def first_block(x, p, norm_mix, w_in, rwkv_mu, rwkv_w0, rwkv_w2, rwkv_a0, rwkv_a2, rwkv_g2,
              rwkv_k_k, rwkv_k_a, rwkv_r_k, rwkv_ln_w, rwkv_ln_b, q_norm, k_norm,
              lambda_q1, lambda_k1, lambda_q2, lambda_k2, subln_w, w_branch_rwkv,
              w_branch_diff, w_out, norm_ffn, w_group, b_group, w_expert_router,
              b_expert_router, w_gate, w_up, w_down, norm_ple, w_ple_gate, w_ple_proj):
    seq = x.shape[1]
    cos, sin = rope_tables(seq, DIFF_HEAD_DIM)
    for l in range(DEPTH):
        lam_init = 0.8 - 0.6 * math.exp(-0.3 * l)
        h = rms_norm(x, norm_mix[l])
        proj = h @ w_in[l]
        p_rwkv = proj[..., :RWKV_COLS]
        p_diff = proj[..., RWKV_COLS:RWKV_COLS + DIFF_COLS]
        g_rwkv, g_diff = jnp.split(proj[..., RWKV_COLS + DIFF_COLS:], 2, axis=-1)
        o_rwkv = rwkv7_branch(p_rwkv, rwkv_mu[l], rwkv_w0[l], rwkv_w2[l], rwkv_a0[l], rwkv_a2[l],
                              rwkv_g2[l], rwkv_k_k[l], rwkv_k_a[l], rwkv_r_k[l], rwkv_ln_w[l],
                              rwkv_ln_b[l])
        o_diff = diff_attention_branch(p_diff, q_norm[l], k_norm[l], lambda_q1[l], lambda_k1[l],
                                       lambda_q2[l], lambda_k2[l], subln_w[l], lam_init, cos, sin)
        mixed = (jax.nn.sigmoid(g_rwkv) * (o_rwkv @ w_branch_rwkv[l])
                 + jax.nn.sigmoid(g_diff) * (o_diff @ w_branch_diff[l]))
        x = x + mixed @ w_out[l]
        x = x + hierarchical_moe(rms_norm(x, norm_ffn[l]), w_group[l], b_group[l],
                                 w_expert_router[l], b_expert_router[l], w_gate[l], w_up[l],
                                 w_down[l])
        ple_gate = jax.nn.sigmoid(rms_norm(x, norm_ple[l]) @ w_ple_gate[l])
        x = x + ple_gate * (p[l] @ w_ple_proj[l])
    return x


MIX_WIDTH = 2 * D_MODEL
SSD_WIDTH = MIX_WIDTH // 2
SSD_HEAD_DIM = 64
SSD_HEADS = SSD_WIDTH // SSD_HEAD_DIM
SSD_GROUPS = 2
SSD_HEADS_PER_GROUP = SSD_HEADS // SSD_GROUPS
SSD_STATE = 128
SSD_CONV = 4
SSD_CHUNK = 128
SSD_CONV_DIM = SSD_WIDTH + 2 * SSD_GROUPS * SSD_STATE
HGRN_WIDTH = MIX_WIDTH // 4
HGRN_HEAD_DIM = 128
HGRN_HEADS = HGRN_WIDTH // HGRN_HEAD_DIM
HGRN_CHUNK = 64
S5_WIDTH = MIX_WIDTH - SSD_WIDTH - HGRN_WIDTH
S5_GROUP_SIZE = 16
S5_GROUPS = S5_WIDTH // S5_GROUP_SIZE
S5_STATE = 64
S5_MIN_NEG = 1e-4

IN_COLS_2 = SSD_WIDTH + SSD_CONV_DIM + SSD_HEADS + 4 * HGRN_WIDTH + 2 * S5_WIDTH
EPS = 1e-6


def _in_proj_splits():
    widths = [SSD_WIDTH, SSD_CONV_DIM, SSD_HEADS, HGRN_WIDTH, HGRN_WIDTH,
              HGRN_WIDTH, HGRN_WIDTH, S5_WIDTH, S5_WIDTH]
    pts, acc = [], 0
    for w in widths[:-1]:
        acc += w
        pts.append(acc)
    return pts

def rms_norm_2(x, w):
    xf = x.astype(jnp.float32)
    y = xf * lax.rsqrt(jnp.mean(xf * xf, axis=-1, keepdims=True) + EPS)
    return (y * w.astype(jnp.float32)).astype(x.dtype)

def grouped_rms_norm(x, w, n_groups):
    shp = x.shape
    xf = x.astype(jnp.float32).reshape(shp[:-1] + (n_groups, shp[-1] // n_groups))
    y = xf * lax.rsqrt(jnp.mean(xf * xf, axis=-1, keepdims=True) + EPS)
    return (y.reshape(shp) * w.astype(jnp.float32)).astype(x.dtype)

def causal_depthwise_conv(x, w, b):
    out = lax.conv_general_dilated(
        x, w[:, None, :].astype(x.dtype), window_strides=(1,),
        padding=[(SSD_CONV - 1, 0)], dimension_numbers=("NWC", "WIO", "NWC"),
        feature_group_count=x.shape[-1])
    return out + b.astype(x.dtype)

def ssd_mixer(z, xbc, dt_raw, conv_w, conv_b, dt_bias, a_log, d_skip, norm_w):
    bsz, seqlen, _ = xbc.shape
    nc = seqlen // SSD_CHUNK
    G, R, P, N, T = SSD_GROUPS, SSD_HEADS_PER_GROUP, SSD_HEAD_DIM, SSD_STATE, SSD_CHUNK
    xbc = jax.nn.silu(causal_depthwise_conv(xbc, conv_w, conv_b))
    xs, b_in, c_in = jnp.split(xbc, [SSD_WIDTH, SSD_WIDTH + G * N], axis=-1)
    xs = xs.reshape(bsz, nc, T, G, R, P)
    b_in = b_in.reshape(bsz, nc, T, G, N)
    c_in = c_in.reshape(bsz, nc, T, G, N)
    dt = jax.nn.softplus(dt_raw.astype(jnp.float32) + dt_bias.astype(jnp.float32))
    dt = dt.reshape(bsz, nc, T, G, R)
    a = -jnp.exp(a_log.astype(jnp.float32)).reshape(G, R)
    a_cum = jnp.cumsum(dt * a, axis=2)
    mask = jnp.tril(jnp.ones((T, T), dtype=bool))[:, :, None, None]
    seg = a_cum[:, :, :, None] - a_cum[:, :, None, :]
    decay = jnp.exp(jnp.where(mask, seg, -jnp.inf))
    x_dt = xs * dt[..., None]
    scores = jnp.einsum("bclgn,bcsgn->bclsg", c_in, b_in)
    y_diag = jnp.einsum("bclsg,bclsgr,bcsgrp->bclgrp", scores, decay, x_dt)
    decay_to_end = jnp.exp(a_cum[:, :, -1:] - a_cum)
    chunk_states = jnp.einsum("bclgn,bclgr,bclgrp->bcgrpn", b_in, decay_to_end, x_dt)
    chunk_decay = jnp.exp(a_cum[:, :, -1])

    def step(h, inp):
        dec, st = inp
        return dec[..., None, None] * h + st, h

    h0 = jnp.zeros((bsz, G, R, P, N), chunk_states.dtype)
    _, prev = lax.scan(step, h0, (jnp.moveaxis(chunk_decay, 1, 0),
                                  jnp.moveaxis(chunk_states, 1, 0)))
    prev = jnp.moveaxis(prev, 0, 1)
    y_off = jnp.einsum("bclgn,bcgrpn,bclgr->bclgrp", c_in, prev, jnp.exp(a_cum))
    y = y_diag + y_off + d_skip.reshape(G, R)[:, :, None] * xs
    y = y.reshape(bsz, seqlen, SSD_WIDTH)
    return grouped_rms_norm(y * jax.nn.silu(z), norm_w, SSD_GROUPS)

def hgrn2_mixer(q, f_raw, i_in, g, lb, norm_w):
    bsz, seqlen, _ = q.shape
    nc = seqlen // HGRN_CHUNK
    H, Dh, T = HGRN_HEADS, HGRN_HEAD_DIM, HGRN_CHUNK
    q = jax.nn.silu(q)
    lbf = lb.astype(jnp.float32)
    log_f = jnp.logaddexp(jnp.log(lbf), jnp.log1p(-lbf) + jax.nn.log_sigmoid(f_raw.astype(jnp.float32)))
    k = -jnp.expm1(log_f)

    def to_chunks(t):
        return t.reshape(bsz, nc, T, H, Dh).transpose(1, 0, 3, 2, 4)

    mask = jnp.tril(jnp.ones((T, T), dtype=bool))[:, :, None]

    def step(state, inp):
        qc, kc, vc, lfc = inp
        cum = jnp.cumsum(lfc, axis=2)
        decay = jnp.exp(jnp.where(mask, cum[:, :, :, None, :] - cum[:, :, None, :, :], -jnp.inf))
        attn = jnp.einsum("bhlk,bhsk,bhlsk->bhls", qc, kc, decay)
        o = (jnp.einsum("bhls,bhsv->bhlv", attn, vc)
             + jnp.einsum("bhlk,bhkv->bhlv", qc * jnp.exp(cum), state))
        last = cum[:, :, -1:, :]
        state = (jnp.exp(last[:, :, 0, :])[..., None] * state
                 + jnp.einsum("bhsk,bhsv->bhkv", kc * jnp.exp(last - cum), vc))
        return state, o

    state0 = jnp.zeros((bsz, H, Dh, Dh), jnp.float32)
    _, o = lax.scan(step, state0, (to_chunks(q), to_chunks(k), to_chunks(i_in), to_chunks(log_f)))
    o = o.transpose(1, 0, 3, 2, 4).reshape(bsz, seqlen, HGRN_WIDTH)
    return grouped_rms_norm(o, norm_w, HGRN_HEADS) * jax.nn.silu(g)

def s5_mixer(u, gate, lam_re, lam_im, log_step, b_re, b_im, c_re, c_im, d_skip, glu_w, glu_b, norm_w):
    bsz, seqlen, _ = u.shape
    G, P, Hg = S5_GROUPS, S5_STATE, S5_GROUP_SIZE
    uf = u.astype(jnp.float32)
    lr = jnp.minimum(lam_re.astype(jnp.float32), -S5_MIN_NEG)
    li = lam_im.astype(jnp.float32)
    step = jnp.exp(log_step.astype(jnp.float32))[:, None]
    mag = jnp.exp(lr * step)
    ang = li * step
    ab_re, ab_im = mag * jnp.cos(ang), mag * jnp.sin(ang)
    den = lr * lr + li * li
    num_re, num_im = ab_re - 1.0, ab_im
    co_re = (num_re * lr + num_im * li) / den
    co_im = (num_im * lr - num_re * li) / den
    bb_re = co_re[..., None] * b_re - co_im[..., None] * b_im
    bb_im = co_re[..., None] * b_im + co_im[..., None] * b_re
    ug = uf.reshape(bsz, seqlen, G, Hg)
    bu_re = jnp.einsum("blgh,gph->lbgp", ug, bb_re)
    bu_im = jnp.einsum("blgh,gph->lbgp", ug, bb_im)
    a_re = jnp.broadcast_to(ab_re, (seqlen, 1, G, P))
    a_im = jnp.broadcast_to(ab_im, (seqlen, 1, G, P))

    def combine(e_i, e_j):
        ar_i, ai_i, br_i, bi_i = e_i
        ar_j, ai_j, br_j, bi_j = e_j
        return (ar_j * ar_i - ai_j * ai_i,
                ar_j * ai_i + ai_j * ar_i,
                ar_j * br_i - ai_j * bi_i + br_j,
                ar_j * bi_i + ai_j * br_i + bi_j)

    _, _, s_re, s_im = lax.associative_scan(combine, (a_re, a_im, bu_re, bu_im), axis=0)
    y = jnp.einsum("lbgp,ghp->blgh", s_re, c_re) - jnp.einsum("lbgp,ghp->blgh", s_im, c_im)
    y = y.reshape(bsz, seqlen, S5_WIDTH) + d_skip * uf
    y = jax.nn.gelu(y)
    hg = y @ glu_w + glu_b
    val, gt = jnp.split(hg, 2, axis=-1)
    y = val * jax.nn.sigmoid(gt) * jax.nn.silu(gate)
    return rms_norm_2(y, norm_w)

def second_inputs(seed: int = 0) -> dict:
    key = jax.random.key(seed)
    ks = jax.random.split(key, 24)
    f32 = jnp.float32
    nrm = lambda k, shp, s: s * jax.random.normal(k, shp, f32)
    dt0 = jnp.exp(jax.random.uniform(ks[6], (DEPTH, SSD_HEADS), f32, math.log(1e-3), math.log(1e-1)))
    lam_im0 = math.pi * jnp.arange(S5_STATE, dtype=f32)
    return {
        "x": jax.random.normal(ks[0], (BATCH, SEQ, D_MODEL), f32),
        "pre_norm_w": 1.0 + nrm(ks[1], (DEPTH, D_MODEL), 0.02),
        "post_norm_w": 1.0 + nrm(ks[2], (DEPTH, D_MODEL), 0.02),
        "w_in": nrm(ks[3], (DEPTH, D_MODEL, IN_COLS_2), D_MODEL ** -0.5),
        "w_out": nrm(ks[4], (DEPTH, MIX_WIDTH, D_MODEL), MIX_WIDTH ** -0.5),
        "ssd_conv_w": nrm(ks[5], (DEPTH, SSD_CONV, SSD_CONV_DIM), SSD_CONV ** -0.5),
        "ssd_conv_b": nrm(ks[7], (DEPTH, SSD_CONV_DIM), 0.02),
        "ssd_dt_bias": dt0 + jnp.log(-jnp.expm1(-dt0)),
        "ssd_a_log": jnp.log(jax.random.uniform(ks[8], (DEPTH, SSD_HEADS), f32, 1.0, 16.0)),
        "ssd_d": 1.0 + nrm(ks[9], (DEPTH, SSD_HEADS), 0.02),
        "ssd_norm_w": 1.0 + nrm(ks[10], (DEPTH, SSD_WIDTH), 0.02),
        "hgrn_lower_bounds": nrm(ks[11], (DEPTH, HGRN_WIDTH), 0.1),
        "hgrn_norm_w": 1.0 + nrm(ks[12], (DEPTH, HGRN_WIDTH), 0.02),
        "s5_lambda_re": -0.5 + nrm(ks[13], (DEPTH, S5_GROUPS, S5_STATE), 0.01),
        "s5_lambda_im": lam_im0 + nrm(ks[14], (DEPTH, S5_GROUPS, S5_STATE), 0.01),
        "s5_log_step": jax.random.uniform(ks[15], (DEPTH, S5_GROUPS), f32, math.log(1e-3), math.log(1e-1)),
        "s5_b_re": nrm(ks[16], (DEPTH, S5_GROUPS, S5_STATE, S5_GROUP_SIZE), (2 * S5_GROUP_SIZE) ** -0.5),
        "s5_b_im": nrm(ks[17], (DEPTH, S5_GROUPS, S5_STATE, S5_GROUP_SIZE), (2 * S5_GROUP_SIZE) ** -0.5),
        "s5_c_re": nrm(ks[18], (DEPTH, S5_GROUPS, S5_GROUP_SIZE, S5_STATE), S5_STATE ** -0.5),
        "s5_c_im": nrm(ks[19], (DEPTH, S5_GROUPS, S5_GROUP_SIZE, S5_STATE), S5_STATE ** -0.5),
        "s5_d": jax.random.normal(ks[20], (DEPTH, S5_WIDTH), f32),
        "s5_glu_w": nrm(ks[21], (DEPTH, S5_WIDTH, 2 * S5_WIDTH), S5_WIDTH ** -0.5),
        "s5_glu_b": nrm(ks[22], (DEPTH, 2 * S5_WIDTH), 0.02),
        "s5_norm_w": 1.0 + nrm(ks[23], (DEPTH, S5_WIDTH), 0.02),
    }

def second_block(x, pre_norm_w, post_norm_w, w_in, w_out, ssd_conv_w, ssd_conv_b, ssd_dt_bias,
              ssd_a_log, ssd_d, ssd_norm_w, hgrn_lower_bounds, hgrn_norm_w, s5_lambda_re,
              s5_lambda_im, s5_log_step, s5_b_re, s5_b_im, s5_c_re, s5_c_im, s5_d, s5_glu_w,
              s5_glu_b, s5_norm_w):
    lb_all = jnp.cumsum(jax.nn.softmax(hgrn_lower_bounds.astype(jnp.float32), axis=0), axis=0)
    lb_all = lb_all - lb_all[0:1]
    splits = _in_proj_splits()
    for l in range(DEPTH):
        h = rms_norm_2(x, pre_norm_w[l])
        proj = h @ w_in[l]
        z, xbc, dt_raw, q, f_raw, i_in, g, u, s5_gate = jnp.split(proj, splits, axis=-1)
        y_ssd = ssd_mixer(z, xbc, dt_raw, ssd_conv_w[l], ssd_conv_b[l], ssd_dt_bias[l],
                          ssd_a_log[l], ssd_d[l], ssd_norm_w[l])
        y_hgrn = hgrn2_mixer(q, f_raw, i_in, g, lb_all[l], hgrn_norm_w[l])
        y_s5 = s5_mixer(u, s5_gate, s5_lambda_re[l], s5_lambda_im[l], s5_log_step[l],
                        s5_b_re[l], s5_b_im[l], s5_c_re[l], s5_c_im[l], s5_d[l],
                        s5_glu_w[l], s5_glu_b[l], s5_norm_w[l])
        mix = jnp.concatenate([y_ssd, y_hgrn, y_s5], axis=-1).astype(x.dtype)
        x = x + rms_norm_2(mix @ w_out[l], post_norm_w[l])
    return x


_first_inputs = second_inputs


def second_inputs(seed=0):
    import zlib

    import numpy as np

    out = dict(_first_inputs(seed))
    spreads = {}
    factors = {'post_norm_w': 31.424,
     'ssd_conv_b': 3.769,
     'ssd_d': 153.159,
     'ssd_norm_w': 129.666,
     'hgrn_norm_w': 200.0,
     's5_lambda_re': 200.0,
     's5_glu_b': 4.563,
     's5_norm_w': 180.005,
     's5_lambda_im': 21.584,
     's5_log_step': 23.04,
     's5_b_re': 30.104,
     's5_b_im': 30.168,
     's5_c_re': 30.064,
     's5_c_im': 30.288,
     'ssd_dt_bias': 6.452,
     'ssd_a_log': 5.952}
    for name, (base, spread) in spreads.items():
        noise = np.random.default_rng([zlib.crc32(name.encode()), seed]).standard_normal(out[name].shape)
        drawn = base * np.exp(spread * noise) if base else spread * noise
        out[name] = __import__('jax').numpy.asarray(drawn.astype(out[name].dtype))
    for name, factor in factors.items():
        out[name] = (out[name] * factor).astype(out[name].dtype)
    return out


_narrow_inputs = second_inputs


def second_inputs(seed=0):
    out = dict(_narrow_inputs(seed))
    wider = {'post_norm_w': 3.13,
     'ssd_dt_bias': 12.0,
     'ssd_a_log': 12.0,
     'ssd_d': 4.81,
     'ssd_norm_w': 5.16,
     'hgrn_norm_w': 7.7,
     's5_norm_w': 5.16}
    for name, times in wider.items():
        mean = out[name].mean()
        out[name] = (mean + times * (out[name] - mean)).astype(out[name].dtype)
    return out


def setup_inputs(seed=0):
    out = dict(first_inputs(seed))
    for name, value in second_inputs(seed + 1).items():
        if name != "x":
            out[name + "_2"] = value
    return out


def reference(
    x, p, norm_mix, w_in, rwkv_mu, rwkv_w0, rwkv_w2, rwkv_a0, rwkv_a2, rwkv_g2, rwkv_k_k,
    rwkv_k_a, rwkv_r_k, rwkv_ln_w, rwkv_ln_b, q_norm, k_norm, lambda_q1, lambda_k1, lambda_q2,
    lambda_k2, subln_w, w_branch_rwkv, w_branch_diff, w_out, norm_ffn, w_group, b_group,
    w_expert_router, b_expert_router, w_gate, w_up, w_down, norm_ple, w_ple_gate, w_ple_proj,
    pre_norm_w_2, post_norm_w_2, w_in_2, w_out_2, ssd_conv_w_2, ssd_conv_b_2, ssd_dt_bias_2,
    ssd_a_log_2, ssd_d_2, ssd_norm_w_2, hgrn_lower_bounds_2, hgrn_norm_w_2, s5_lambda_re_2,
    s5_lambda_im_2, s5_log_step_2, s5_b_re_2, s5_b_im_2, s5_c_re_2, s5_c_im_2, s5_d_2,
    s5_glu_w_2, s5_glu_b_2, s5_norm_w_2,
):
    x = first_block(
        x, p, norm_mix, w_in, rwkv_mu, rwkv_w0, rwkv_w2, rwkv_a0, rwkv_a2, rwkv_g2, rwkv_k_k,
        rwkv_k_a, rwkv_r_k, rwkv_ln_w, rwkv_ln_b, q_norm, k_norm, lambda_q1, lambda_k1,
        lambda_q2, lambda_k2, subln_w, w_branch_rwkv, w_branch_diff, w_out, norm_ffn, w_group,
        b_group, w_expert_router, b_expert_router, w_gate, w_up, w_down, norm_ple, w_ple_gate,
        w_ple_proj,
    )
    return second_block(
        x, pre_norm_w_2, post_norm_w_2, w_in_2, w_out_2, ssd_conv_w_2, ssd_conv_b_2,
        ssd_dt_bias_2, ssd_a_log_2, ssd_d_2, ssd_norm_w_2, hgrn_lower_bounds_2, hgrn_norm_w_2,
        s5_lambda_re_2, s5_lambda_im_2, s5_log_step_2, s5_b_re_2, s5_b_im_2, s5_c_re_2,
        s5_c_im_2, s5_d_2, s5_glu_w_2, s5_glu_b_2, s5_norm_w_2,
    )


_drawn_inputs = setup_inputs


def setup_inputs(seed=0):
    import zlib

    import numpy as np

    out = dict(_drawn_inputs(seed))
    spreads = {}
    factors = {'rwkv_ln_b': 3.526,
     'lambda_q2': 2.694,
     'lambda_k2': 3.577,
     'b_group': 3.005,
     'b_expert_router': 2.769}
    for name, (base, spread) in spreads.items():
        noise = np.random.default_rng([zlib.crc32(name.encode()), seed]).standard_normal(out[name].shape)
        drawn = base * np.exp(spread * noise) if base else spread * noise
        out[name] = __import__('jax').numpy.asarray(drawn.astype(out[name].dtype))
    for name, factor in factors.items():
        out[name] = (out[name] * factor).astype(out[name].dtype)
    return out
```

```python
import math
from contextlib import ExitStack

import numpy as np
import concourse.bass as bass
from concourse import mybir

F32 = mybir.dt.float32
I32 = mybir.dt.int32
U32 = mybir.dt.uint32
ALU = mybir.AluOpType
ACT = mybir.ActivationFunctionType
AX = mybir.AxisListType.X

P = 128
D = 1024
SEQ = 1024
NT = SEQ // P
KD = D // P
EPS = 1e-6


class Steps:

    def __init__(self, sem, names, base):
        self.base = base
        self.sem = sem
        self.names = names.split() if isinstance(names, str) else list(names)
        assert len(set(self.names)) == len(self.names)
        self.last = -1

    def step(self, name):
        self.last += 1
        assert self.names[self.last % len(self.names)] == name, (self.names[self.last % len(self.names)], name)
        return 1

    def at(self, name, turn=0):
        return turn * len(self.names) + (self.names.index(name) + 1 + self.base)

    def begin(self, eng):
        assert self.base == 1
        eng.sem_inc(self.sem, 1)

    def start(self, turn):
        return turn * len(self.names) + self.base


class Count:

    def __init__(self, sem):
        self.sem = sem

    def begin(self, eng):
        eng.sem_inc(self.sem, 2)

    def done(self, t):
        return t + 3


def each_tile(eng, body):
    body(0, 0, 0)
    with eng.Fori(0, NT // 2 - 1) as j:
        body(2 * j + 1, 1, j)
        body(2 * j + 2, 0, j + 1)
    body(NT - 1, 1, NT // 2 - 1)


def first(t):
    return isinstance(t, int) and t == 0


def last(t):
    return isinstance(t, int) and t == NT - 1


class Phase:

    def __init__(self, nc, name):
        self.nc, self.name, self.ctx, self.sems = nc, name, ExitStack(), []

    def __enter__(self):
        self.ctx.__enter__()
        return self

    def __exit__(self, *a):
        self.ctx.__exit__(*a)
        self.nc.clear_and_free_semaphores(self.sems)
        self.nc.all_engine_barrier()

    def sb(self, name, shape, dt=F32):
        return self.ctx.enter_context(self.nc.sbuf_tensor(f"{self.name}_sb_{name}", shape, dt))

    def psum(self, name="psum"):
        return self.ctx.enter_context(self.nc.psum_tensor(f"{self.name}_{name}", [P, 8, 512], F32))

    def sem(self, name):
        self.sems.append(self.nc.alloc_semaphore(f"{self.name}_{name}"))
        return self.sems[-1]

    def steps(self, name, names):
        return Steps(self.sem(name), names, 1)

    def marks(self, name, names):
        return Steps(self.sem(name), names, 0)

    def count(self, name):
        return Count(self.sem(name))

    def block(self):
        return self.ctx.enter_context(self.nc.Block())


def bcast(ap, n):
    p, a = ap.shape
    return ap.unsqueeze(2).to_broadcast([p, a, n])


def over(ap, n):
    p, a = ap.shape
    return ap.unsqueeze(1).to_broadcast([p, n, a])


def banks(ps, b, n=2):
    return ps[:, b:b + n, :].rearrange("p b c -> p (b c)")


def blocks(ps, b, n):
    return ps[:, b:b + (n + 3) // 4, :].rearrange("p b (k c) -> p (b k) c", c=P)[:, 0:n, :]


def block_of(ps, b, j):
    return ps[:, b + j // 4, (j % 4) * P:(j % 4 + 1) * P]


def norm_project(nc, name, x, gain, w, width, out, pad_rows, ident_d):
    n_cols = w.shape[1]
    pairs = n_cols // (2 * width)
    assert pairs * 2 * width == n_cols
    with Phase(nc, name) as ph:
        ident = ph.sb("ident", [P, P])
        gcol = ph.sb("gcol", [P, KD])
        xt = ph.sb("xt", [P, NT, D])
        h = [ph.sb(f"h{b}", [P, D]) for b in range(2)]
        junk = ph.sb("junk", [P, D])
        ss = ph.sb("ss", [P, 4, NT])
        hT = ph.sb("hT", [P, KD, SEQ])
        wt = [ph.sb(f"w{b}", [P, KD, width]) for b in range(2)]
        og = [ph.sb(f"o{b}", [P, NT, width]) for b in range(2)]
        zero = ph.sb("zero", [4, n_cols]) if pad_rows else None
        ps = ph.psum()
        const_in = ph.sem("const_in")
        x_in = [ph.sem(f"x_in{t}") for t in range(NT)]
        w_in = [ph.sem(f"w_in{b}") for b in range(2)]
        out_st = [ph.sem(f"out_st{b}") for b in range(2)]
        zero_set = ph.sem("zero_set")
        zero_st = ph.sem("zero_st")
        squared, mean, root, inverse = (ph.sem(n) for n in ("squared", "mean", "root", "inverse"))
        normed, turned, copied = (ph.count(n) for n in ("normed", "turned", "copied"))
        bank_full = ph.sem("bank_full")
        act_free = ph.sem("act_free")
        dve_free = ph.sem("dve_free")
        chunks = out[pad_rows:pad_rows + SEQ, :].rearrange("(t p) n -> p t n", p=P)
        w_v = w.rearrange("(k p) n -> p k n", p=P)
        blk = ph.block()

        @blk.sync
        def _(sp):
            for t in range(NT):
                sp.dma_start(xt[:, t, :], x[t * P:(t + 1) * P, :]).then_inc(x_in[t], 16)
            sp.dma_start(ident[:, :], ident_d).then_inc(const_in, 16)
            sp.dma_start(gcol[:, :], gain.rearrange("(k p) -> p k", p=P),
                         allow_slow_non_contiguous=True).then_inc(const_in, 16)
            with sp.Fori(0, pairs) as j:
                for b in range(2):
                    sp.wait_ge(bank_full, 8 * (2 * j + b) + 8)
                    sp.dma_start(wt[b][:, :, :], w_v[:, :, bass.ds((2 * j + b) * width, width)])\
                        .then_inc(w_in[b], 16)

        @blk.gpsimd
        def _(pool):
            if pad_rows:
                pool.memset(zero[:, :], 0.0).then_inc(zero_set, 1)
                pool.wait_ge(zero_set, 1)
                pool.dma_start(out[0:pad_rows, :], zero[0:pad_rows, :]).then_inc(zero_st, 16)
                pool.wait_ge(zero_st, 16)

        @blk.scalar
        def _(a):
            for t in range(NT):
                a.drain()
                a.wait_ge(x_in[t], 16)
                a.activation(junk[:, :], xt[:, t, :], ACT.Square, accum_out=ss[:, 0, t:t + 1]).then_inc(squared, 1)
            a.wait_ge(mean, 1)
            a.activation(ss[:, 2, :], ss[:, 1, :], ACT.Sqrt).then_inc(root, 1)
            a.wait_ge(inverse, 1)

            def norm(t, b, n):
                a.wait_ge(turned.sem, turned.done(t - 2))
                one = t if isinstance(t, int) else None
                row = xt[:, t, :] if one is not None else xt[:, bass.ds(t, 1), :].rearrange("p o d -> p (o d)")
                rstd = ss[:, 3, t:t + 1] if one is not None else ss[:, 3, bass.ds(t, 1)]
                a.activation(h[b][:, :], row, ACT.Copy, scale=rstd).then_inc(normed.sem, 1)

            normed.begin(a)
            each_tile(a, norm)
            a.sem_inc(act_free, 4)
            for b in range(2):
                a.sem_inc(out_st[b], 16)
            with a.Fori(0, pairs) as j:
                for b in range(2):
                    a.wait_ge(out_st[b], 16 * j + 16)
                    for t in range(0, NT, 2):
                        a.wait_ge(bank_full, 8 * (2 * j + b) + 16 + t + 1)
                        a.activation(og[b][:, t, :], ps[:, t, 0:width], ACT.Copy).then_inc(act_free, 1)
                    a.wait_ge(act_free, 4 * (2 * j + b) + 8)
                    a.wait_ge(dve_free, 4 * (2 * j + b) + 8)
                    a.dma_start(chunks[:, :, bass.ds((2 * j + b) * width, width)], og[b][:, :, :])\
                        .then_inc(out_st[b], 16)
            for b in range(2):
                a.wait_ge(out_st[b], 16 * (pairs + 1))

        @blk.vector
        def _(v):
            v.wait_ge(const_in, 32)
            v.wait_ge(squared, NT)
            v.tensor_scalar(ss[:, 1, :], ss[:, 0, :], 1.0 / D, EPS, ALU.mult, ALU.add).then_inc(mean, 1)
            v.wait_ge(root, 1)
            v.reciprocal(ss[:, 3, :], ss[:, 2, :]).then_inc(inverse, 1)
            copied.begin(v)

            def copy(t, b, n):
                v.wait_ge(turned.sem, turned.done(t))
                v.tensor_tensor(hT[:, :, bass.ds(t * P, P)], blocks(ps, 2 * b, 8), bcast(gcol[:, :], P), ALU.mult)\
                    .then_inc(copied.sem, 1)

            each_tile(v, copy)
            v.sem_inc(dve_free, 4)
            with v.Fori(0, pairs) as j:
                for b in range(2):
                    v.wait_ge(out_st[b], 16 * j + 16)
                    for t in range(1, NT, 2):
                        v.wait_ge(bank_full, 8 * (2 * j + b) + 16 + t + 1)
                        v.tensor_copy(og[b][:, t, :], ps[:, t, 0:width]).then_inc(dve_free, 1)

        @blk.tensor
        def _(te):
            te.sem_inc(bank_full, 16)
            te.wait_ge(const_in, 32)
            def turn(t, b, n):
                te.wait_ge(normed.sem, normed.done(t))
                te.wait_ge(copied.sem, copied.done(t - 2))
                for k in range(KD):
                    mm = te.transpose(block_of(ps, 2 * b, k), h[b][:, k * P:(k + 1) * P], ident[:, :])
                mm.then_inc(turned.sem, 1)

            turned.begin(te)
            each_tile(te, turn)
            te.wait_ge(copied.sem, copied.done(NT - 1))
            with te.Fori(0, pairs) as j:
                for b in range(2):
                    te.wait_ge(w_in[b], 16 * j + 16)
                    for t in range(NT):
                        te.wait_ge(dve_free if t % 2 else act_free, 4 * (2 * j + b) + t // 2 + 1)
                        for k in range(KD):
                            mm = te.matmul(ps[:, t, 0:width], hT[:, k, t * P:(t + 1) * P], wt[b][:, k, :],
                                           start=(k == 0), stop=(k == KD - 1))
                        mm.then_inc(bank_full, 1)


def mix_branches(nc, x, proj, gcol, o_rwkv, o_diff, out, g):
    with Phase(nc, "mix") as ph:
        ident = ph.sb("ident", [P, P])
        wr = ph.sb("wr", [P, 4, D])
        wd = ph.sb("wd", [P, 4, D])
        wo = ph.sb("wo", [P, KD, D])
        two = lambda n, shape: [ph.sb(f"{n}{b}", shape) for b in range(2)]
        ob = two("ob", [P, 2, 512])
        gt = two("gt", [P, 2 * D])
        xt = two("xt", [P, D])
        sg = two("sg", [P, 2 * D])
        oT = ph.sb("oT", [P, KD, P])
        m = ph.sb("m", [P, D])
        m2 = ph.sb("m2", [P, D])
        mT = ph.sb("mT", [P, KD, P])
        y = two("y", [P, D])
        ps = ph.psum()
        const_in, passed = ph.sem("const_in"), ph.sem("passed")
        o_in, g_in, x_in, y_st = ([ph.sem(f"{n}{b}") for b in range(2)] for n in ("o_in", "g_in", "x_in", "y_st"))
        gates, turned, copied, branches, mixed, mturned, mcopied, summed, added = (ph.count(n) for n in (
            "gates", "turned", "copied", "branches", "mixed", "mturned", "mcopied", "summed", "added"))
        blk = ph.block()

        @blk.sync
        def _(sp):
            for dst, src in ((ident[:, :], g["ident"]),
                             (wr[:, :, :], g["w_branch_rwkv"].rearrange("(k p) n -> p k n", p=P)),
                             (wd[:, :, :], g["w_branch_diff"].rearrange("(k p) n -> p k n", p=P)),
                             (wo[:, :, :], g["w_out"].rearrange("(k p) n -> p k n", p=P))):
                sp.dma_start(dst, src).then_inc(const_in, 16)

            def load_branches(t, b):
                sp.dma_start(ob[b][:, 0, :], o_rwkv[bass.ds(t * P, P), :]).then_inc(o_in[b], 16)
                sp.dma_start(ob[b][:, 1, :], o_diff[bass.ds(t * P, P), :]).then_inc(o_in[b], 16)
                sp.dma_start(gt[b][:, :], proj[bass.ds(t * P, P), gcol:gcol + 2 * D]).then_inc(g_in[b], 16)

            def load_x(t, b):
                sp.dma_start(xt[b][:, :], x[bass.ds(t * P, P), :]).then_inc(x_in[b], 16)

            def store(t, b):
                sp.wait_ge(added.sem, added.done(t))
                sp.dma_start(out[bass.ds(t * P, P), :], y[b][:, :]).then_inc(y_st[b], 16)

            for b in range(2):
                sp.sem_inc(y_st[b], 16)
                load_branches(b, b)
                load_x(b, b)
            with sp.Fori(0, NT // 2 - 1) as j:
                for b in range(2):
                    t = 2 * j + b
                    sp.wait_ge(turned.sem, turned.done(t))
                    sp.sem_inc(passed, 1)
                    sp.wait_ge(gates.sem, gates.done(t))
                    load_branches(t + 2, b)
                    store(t, b)
                    load_x(t + 2, b)
            for b in range(2):
                store(NT - 2 + b, b)
            for b in range(2):
                sp.wait_ge(y_st[b], 16 * (NT // 2 + 1))

        @blk.scalar
        def _(s):
            def body(t, b, n):
                s.wait_ge(g_in[b], 16 * n + 16)
                s.wait_ge(mixed.sem, mixed.done(t - 2))
                s.activation(sg[b][:, :], gt[b][:, :], ACT.Sigmoid).then_inc(gates.sem, 1)

            gates.begin(s)
            each_tile(s, body)

        @blk.vector
        def _(ve):
            tt = ve.tensor_tensor

            def turn_inputs(t):
                ve.drain()
                ve.wait_ge(turned.sem, turned.done(t))
                ve.tensor_copy(oT[:, :, :], blocks(ps, 0, 8)).then_inc(copied.sem, 1)

            def turn_mix(t):
                ve.drain()
                ve.wait_ge(mturned.sem, mturned.done(t))
                ve.tensor_copy(mT[:, :, :], blocks(ps, 0, 8)).then_inc(mcopied.sem, 1)

            def add(t, b, n):
                ve.drain()
                ve.wait_ge(summed.sem, summed.done(t))
                ve.wait_ge(x_in[b], 16 * n + 16)
                ve.wait_ge(y_st[b], 16 * n + 16)
                tt(y[b][:, :], xt[b][:, :], banks(ps, 6), ALU.add).then_inc(added.sem, 1)

            def body(t, b, n):
                if not first(t):
                    turn_mix(t - 1)
                ve.drain()
                ve.wait_ge(gates.sem, gates.done(t))
                ve.wait_ge(branches.sem, branches.done(t))
                tt(m[:, :], sg[b][:, 0:D], banks(ps, 2), ALU.mult)
                tt(m2[:, :], sg[b][:, D:2 * D], banks(ps, 4), ALU.mult)
                ve.drain()
                tt(m[:, :], m[:, :], m2[:, :], ALU.add).then_inc(mixed.sem, 1)
                if not last(t):
                    turn_inputs(t + 1)
                if not first(t):
                    add(t - 1, 1 - b, n - 1 + b)

            for c in (copied, mixed, mcopied, added):
                c.begin(ve)
            turn_inputs(0)
            each_tile(ve, body)
            turn_mix(NT - 1)
            add(NT - 1, 1, NT // 2 - 1)

        @blk.tensor
        def _(te):
            def turn_inputs(t, b, n):
                te.wait_ge(o_in[b], 32 * n + 32)
                te.wait_ge(mcopied.sem, mcopied.done(t - 2))
                for i in range(8):
                    mm = te.transpose(block_of(ps, 0, i), ob[b][:, i // 4, (i % 4) * P:(i % 4 + 1) * P], ident[:, :])
                mm.then_inc(turned.sem, 1)

            def out_product(t):
                te.wait_ge(mcopied.sem, mcopied.done(t))
                te.wait_ge(added.sem, added.done(t - 1))
                for n in range(2):
                    for k in range(KD):
                        mm = te.matmul(ps[:, 6 + n, :], mT[:, k, :], wo[:, k, n * 512:(n + 1) * 512],
                                       start=(k == 0), stop=(k == KD - 1))
                mm.then_inc(summed.sem, 1)

            def body(t, b, n):
                te.wait_ge(copied.sem, copied.done(t))
                te.wait_ge(mixed.sem, mixed.done(t - 1))
                for bank, w, k0 in ((2, wr, 0), (4, wd, 4)):
                    for h in range(2):
                        for k in range(4):
                            mm = te.matmul(ps[:, bank + h, :], oT[:, k0 + k, :], w[:, k, h * 512:(h + 1) * 512],
                                           start=(k == 0), stop=(k == 3))
                mm.then_inc(branches.sem, 1)
                if not last(t):
                    turn_inputs(t + 1, 1 - b, n + b)
                if not first(t):
                    out_product(t - 1)
                te.wait_ge(mixed.sem, mixed.done(t))
                if not last(t):
                    te.wait_ge(copied.sem, copied.done(t + 1))
                for i in range(8):
                    mm = te.transpose(block_of(ps, 0, i), m[:, i * P:(i + 1) * P], ident[:, :])
                mm.then_inc(mturned.sem, 1)

            for c in (turned, branches, mturned, summed):
                c.begin(te)
            te.wait_ge(const_in, 64)
            turn_inputs(0, 0, 0)
            each_tile(te, body)
            out_product(NT - 1)


def ple(nc, x, p, out, g):
    with Phase(nc, "ple") as ph:
        ident = ph.sb("ident", [P, P])
        gcol = ph.sb("gcol", [P, KD])
        wg = ph.sb("wg", [P, KD, D])
        wp = ph.sb("wp", [P, 2, D])
        two = lambda n, shape: [ph.sb(f"{n}{b}", shape) for b in range(2)]
        xt = two("xt", [P, D])
        pt = two("pt", [P, 2, P])
        junk = ph.sb("junk", [P, D])
        ss = two("ss", [P, 4])
        h = ph.sb("h", [P, D])
        hT = ph.sb("hT", [P, KD, P])
        pT = two("pT", [P, 2, P])
        sg = ph.sb("sg", [P, D])
        m = ph.sb("m", [P, D])
        y = two("y", [P, D])
        ps = ph.psum()
        const_in = ph.sem("const_in")
        x_in, y_st = ([ph.sem(f"{n}{b}") for b in range(2)] for n in ("x_in", "y_st"))
        squared, mean, root, normed, turned, copied, gate_sums, proj_sums, gates, added = (ph.count(n) for n in (
            "squared", "mean", "root", "normed", "turned", "copied", "gate_sums", "proj_sums", "gates", "added"))
        blk = ph.block()

        @blk.sync
        def _(sp):
            for dst, src in ((ident[:, :], g["ident"]), (gcol[:, :], g["norm_ple"].rearrange("(k p) -> p k", p=P)),
                             (wg[:, :, :], g["w_ple_gate"].rearrange("(k p) n -> p k n", p=P)),
                             (wp[:, :, :], g["w_ple_proj"].rearrange("(k p) n -> p k n", p=P))):
                sp.dma_start(dst, src, allow_slow_non_contiguous=True).then_inc(const_in, 16)

            def load(t, b):
                sp.dma_start(xt[b][:, :], x[bass.ds(t * P, P), :]).then_inc(x_in[b], 16)
                sp.dma_start(pt[b][:, :, :].rearrange("p a c -> p (a c)"), p[bass.ds(t * P, P), :]).then_inc(x_in[b], 16)

            def store(t, b):
                sp.wait_ge(added.sem, added.done(t))
                sp.dma_start(out[bass.ds(t * P, P), :], y[b][:, :]).then_inc(y_st[b], 16)

            for b in range(2):
                sp.sem_inc(y_st[b], 16)
                load(b, b)
            with sp.Fori(0, NT // 2 - 1) as j:
                for b in range(2):
                    store(2 * j + b, b)
                    load(2 * j + b + 2, b)
            for b in range(2):
                store(NT - 2 + b, b)
            for b in range(2):
                sp.wait_ge(y_st[b], 16 * (NT // 2 + 1))

        @blk.scalar
        def _(s):
            def norm(t, b, n):
                s.wait_ge(x_in[b], 32 * n + 32)
                s.wait_ge(normed.sem, normed.done(t - 1))
                s.activation(junk[:, :], xt[b][:, :], ACT.Square, accum_out=ss[b][:, 0:1]).then_inc(squared.sem, 1)
                s.wait_ge(mean.sem, mean.done(t))
                s.activation(ss[b][:, 2:3], ss[b][:, 1:2], ACT.Sqrt).then_inc(root.sem, 1)

            def body(t, b, n):
                if not last(t):
                    norm(t + 1, 1 - b, n + b)
                s.wait_ge(gate_sums.sem, gate_sums.done(t))
                s.wait_ge(added.sem, added.done(t - 1))
                s.activation(sg[:, :], banks(ps, 4), ACT.Sigmoid).then_inc(gates.sem, 1)

            for c in (squared, root, gates):
                c.begin(s)
            norm(0, 0, 0)
            each_tile(s, body)

        @blk.vector
        def _(ve):
            tt = ve.tensor_tensor

            def norm(t, b, n):
                ve.drain()
                ve.wait_ge(squared.sem, squared.done(t))
                ve.tensor_scalar(ss[b][:, 1:2], ss[b][:, 0:1], 1.0 / D, EPS, ALU.mult, ALU.add).then_inc(mean.sem, 1)
                ve.drain()
                ve.wait_ge(root.sem, root.done(t))
                ve.reciprocal(ss[b][:, 3:4], ss[b][:, 2:3])
                ve.drain()
                ve.wait_ge(turned.sem, turned.done(t - 1))
                ve.tensor_scalar(h[:, :], xt[b][:, :], ss[b][:, 3:4], None, ALU.mult).then_inc(normed.sem, 1)

            def copy(t, b, n):
                ve.drain()
                ve.wait_ge(turned.sem, turned.done(t))
                ve.tensor_copy(pT[b][:, :, :], blocks(ps, 2, 2))
                tt(hT[:, :, :], blocks(ps, 0, 8), bcast(gcol[:, :], P), ALU.mult).then_inc(copied.sem, 1)

            def body(t, b, n):
                if not last(t):
                    norm(t + 1, 1 - b, n + b)
                    copy(t + 1, 1 - b, n + b)
                ve.drain()
                ve.wait_ge(gates.sem, gates.done(t))
                ve.wait_ge(proj_sums.sem, proj_sums.done(t))
                tt(m[:, :], sg[:, :], banks(ps, 6), ALU.mult)
                ve.drain()
                ve.wait_ge(y_st[b], 16 * n + 16)
                tt(y[b][:, :], xt[b][:, :], m[:, :], ALU.add).then_inc(added.sem, 1)

            for c in (mean, normed, copied, added):
                c.begin(ve)
            ve.wait_ge(const_in, 64)
            norm(0, 0, 0)
            copy(0, 0, 0)
            each_tile(ve, body)

        @blk.tensor
        def _(te):
            def turn(t, b, n):
                te.wait_ge(normed.sem, normed.done(t))
                for i in range(8):
                    te.transpose(block_of(ps, 0, i), h[:, i * P:(i + 1) * P], ident[:, :])
                for i in range(2):
                    mm = te.transpose(block_of(ps, 2, i), pt[b][:, i, :], ident[:, :])
                mm.then_inc(turned.sem, 1)

            def product(bank, a, w, n_k):
                for h in range(2):
                    for k in range(n_k):
                        mm = te.matmul(ps[:, bank + h, :], a[:, k, :], w[:, k, h * 512:(h + 1) * 512],
                                       start=(k == 0), stop=(k == n_k - 1))
                return mm

            def body(t, b, n):
                te.wait_ge(copied.sem, copied.done(t))
                te.wait_ge(gates.sem, gates.done(t - 1))
                product(4, hT, wg, KD).then_inc(gate_sums.sem, 1)
                if not last(t):
                    turn(t + 1, 1 - b, n + b)
                te.wait_ge(added.sem, added.done(t - 1))
                product(6, pT[b], wp, 2).then_inc(proj_sums.sem, 1)

            for c in (turned, gate_sums, proj_sums):
                c.begin(te)
            te.wait_ge(const_in, 64)
            turn(0, 0, 0)
            each_tile(te, body)


def mix_out(nc, x, mixes, out, g):
    KM = 16
    with Phase(nc, "fin") as ph:
        ident = ph.sb("ident", [P, P])
        w = ph.sb("w", [P, KM, D])
        post = ph.sb("post", [P, D])
        two = lambda n, shape: [ph.sb(f"{n}{b}", shape) for b in range(2)]
        mt = two("mt", [P, KM * P])
        xt = two("xt", [P, D])
        mT = two("mT", [P, KM, P])
        z = ph.sb("z", [P, D])
        junk = ph.sb("junk", [P, D])
        ss = ph.sb("ss", [P, 4])
        y = two("y", [P, D])
        ps = ph.psum()
        const_in, passed = ph.sem("const_in"), ph.sem("passed")
        mix_in, x_in, y_st = ([ph.sem(f"{n}{b}") for b in range(2)] for n in ("mix_in", "x_in", "y_st"))
        turned, copied, summed, squared, mean, root, scaled, added = (ph.count(n) for n in (
            "turned", "copied", "summed", "squared", "mean", "root", "scaled", "added"))
        blk = ph.block()

        @blk.sync
        def _(sp):
            for dst, src in ((ident[:, :], g["ident"]), (post[:, :], g["post_norm_w_2"].partition_broadcast(P))):
                sp.dma_start(dst, src).then_inc(const_in, 16)

            def load_mix(t, b):
                at = 0
                for mix in mixes:
                    n = mix.shape[1]
                    sp.dma_start(mt[b][:, at:at + n], mix[bass.ds(t * P, P), :]).then_inc(mix_in[b], 16)
                    at += n

            def load_x(t, b):
                sp.dma_start(xt[b][:, :], x[bass.ds(t * P, P), :]).then_inc(x_in[b], 16)

            def store(t, b):
                sp.wait_ge(added.sem, added.done(t))
                sp.dma_start(out[bass.ds(t * P, P), :], y[b][:, :]).then_inc(y_st[b], 16)

            for b in range(2):
                sp.sem_inc(y_st[b], 16)
                load_mix(b, b)
                load_x(b, b)
            with sp.Fori(0, NT // 2 - 1) as j:
                for b in range(2):
                    t = 2 * j + b
                    sp.wait_ge(turned.sem, turned.done(t))
                    sp.sem_inc(passed, 1)
                    load_mix(t + 2, b)
                    store(t, b)
                    load_x(t + 2, b)
            for b in range(2):
                store(NT - 2 + b, b)
            for b in range(2):
                sp.wait_ge(y_st[b], 16 * (NT // 2 + 1))

        @blk.scalar
        def _(s):
            def body(t, b, n):
                s.wait_ge(summed.sem, summed.done(t))
                s.wait_ge(scaled.sem, scaled.done(t - 1))
                s.activation(junk[:, :], banks(ps, 4 + 2 * b), ACT.Square, accum_out=ss[:, 0:1]).then_inc(squared.sem, 1)
                s.wait_ge(mean.sem, mean.done(t))
                s.activation(ss[:, 2:3], ss[:, 1:2], ACT.Sqrt).then_inc(root.sem, 1)

            s.dma_start(w[:, :, :], g["w_out_2"].rearrange("(k p) n -> p k n", p=P)).then_inc(const_in, 16)
            for c in (squared, root):
                c.begin(s)
            each_tile(s, body)

        @blk.vector
        def _(ve):
            def copy(t, b):
                ve.drain()
                ve.wait_ge(turned.sem, turned.done(t))
                ve.wait_ge(summed.sem, summed.done(t - 2))
                ve.tensor_copy(mT[b][:, :, :], blocks(ps, 0, KM)).then_inc(copied.sem, 1)

            def body(t, b, n):
                if not last(t):
                    copy(t + 1, 1 - b)
                ve.drain()
                ve.wait_ge(squared.sem, squared.done(t))
                ve.tensor_scalar(ss[:, 1:2], ss[:, 0:1], 1.0 / D, EPS, ALU.mult, ALU.add).then_inc(mean.sem, 1)
                ve.drain()
                ve.wait_ge(root.sem, root.done(t))
                ve.reciprocal(ss[:, 3:4], ss[:, 2:3])
                ve.drain()
                ve.scalar_tensor_tensor(z[:, :], banks(ps, 4 + 2 * b), ss[:, 3:4], post[:, :], ALU.mult, ALU.mult)\
                    .then_inc(scaled.sem, 1)
                ve.drain()
                ve.wait_ge(x_in[b], 16 * n + 16)
                ve.wait_ge(y_st[b], 16 * n + 16)
                ve.tensor_tensor(y[b][:, :], xt[b][:, :], z[:, :], ALU.add).then_inc(added.sem, 1)

            for c in (copied, mean, scaled, added):
                c.begin(ve)
            ve.wait_ge(const_in, 48)
            copy(0, 0)
            each_tile(ve, body)

        @blk.tensor
        def _(te):
            def turn(t, b, n):
                te.wait_ge(mix_in[b], 48 * n + 48)
                te.wait_ge(copied.sem, copied.done(t - 1))
                for i in range(KM):
                    mm = te.transpose(block_of(ps, 0, i), mt[b][:, i * P:(i + 1) * P], ident[:, :])
                mm.then_inc(turned.sem, 1)

            def body(t, b, n):
                if not last(t):
                    turn(t + 1, 1 - b, n + b)
                te.wait_ge(copied.sem, copied.done(t))
                te.wait_ge(scaled.sem, scaled.done(t - 2))
                for h in range(2):
                    for k in range(KM):
                        mm = te.matmul(ps[:, 4 + 2 * b + h, :], mT[b][:, k, :], w[:, k, h * 512:(h + 1) * 512],
                                       start=(k == 0), stop=(k == KM - 1))
                mm.then_inc(summed.sem, 1)

            for c in (turned, summed):
                c.begin(te)
            te.wait_ge(const_in, 48)
            turn(0, 0, 0)
            each_tile(te, body)


RH, RD = 8, 64
RW = RH * RD
RWKV_COLS = 1792
GN_EPS = 64e-5
CH = 64


def rwkv_masks():
    s, t = np.arange(P)[:, None], np.arange(P)[None, :]
    same = lambda n: (s // n) == (t // n)
    up = s < t
    m = dict(
        ident=s == t,
        cum=same(64) & (s <= t),
        suf=same(64) & (s > t),
        m16=same(16) & up, n16=same(16) & (s > t),
        strict=same(64) & up, incl=same(64) & (s <= t),
        n32=same(32) & ~same(16) & (s > t),
        n64=same(64) & ~same(32) & (s > t),
    )
    return list(m), np.concatenate([v.astype(np.float32) for v in m.values()], axis=1)


def rwkv(nc, pr, out, masks_d, g):
    mnames, _ = rwkv_masks()
    with Phase(nc, "rwkv") as ph:
        masks = ph.sb("masks", [P, len(mnames) * P])
        M = {n: masks[:, i * P:(i + 1) * P] for i, n in enumerate(mnames)}
        ind = ph.sb("ind", [P, 2])
        mu = ph.sb("mu", [P, RWKV_COLS])
        rows = ph.sb("rows", [P, 7, RW])
        w0, a0, k_k, k_a, r_k, ln_w, ln_b = (rows[:, i, :] for i in range(7))
        w2 = ph.sb("w2", [64, RW])
        a2 = ph.sb("a2", [64, RW])
        g2 = ph.sb("g2", [P, RW])
        x = ph.sb("x", [P, RWKV_COLS])
        prev = ph.sb("prev", [P, RWKV_COLS])
        xs = ph.sb("xs", [P, RWKV_COLS])
        r, k, v = (xs[:, i * RW:(i + 1) * RW] for i in range(3))
        xw, xa, xg = xs[:, 1536:1600], xs[:, 1600:1664], xs[:, 1664:1792]
        lo = ph.sb("lo", [P, 2, P])
        loT = ph.sb("loT", [P, 3, P])
        wide = ph.sb("wide", [P, 20, RW])
        wp, ap_, gg, sw, a, ld, kk, sq, km, tmp, eL, enL, eS, eLm, al, rh, be, ka, bE, kE = (
            wide[:, i, :] for i in range(20))
        small = ph.sb("small", [P, 6, RH])
        arT = ph.sb("arT", [P, 4, 2, P])
        beT = ph.sb("beT", [P, 4, P])
        kaT = ph.sb("kaT", [P, 4, P])
        pend = ph.sb("pend", [64, RH, 2])
        G4 = [P, 4, P]
        two = lambda n, shape: [ph.sb(f"{n}{q}", shape) for q in range(2)]
        M1, N1, X, XT, M2, N2, M4, N4, M8, N32, N64, QB, Km, QK, Z = (two(n, G4) for n in (
            "M1", "N1", "X", "XT", "M2", "N2", "M4", "N4", "M8", "N32", "N64", "QB", "Km", "QK", "Z"))
        aKV = two("aKV", [P, 4, 2, 64])
        AG = two("AG", [P, 4, 2, 64])
        side = ph.sb("side", [P, 4, RW])
        bon, bk, lg, bg = (side[:, i, :] for i in range(4))
        bsum = ph.sb("bsum", [P, RH])
        ET = ph.sb("ET", [64, RH, P])
        F = ph.sb("F", [P, RH, 64])
        HT = ph.sb("HT", [64, RH, 2, 64])
        J = ph.sb("J", [64, RH, 2, 64])
        S = ph.sb("S", [64, RH, 64])
        y = ph.sb("y", [P, RH, 64])
        yo = ph.sb("yo", [P, RH, 64])
        ps = ph.psum()
        const_in, x_in, o_st = ph.sem("const_in"), ph.sem("x_in"), ph.sem("o_st")
        passed = ph.sem("passed")

        groups = range(2)
        both = lambda names: " ".join(f"{n}_{q}" for n in names.split() for q in groups)
        act = ph.steps("act", "lora_in gate decays norm exps lmexp arT " + both("p2 x2 x4 z32 z64 ag eh") + " gn")
        dve = ph.steps("dve", "xs loT lora ld lm scaled bkT " + both("masked") + " " + both("x1") + " "
                       + both("p2") + " bsum " + both("x2 x4 x8 x32 x64 eh") + " s0 s1 var out")
        pe = ph.steps("pe", "lora_t lora sums turned " + both("scores p2 qk x2 x4 x8 z32 x32 z64 x64 ag eh") + " y0 y1")
        pool = ph.steps("pool", "shift diag alpha rk bonus")
        blk = ph.block()

        def pg(b, n=P):
            return ps[:, b, 0:4 * n].rearrange("p (h c) -> p h c", c=n)

        @blk.sync
        def _(sp):
            for dst, src in ((masks[:, :], masks_d), (ind[:, :], g["ind64"]),
                             (mu[:, :], g["rwkv_mu"].partition_broadcast(P)),
                             (w0, g["rwkv_w0"].partition_broadcast(P)), (a0, g["rwkv_a0"].partition_broadcast(P)),
                             (k_k, g["rwkv_k_k"].partition_broadcast(P)), (k_a, g["rwkv_k_a"].partition_broadcast(P)),
                             (r_k, g["rwkv_r_k"].rearrange("h d -> (h d)").partition_broadcast(P)),
                             (ln_w, g["rwkv_ln_w"].partition_broadcast(P)),
                             (ln_b, g["rwkv_ln_b"].partition_broadcast(P)),
                             (w2[:, :], g["rwkv_w2"]), (a2[:, :], g["rwkv_a2"]), (g2[:, :], g["rwkv_g2"])):
                sp.dma_start(dst, src).then_inc(const_in, 16)
            sp.sem_inc(o_st, 16)

            def load(t):
                sp.dma_start(x[:, :], pr[bass.ds(t * P + 1, P), 0:RWKV_COLS]).then_inc(x_in, 16)
                sp.dma_start(prev[:, :], pr[bass.ds(t * P, P), 0:RWKV_COLS]).then_inc(x_in, 16)

            def store(t):
                sp.wait_ge(dve.sem, dve.at("out", t))
                sp.dma_start(out[bass.ds(t * P, P), :], yo[:, :, :].rearrange("p h d -> p (h d)")).then_inc(o_st, 16)

            load(0)
            with sp.Fori(0, NT - 1) as t:
                sp.wait_ge(dve.sem, dve.at("xs", t))
                load(t + 1)
                store(t)
            store(NT - 1)
            sp.wait_ge(o_st, 16 * (NT + 1))

        @blk.scalar
        def _(s):
            act.begin(s)
            with s.Fori(0, NT) as t:
                s.wait_ge(dve.sem, dve.at("xs", t))
                s.activation(lo[:, 0, 0:64], xw, ACT.Tanh)
                s.activation(lo[:, 1, :], xg, ACT.Sigmoid).then_inc(act.sem, act.step("lora_in"))
                s.wait_ge(pe.sem, pe.at("lora", t))
                s.activation(gg, ps[:, 3, :], ACT.Copy).then_inc(act.sem, act.step("gate"))
                s.wait_ge(dve.sem, dve.at("lora", t))
                s.activation(sw, wp, ACT.Sigmoid)
                s.activation(a, ap_, ACT.Sigmoid).then_inc(act.sem, act.step("decays"))
                s.activation(small[:, 1, :], small[:, 0, :], ACT.Sqrt).then_inc(act.sem, act.step("norm"))
                s.wait_ge(pe.sem, pe.at("sums", t))
                s.activation(eL, ps[:, 4, :], ACT.Exp)
                s.activation(enL, ps[:, 4, :], ACT.Exp, scale=-1.0)
                s.activation(eS, ps[:, 5, :], ACT.Exp)
                s.activation(pend[:, :, :].rearrange("p h c -> p (h c)"), ps[0:64, 6, 0:16], ACT.Exp).then_inc(act.sem, act.step("exps"))
                s.wait_ge(dve.sem, dve.at("lm", t))
                s.activation(eLm, tmp, ACT.Exp).then_inc(act.sem, act.step("lmexp"))
                s.wait_ge(pe.sem, pe.at("turned", t))
                s.activation(arT[:, :, 0, :], pg(0), ACT.Copy)
                s.activation(arT[:, :, 1, :], pg(1), ACT.Copy).then_inc(act.sem, act.step("arT"))
                for stage, outs in (("p2", ((0, M2), (1, N2))), ("x2", ((2, M4), (3, N4))), ("x4", ((2, M8),)),
                                    ("z32", ((2, Z),)), ("z64", ((2, Z),))):
                    for q in groups:
                        s.wait_ge(pe.sem, pe.at(f"{stage}_{q}", t))
                        for b, dst in outs:
                            copy = s.activation(dst[q][:, :, :], pg(4 * q + b), ACT.Copy)
                        copy.then_inc(act.sem, act.step(f"{stage}_{q}"))
                for q in groups:
                    s.wait_ge(pe.sem, pe.at(f"ag_{q}", t))
                    s.activation(AG[q][:, :, :, :].rearrange("p h a c -> p h (a c)"), pg(4 * q + 1), ACT.Copy)\
                        .then_inc(act.sem, act.step(f"ag_{q}"))
                for q in groups:
                    s.wait_ge(pe.sem, pe.at(f"eh_{q}", t))
                    s.activation(ET[:, slice(q, RH, 2), :], ps[0:64, 4 * q, :].rearrange("p (h c) -> p h c", c=P), ACT.Copy)
                    s.activation(F[:, slice(q, RH, 2), :], pg(4 * q + 1, 64), ACT.Copy).then_inc(act.sem, act.step(f"eh_{q}"))
                s.wait_ge(dve.sem, dve.at("var", t))
                s.activation(small[:, 3, :], small[:, 2, :], ACT.Sqrt).then_inc(act.sem, act.step("gn"))

        @blk.gpsimd
        def _(po):
            h8 = lambda z: z.rearrange("p (h d) -> p h d", d=RD)
            tt = po.tensor_tensor
            po.wait_ge(const_in, 16 * 13)
            pool.begin(po)
            with po.Fori(0, NT) as t:
                po.drain()
                po.wait_ge(x_in, 32 * t + 32)
                tt(prev[:, :], prev[:, :], x[:, :], ALU.subtract)
                po.drain()
                tt(prev[:, :], prev[:, :], mu[:, :], ALU.mult).then_inc(pool.sem, pool.step("shift"))
                po.drain()
                po.wait_ge(act.sem, act.at("exps", t))
                for c in range(2):
                    last = tt(HT[:, :, c, :], bcast(pend[:, :, c], 64), over(M["ident"][0:64, 0:64], RH), ALU.mult)
                last.then_inc(pool.sem, pool.step("diag"))
                po.drain()
                po.wait_ge(dve.sem, dve.at("scaled", t))
                tt(bon, r, km, ALU.mult)
                for q in groups:
                    last = po.tensor_copy(aKV[q][:, :, 0, :], h8(al)[:, slice(q, RH, 2), :])
                last.then_inc(pool.sem, pool.step("alpha"))
                tt(lg, ln_w, gg, ALU.mult)
                po.drain()
                tt(bon, bon, r_k, ALU.mult).then_inc(pool.sem, pool.step("rk"))
                po.drain()
                po.wait_ge(dve.sem, dve.at("bsum", t))
                tt(h8(bk), h8(v), bcast(bsum[:, :], RD), ALU.mult)
                po.drain()
                tt(bon, bk, ln_b, ALU.add)
                po.drain()
                tt(bg, bon, gg, ALU.mult).then_inc(pool.sem, pool.step("bonus"))

        @blk.vector
        def _(ve):
            h8 = lambda z: z.rearrange("p (h d) -> p h d", d=RD)

            def tt(o, i0, i1, op):
                return ve.tensor_tensor(o, i0, i1, op)

            ve.memset(S[:, :, :], 0.0)
            ve.drain()
            ve.wait_ge(const_in, 16 * 13)
            dve.begin(ve)
            with ve.Fori(0, NT) as t:
                ve.wait_ge(pool.sem, pool.at("shift", t))
                tt(xs[:, :], prev[:, :], x[:, :], ALU.add).then_inc(dve.sem, dve.step("xs"))
                ve.drain()
                ve.wait_ge(pe.sem, pe.at("lora_t", t))
                ve.tensor_copy(loT[0:64, 0:2, :], ps[0:64, 0, 0:2 * P].rearrange("p (a c) -> p a c", c=P))
                ve.tensor_copy(loT[:, 2, :], ps[:, 0, 2 * P:3 * P]).then_inc(dve.sem, dve.step("loT"))
                tt(kk, k, k_k, ALU.mult)
                ve.drain()
                tt(sq, kk, kk, ALU.mult)
                ve.drain()
                ve.tensor_reduce(small[:, 0, :], h8(sq), AX, ALU.add)
                ve.drain()
                ve.wait_ge(pe.sem, pe.at("lora", t))
                tt(wp, ps[:, 1, :], w0, ALU.add)
                tt(ap_, ps[:, 2, :], a0, ALU.add).then_inc(dve.sem, dve.step("lora"))
                ve.drain()
                ve.wait_ge(act.sem, act.at("decays", t))
                ve.tensor_scalar(ld, sw, -math.exp(-0.5), None, ALU.mult).then_inc(dve.sem, dve.step("ld"))
                ve.drain()
                ve.wait_ge(act.sem, act.at("norm", t))
                ve.tensor_scalar(small[:, 4, :], small[:, 1, :], 1e-12, None, ALU.max)
                ve.scalar_tensor_tensor(km, a, 1.0, k_a, ALU.subtract, ALU.mult)
                ve.drain()
                ve.reciprocal(small[:, 5, :], small[:, 4, :])
                ve.scalar_tensor_tensor(km, km, 1.0, k, ALU.add, ALU.mult)
                ve.drain()
                tt(h8(kk), h8(kk), bcast(small[:, 5, :], RD), ALU.mult)
                ve.drain()
                ve.scalar_tensor_tensor(sq, kk, -1.0, a, ALU.mult, ALU.mult)
                ve.drain()
                ve.wait_ge(act.sem, act.at("exps", t))
                tt(tmp, ps[:, 4, :], ld, ALU.subtract).then_inc(dve.sem, dve.step("lm"))
                tt(rh, r, eL, ALU.mult)
                tt(be, sq, enL, ALU.mult)
                tt(ka, km, enL, ALU.mult)
                tt(bE, sq, eS, ALU.mult)
                tt(kE, km, eS, ALU.mult)
                ve.drain()
                ve.wait_ge(act.sem, act.at("lmexp", t))
                tt(al, kk, eLm, ALU.mult).then_inc(dve.sem, dve.step("scaled"))
                ve.drain()
                ve.wait_ge(pe.sem, pe.at("turned", t))
                ve.tensor_copy(beT[:, :, :], pg(2))
                ve.tensor_copy(kaT[:, :, :], pg(3)).then_inc(dve.sem, dve.step("bkT"))
                m4 = lambda n: over(M[n], 4)
                for q in groups:
                    ve.drain()
                    ve.wait_ge(pe.sem, pe.at(f"scores_{q}", t))
                    tt(M1[q][:, :, :], pg(4 * q), m4("m16"), ALU.mult)
                    tt(N1[q][:, :, :], pg(4 * q + 1), m4("n16"), ALU.mult)
                    tt(Km[q][:, :, :], pg(4 * q + 2), m4("strict"), ALU.mult)
                    tt(N32[q][:, :, :], pg(4 * q + 1), m4("n32"), ALU.mult)
                    tt(N64[q][:, :, :], pg(4 * q + 1), m4("n64"), ALU.mult).then_inc(dve.sem, dve.step(f"masked_{q}"))
                for q in groups:
                    ve.drain()
                    tt(QB[q][:, :, :], pg(4 * q + 3), m4("incl"), ALU.mult)
                    tt(X[q][:, :, :], M1[q][:, :, :], m4("ident"), ALU.add)
                    tt(XT[q][:, :, :], N1[q][:, :, :], m4("ident"), ALU.add).then_inc(dve.sem, dve.step(f"x1_{q}"))
                for q in groups:
                    ve.wait_ge(pe.sem, pe.at(f"qk_{q}", t))
                    ve.tensor_copy(aKV[q][:, :, 1, :], pg(4 * q + 2, 64))
                    tt(QK[q][:, :, :], pg(4 * q + 3), m4("incl"), ALU.mult).then_inc(dve.sem, dve.step(f"p2_{q}"))
                ve.drain()
                ve.wait_ge(pool.sem, pool.at("rk", t))
                ve.tensor_reduce(bsum[:, :], h8(bon), AX, ALU.add).then_inc(dve.sem, dve.step("bsum"))
                for stage in ("x2", "x4", "x8", "x32", "x64"):
                    for q in groups:
                        ve.drain()
                        ve.wait_ge(pe.sem, pe.at(f"{stage}_{q}", t))
                        last = tt(X[q][:, :, :], X[q][:, :, :], pg(4 * q), ALU.add)
                        if stage != "x64":
                            last = tt(XT[q][:, :, :], XT[q][:, :, :], pg(4 * q + 1), ALU.add)
                        last.then_inc(dve.sem, dve.step(f"{stage}_{q}"))
                for q in groups:
                    hs = slice(q, RH, 2)
                    half = lambda c, at: ps[0:64, 4 * q + 2 + c, at:at + 256].rearrange("p (h c) -> p h c", c=64)
                    ve.drain()
                    ve.wait_ge(pool.sem, pool.at("diag", t))
                    ve.wait_ge(pe.sem, pe.at(f"eh_{q}", t))
                    for c in range(2):
                        tt(HT[:, hs, c, :], HT[:, hs, c, :], half(c, 0), ALU.add)
                    for c in range(2):
                        last = ve.tensor_copy(J[:, hs, c, :], half(c, 256))
                    last.then_inc(dve.sem, dve.step(f"eh_{q}"))
                for c in range(2):
                    ve.drain()
                    ve.wait_ge(pe.sem, pe.at(f"y{c}", t))
                    tt(S[:, :, :], J[:, :, c, :], ps[0:64, 7, :].rearrange("p (h c) -> p h c", c=64), ALU.add)\
                        .then_inc(dve.sem, dve.step(f"s{c}"))
                tt(y[:, :, :], F[:, :, :], ps[:, 6, :].rearrange("p (h c) -> p h c", c=64), ALU.add)
                ve.drain()
                ve.tensor_reduce(small[:, 4, :], y[:, :, :], AX, ALU.add)
                ve.drain()
                ve.tensor_scalar(small[:, 4, :], small[:, 4, :], 1.0 / RD, None, ALU.mult)
                ve.drain()
                tt(y[:, :, :], y[:, :, :], bcast(small[:, 4, :], RD), ALU.subtract)
                ve.drain()
                tt(h8(sq), y[:, :, :], y[:, :, :], ALU.mult)
                ve.drain()
                ve.tensor_reduce(small[:, 2, :], h8(sq), AX, ALU.add)
                ve.drain()
                ve.tensor_scalar(small[:, 2, :], small[:, 2, :], 1.0 / RD, GN_EPS, ALU.mult, ALU.add)\
                    .then_inc(dve.sem, dve.step("var"))
                ve.drain()
                ve.wait_ge(act.sem, act.at("gn", t))
                ve.reciprocal(small[:, 4, :], small[:, 3, :])
                ve.drain()
                tt(y[:, :, :], y[:, :, :], bcast(small[:, 4, :], RD), ALU.mult)
                ve.drain()
                ve.wait_ge(pool.sem, pool.at("bonus", t))
                tt(y[:, :, :], y[:, :, :], h8(lg), ALU.mult)
                ve.drain()
                ve.wait_ge(o_st, 16 * t + 16)
                tt(yo[:, :, :], y[:, :, :], h8(bg), ALU.add).then_inc(dve.sem, dve.step("out"))
                ve.drain()

        @blk.tensor
        def _(te):
            I = M["ident"]
            hd = lambda z, h: z[:, h * RD:(h + 1) * RD]
            te.wait_ge(const_in, 16 * 13)
            pe.begin(te)
            with te.Fori(0, NT) as t:
                te.wait_ge(act.sem, act.at("lora_in", t))
                te.transpose(ps[:, 0, 2 * P:3 * P], lo[:, 1, :], I)
                te.transpose(ps[0:64, 0, 0:P], lo[:, 0, 0:64], I)
                te.transpose(ps[0:64, 0, P:2 * P], xa, I).then_inc(pe.sem, pe.step("lora_t"))
                te.wait_ge(dve.sem, dve.at("loT", t))
                te.matmul(ps[:, 1, :], loT[0:64, 0, :], w2[:, :], start=True, stop=True)
                te.matmul(ps[:, 2, :], loT[0:64, 1, :], a2[:, :], start=True, stop=True)
                te.matmul(ps[:, 3, :], loT[:, 2, :], g2[:, :], start=True, stop=True).then_inc(pe.sem, pe.step("lora"))
                te.wait_ge(dve.sem, dve.at("ld", t))
                te.matmul(ps[:, 4, :], M["cum"], ld, start=True, stop=True)
                te.matmul(ps[:, 5, :], M["suf"], ld, start=True, stop=True)
                for h in range(RH):
                    mm = te.matmul(ps[0:64, 6, 2 * h:2 * h + 2], hd(ld, h), ind[:, :], start=True, stop=True)
                mm.then_inc(pe.sem, pe.step("sums"))
                te.wait_ge(dve.sem, dve.at("scaled", t))
                for b, z in enumerate((al, rh, be, ka)):
                    for j in range(4):
                        mm = te.transpose(ps[:, b, j * P:(j + 1) * P], z[:, j * P:(j + 1) * P], I)
                mm.then_inc(pe.sem, pe.step("turned"))
                te.wait_ge(act.sem, act.at("arT", t))
                te.wait_ge(dve.sem, dve.at("bkT", t))

                def four(q, bank, lhsT, rhs, n=P):
                    for i in range(4):
                        mm = te.matmul(ps[:, 4 * q + bank, i * n:(i + 1) * n], lhsT[q][:, i, :], rhs(q, i),
                                       start=True, stop=True)
                    return mm

                of = lambda z: lambda q, i: z[q][:, i, :]
                for q in groups:
                    o = slice(64 * q, 64 * q + 64)
                    for i in range(4):
                        for b, lhsT, rhs in ((0, beT[o, i, :], arT[o, i, 0, :]), (1, arT[o, i, 0, :], beT[o, i, :]),
                                             (2, kaT[o, i, :], arT[o, i, 0, :]), (3, beT[o, i, :], arT[o, i, 1, :])):
                            mm = te.matmul(ps[:, 4 * q + b, i * P:(i + 1) * P], lhsT, rhs, start=True, stop=True)
                    mm.then_inc(pe.sem, pe.step(f"scores_{q}"))
                for q in groups:
                    te.wait_ge(dve.sem, dve.at(f"masked_{q}", t))
                    four(q, 0, N1, of(M1))
                    four(q, 1, M1, of(N1))
                    four(q, 2, Km, lambda q, i: hd(v, 2 * i + q), 64).then_inc(pe.sem, pe.step(f"p2_{q}"))
                for q in groups:
                    o = slice(64 * q, 64 * q + 64)
                    te.wait_ge(dve.sem, dve.at(f"x1_{q}", t))
                    te.sem_inc(passed, 1)
                    for i in range(4):
                        mm = te.matmul(ps[:, 4 * q + 3, i * P:(i + 1) * P], kaT[o, i, :], arT[o, i, 1, :],
                                       start=True, stop=True)
                    mm.then_inc(pe.sem, pe.step(f"qk_{q}"))
                for q in groups:
                    te.wait_ge(act.sem, act.at(f"p2_{q}", t))
                    te.wait_ge(dve.sem, dve.at(f"p2_{q}", t))
                    four(q, 0, XT, of(M2))
                    four(q, 1, M2, of(XT))
                    four(q, 2, N2, of(M2))
                    four(q, 3, M2, of(N2)).then_inc(pe.sem, pe.step(f"x2_{q}"))
                for q in groups:
                    te.wait_ge(act.sem, act.at(f"x2_{q}", t))
                    te.wait_ge(dve.sem, dve.at(f"x2_{q}", t))
                    four(q, 0, XT, of(M4))
                    four(q, 1, M4, of(XT))
                    four(q, 2, N4, of(M4)).then_inc(pe.sem, pe.step(f"x4_{q}"))
                for q in groups:
                    te.wait_ge(act.sem, act.at(f"x4_{q}", t))
                    te.wait_ge(dve.sem, dve.at(f"x4_{q}", t))
                    four(q, 0, XT, of(M8))
                    four(q, 1, M8, of(XT)).then_inc(pe.sem, pe.step(f"x8_{q}"))
                before = "x8"
                for n, off in ((32, N32), (64, N64)):
                    for q in groups:
                        te.wait_ge(dve.sem, dve.at(f"{before}_{q}", t))
                        four(q, 2, off, of(X)).then_inc(pe.sem, pe.step(f"z{n}_{q}"))
                    for q in groups:
                        te.wait_ge(act.sem, act.at(f"z{n}_{q}", t))
                        mm = four(q, 0, XT, of(Z))
                        if n == 32:
                            mm = four(q, 1, Z, of(XT))
                        mm.then_inc(pe.sem, pe.step(f"x{n}_{q}"))
                    before = f"x{n}"
                te.wait_ge(pool.sem, pool.at("alpha", t))
                for q in groups:
                    te.wait_ge(dve.sem, dve.at(f"x64_{q}", t))
                    four(q, 1, X, lambda q, i: aKV[q][:, i, :, :].rearrange("p a c -> p (a c)"))\
                        .then_inc(pe.sem, pe.step(f"ag_{q}"))
                for q in groups:
                    te.wait_ge(act.sem, act.at(f"ag_{q}", t))
                    for i in range(4):
                        h = 2 * i + q
                        e = ps[0:64, 4 * q, i * P:(i + 1) * P]
                        te.matmul(e, hd(rh, h), I, start=True, stop=False)
                        te.matmul(e, AG[q][:, i, 0, :], QB[q][:, i, :], start=False, stop=True)
                        f = ps[:, 4 * q + 1, i * 64:(i + 1) * 64]
                        te.matmul(f, QK[q][:, i, :], hd(v, h), start=True, stop=False)
                        te.matmul(f, QB[q][:, i, :], AG[q][:, i, 1, :], start=False, stop=True)
                        for c in range(2):
                            o, n, b = slice(64 * c, 64 * c + 64), 64 * i, 4 * q + 2 + c
                            te.matmul(ps[0:64, b, n:n + 64], AG[q][o, i, 0, :], hd(bE, h)[o, :], start=True, stop=True)
                            n += 256
                            te.matmul(ps[0:64, b, n:n + 64], hd(kE, h)[o, :], hd(v, h)[o, :], start=True, stop=False)
                            mm = te.matmul(ps[0:64, b, n:n + 64], hd(bE, h)[o, :], AG[q][o, i, 1, :], start=False, stop=True)
                    mm.then_inc(pe.sem, pe.step(f"eh_{q}"))
                for c in range(2):
                    te.wait_ge(dve.sem, dve.at("s0" if c else "eh_1", t))
                    te.sem_inc(passed, 1)
                    te.wait_ge(act.sem, act.at("eh_1", t))
                    te.sem_inc(passed, 1)
                    o = slice(64 * c, 64 * c + 64)
                    for h in range(RH):
                        te.matmul(ps[o, 6, h * 64:(h + 1) * 64], ET[:, h, o], S[:, h, :], start=True, stop=True)
                        mm = te.matmul(ps[0:64, 7, h * 64:(h + 1) * 64], HT[:, h, c, :], S[:, h, :], start=True, stop=True)
                    mm.then_inc(pe.sem, pe.step(f"y{c}"))


AH, AD = 4, 64
AV = 2 * AD
LAM_INIT = 0.8 - 0.6 * math.exp(-0.3 * 0)
NEG = -1e30


def rope_consts():
    inv = np.float32(10000.0) ** (-np.arange(0, AD, 2, dtype=np.float32) / np.float32(AD))
    ang = np.arange(SEQ, dtype=np.float32)[:, None] * inv[None, :].astype(np.float32)
    c, s = np.cos(ang), np.sin(ang)
    return np.concatenate([c, c, -s, s], axis=1).astype(np.float32)


def attention(nc, proj, col, out, g):
    with Phase(nc, "att") as ph:
        ident = ph.sb("ident", [P, P])
        causal = ph.sb("causal", [P, P])
        gains = ph.sb("gains", [P, 2, AD])
        subw = ph.sb("subw", [P, AV])
        lq = ph.sb("lq", [P, 4, AD])
        lam = ph.sb("lam", [P, 8])
        rope = ph.sb("rope", [P, NT, 2, AD])
        rg = ph.sb("rg", [P, NT, 2, 2, AD])
        pair = range(2)
        two = lambda n, shape: [ph.sb(f"{n}{b}", shape) for b in pair]
        qk = two("qk", [P, 16, AD])
        sq = two("sq", [P, 16, AD])
        n16 = two("n16", [P, 4, 16])
        qkT = ph.sb("qkT", [P, 2, AH, SEQ])
        qh = two("qh", [P, SEQ])
        kh = two("kh", [P, SEQ])
        vh = two("vh", [P, NT, AV])
        e = [two(f"e{c}_", [P, SEQ]) for c in range(2)]
        at = two("at", [P, SEQ])
        aT = two("aT", [P, SEQ])
        mx = two("mx", [P, 2, 2])
        sm = two("sm", [P, 2])
        rs = two("rs", [P, 3])
        o = two("o", [P, NT, AV])
        o2 = ph.sb("o2", [P, NT, AV])
        on = two("on", [P, NT, AV])
        n8 = ph.sb("n8", [P, 4, NT])
        ps = ph.psum()
        const_in, passed = ph.sem("const_in"), ph.sem("passed")
        x_in = [ph.sem(f"x_in{b}") for b in pair]
        h_in = [ph.sem(f"h_in{b}") for b in pair]
        o_st = ph.sem("o_st")
        lams = ph.marks("lam", "dots exps")
        tab = ph.marks("tab", "gains")
        pa = ph.steps("prep_act", "root_0 root_1 qkT_0 qkT_1")
        pd = ph.steps("prep_dve", "mean_0 mean_1 roped_0 roped_1")
        pp = ph.steps("prep_pe", "turned_0 turned_1")
        N = 2 * NT
        act = ph.steps("act", " ".join(f"exp{s}_0 exp{s}_1 aT{s - 1}" if s else "exp0_0 exp0_1" for s in range(N))
                       + f" aT{N - 1} root_0 root_1")
        dve = ph.steps("dve", "max0_0 max0_1 " + " ".join(
            f"attn{s}" + (f" max{s + 1}_0 max{s + 1}_1" if s < N - 1 else "") + (f" o{s - 1}" if s else "") for s in range(N))
            + f" o{N - 1} mean_0 mean_1 out_0 out_1")
        pe = ph.steps("pe", "scores0_0 scores0_1 " + " ".join(
            (f"scores{s + 1}_0 scores{s + 1}_1 " if s < N - 1 else "") + (f"o{s - 1} " if s else "") + f"turned{s}"
            for s in range(N)) + f" o{N - 1}")
        blk = ph.block()
        width = lambda i: (i % NT + 1) * P
        row = lambda b: banks(ps, b)
        SC = AD ** -0.5

        @blk.sync
        def _(sp):
            for dst, src in ((ident[:, :], g["ident"]), (causal[:, :], g["causal"]),
                             (rope[:, :, :, :].rearrange("p t a d -> p t (a d)"), g["rope"].rearrange("(t p) c -> p t c", p=P)),
                             (gains[:, 0, :], g["q_norm"].partition_broadcast(P)),
                             (gains[:, 1, :], g["k_norm"].partition_broadcast(P)),
                             (subw[:, :], g["subln_w"].partition_broadcast(P)),
                             (lq[:, 0, :], g["lambda_q1"].partition_broadcast(P)),
                             (lq[:, 1, :], g["lambda_q2"].partition_broadcast(P)),
                             (lq[:, 2, :], g["lambda_k1"].partition_broadcast(P)),
                             (lq[:, 3, :], g["lambda_k2"].partition_broadcast(P))):
                sp.dma_start(dst, src).then_inc(const_in, 16)
            def load(t, b):
                sp.dma_start(qk[b][:, :, :].rearrange("p g d -> p (g d)"), proj[bass.ds(t * P, P), col:col + 1024])\
                    .then_inc(x_in[b], 16)

            for b in pair:
                load(b, b)
            with sp.Fori(0, NT // 2 - 1) as j:
                for b in pair:
                    sp.wait_ge(pp.sem, pp.at(f"turned_{b}", j))
                    sp.sem_inc(passed, 1)
                    load(2 * j + 2 + b, b)
            sp.wait_ge(pa.sem, pa.start(NT // 2))

            def load_head(h):
                sp.dma_start(qh[h % 2][:, :], qkT[:, 0, h:h + 1, :]).then_inc(h_in[h % 2], 16)
                sp.dma_start(kh[h % 2][:, :], qkT[:, 1, h:h + 1, :]).then_inc(h_in[h % 2], 16)
                sp.dma_start(vh[h % 2][:, :, :], proj[:, h * AV + col + 1024:(h + 1) * AV + col + 1024]
                             .rearrange("(t p) d -> p t d", p=P)).then_inc(h_in[h % 2], 16)

            for h in range(2):
                load_head(h)
            for h in range(AH):
                if h + 2 < AH:
                    sp.wait_ge(pe.sem, pe.at(f"o{NT * (h % 2 + 1) - 1}", h // 2))
                    load_head(h + 2)
            sp.wait_ge(o_st, 16 * (AH + 1))

        @blk.gpsimd
        def _(po):
            po.wait_ge(const_in, 160)
            for a in range(2):
                po.tensor_tensor(rg[:, :, a, 0, :], rope[:, :, 0, :], over(gains[:, a, :], NT), ALU.mult)
                for lo, hi in ((slice(0, 32), slice(32, 64)), (slice(32, 64), slice(0, 32))):
                    last = po.tensor_tensor(rg[:, :, a, 1, lo], rope[:, :, 1, lo], over(gains[:, a, hi], NT), ALU.mult)
            last.then_inc(tab.sem, tab.step("gains"))

        @blk.scalar
        def _(s):
            s.wait_ge(lams.sem, 1)
            s.activation(lam[:, 2:4], lam[:, 0:2], ACT.Exp).then_inc(lams.sem, lams.step("dots"))
            pa.begin(s)
            with s.Fori(0, NT // 2) as j:
                for b in pair:
                    s.wait_ge(pd.sem, pd.at(f"mean_{b}", j))
                    s.activation(n16[b][:, 1, :], n16[b][:, 0, :], ACT.Sqrt).then_inc(pa.sem, pa.step(f"root_{b}"))
                for b in pair:
                    s.wait_ge(pp.sem, pp.at(f"turned_{b}", j))
                    s.activation(qkT[:, :, :, bass.ds((2 * j + b) * P, P)].rearrange("p a h c -> p (a h) c"),
                                 ps[:, 2 * b:2 * b + 2, :].rearrange("p b (h c) -> p (b h) c", c=P), ACT.Copy)\
                        .then_inc(pa.sem, pa.step(f"qkT_{b}"))
            act.begin(s)
            s.sem_inc(o_st, 16)

            def turn(i):
                s.wait_ge(pe.sem, pe.at(f"turned{i}", j))
                s.activation(aT[i % 2][:, 0:width(i)], row(4)[:, 0:width(i)], ACT.Copy).then_inc(act.sem, act.step(f"aT{i}"))

            with s.Fori(0, AH // 2) as j:
                for i in range(N):
                    for c in range(2):
                        s.wait_ge(dve.sem, dve.at(f"max{i}_{c}", j))
                        s.activation(e[c][i % 2][:, 0:width(i)], row(2 * c)[:, 0:width(i)], ACT.Exp,
                                     bias=mx[i % 2][:, 1, c:c + 1], scale=SC, accum_out=sm[i % 2][:, c:c + 1])\
                            .then_inc(act.sem, act.step(f"exp{i}_{c}"))
                    if i:
                        turn(i - 1)
                turn(N - 1)
                for b in pair:
                    s.wait_ge(dve.sem, dve.at(f"mean_{b}", j))
                    s.activation(n8[:, 2 * b + 1, :], n8[:, 2 * b, :], ACT.Sqrt).then_inc(act.sem, act.step(f"root_{b}"))
                for b in pair:
                    s.wait_ge(dve.sem, dve.at(f"out_{b}", j))
                    s.sem_inc(passed, 1)
                    s.dma_start(out[:, bass.ds((2 * j + b) * AV, AV)].rearrange("(t p) d -> p t d", p=P),
                                on[b][:, :, :]).then_inc(o_st, 16)

        @blk.vector
        def _(ve):
            tt = ve.tensor_tensor
            ve.wait_ge(const_in, 160)
            tt(lq[:, 0:2, :], lq[:, 0:2, :], lq[:, 2:4, :], ALU.mult)
            ve.drain()
            ve.tensor_reduce(lam[:, 0:2], lq[:, 0:2, :], AX, ALU.add).then_inc(lams.sem, 1)
            ve.drain()
            ve.wait_ge(lams.sem, 2)
            tt(lam[:, 4:5], lam[:, 3:4], lam[:, 2:3], ALU.subtract)
            ve.drain()
            ve.tensor_scalar(lam[:, 5:6], lam[:, 4:5], LAM_INIT, None, ALU.subtract)
            ve.drain()
            ve.wait_ge(tab.sem, 1)
            pd.begin(ve)
            with ve.Fori(0, NT // 2) as j:
                for b in pair:
                    ve.drain()
                    ve.wait_ge(x_in[b], 16 * j + 16)
                    tt(sq[b][:, :, :], qk[b][:, :, :], qk[b][:, :, :], ALU.mult)
                    ve.drain()
                    ve.tensor_reduce(n16[b][:, 2, :], sq[b][:, :, :], AX, ALU.add)
                    ve.drain()
                    ve.tensor_scalar(n16[b][:, 0, :], n16[b][:, 2, :], 1.0 / AD, EPS, ALU.mult, ALU.add)\
                        .then_inc(pd.sem, pd.step(f"mean_{b}"))
                for b in pair:
                    q, s2 = qk[b], sq[b]
                    ve.drain()
                    ve.wait_ge(pa.sem, pa.at(f"root_{b}", j))
                    ve.reciprocal(n16[b][:, 3, :], n16[b][:, 1, :])
                    ve.drain()
                    tt(q[:, :, :], q[:, :, :], bcast(n16[b][:, 3, :], AD), ALU.mult)
                    ve.drain()
                    table = rg[:, bass.ds(2 * j + b, 1), :, :, :].rearrange("p o a c d -> p (o a) c d")
                    for a in range(2):
                        part, cs, sn = slice(8 * a, 8 * a + 8), table[:, a, 0, :], table[:, a, 1, :]
                        tt(s2[:, part, 0:32], q[:, part, 32:64], over(sn[:, 0:32], 8), ALU.mult)
                        tt(s2[:, part, 32:64], q[:, part, 0:32], over(sn[:, 32:64], 8), ALU.mult)
                    ve.drain()
                    for a in range(2):
                        part, cs = slice(8 * a, 8 * a + 8), table[:, a, 0, :]
                        tt(q[:, part, :], q[:, part, :], over(cs, 8), ALU.mult)
                    ve.drain()
                    tt(q[:, :, :], q[:, :, :], s2[:, :, :], ALU.add).then_inc(pd.sem, pd.step(f"roped_{b}"))

            def largest(i):
                W = width(i)
                for c in range(2):
                    ve.drain()
                    ve.wait_ge(pe.sem, pe.at(f"scores{i}_{c}", j))
                    sc = row(2 * c)
                    tt(sc[:, W - P:W], sc[:, W - P:W], causal[:, :], ALU.add)
                    ve.drain()
                    ve.tensor_reduce(mx[i % 2][:, 0, c:c + 1], sc[:, 0:W], AX, ALU.max)
                    ve.drain()
                    ve.tensor_scalar(mx[i % 2][:, 1, c:c + 1], mx[i % 2][:, 0, c:c + 1], -SC, None, ALU.mult)\
                        .then_inc(dve.sem, dve.step(f"max{i}_{c}"))

            def output(i):
                ve.drain()
                ve.wait_ge(pe.sem, pe.at(f"o{i}", j))
                ve.tensor_scalar(o[i // NT][:, i % NT, :], ps[:, 6 + i % 2, 0:AV], rs[i % 2][:, 0:1], None, ALU.mult)\
                    .then_inc(dve.sem, dve.step(f"o{i}"))

            dve.begin(ve)
            with ve.Fori(0, AH // 2) as j:
                largest(0)
                for i in range(N):
                    W, b = width(i), i % 2
                    ve.drain()
                    ve.wait_ge(act.sem, act.at(f"exp{i}_1", j))
                    ve.reciprocal(rs[b][:, 0:2], sm[b][:, :])
                    ve.drain()
                    ve.scalar_tensor_tensor(rs[b][:, 2:3], rs[b][:, 1:2], sm[b][:, 0:1], lam[:, 5:6], ALU.mult, ALU.mult)
                    ve.drain()
                    ve.scalar_tensor_tensor(at[b][:, 0:W], e[1][b][:, 0:W], rs[b][:, 2:3], e[0][b][:, 0:W], ALU.mult, ALU.add)\
                        .then_inc(dve.sem, dve.step(f"attn{i}"))
                    if i + 1 < N:
                        largest(i + 1)
                    if i:
                        output(i - 1)
                output(N - 1)
                for b in pair:
                    ve.drain()
                    tt(o2[:, :, :], o[b][:, :, :], o[b][:, :, :], ALU.mult)
                    ve.drain()
                    ve.tensor_reduce(n8[:, 2 * b + 1, :], o2[:, :, :], AX, ALU.add)
                    ve.drain()
                    ve.tensor_scalar(n8[:, 2 * b, :], n8[:, 2 * b + 1, :], 1.0 / AV, EPS, ALU.mult, ALU.add)\
                        .then_inc(dve.sem, dve.step(f"mean_{b}"))
                for b in pair:
                    ve.drain()
                    ve.wait_ge(act.sem, act.at(f"root_{b}", j))
                    ve.reciprocal(n8[:, 2 * b, :], n8[:, 2 * b + 1, :])
                    ve.drain()
                    ve.tensor_scalar(n8[:, 2 * b + 1, :], n8[:, 2 * b, :], 1.0 - LAM_INIT, None, ALU.mult)
                    ve.drain()
                    tt(o2[:, :, :], o[b][:, :, :], bcast(n8[:, 2 * b + 1, :], AV), ALU.mult)
                    ve.drain()
                    ve.wait_ge(o_st, 32 * j + 16)
                    tt(on[b][:, :, :], o2[:, :, :], over(subw[:, :], NT), ALU.mult).then_inc(dve.sem, dve.step(f"out_{b}"))

        @blk.tensor
        def _(te):
            te.wait_ge(const_in, 160)
            pp.begin(te)
            with te.Fori(0, NT // 2) as j:
                for b in pair:
                    te.wait_ge(pd.sem, pd.at(f"roped_{b}", j))
                    te.wait_ge(pa.sem, pa.start(j))
                    for t in range(8):
                        mm = te.transpose(block_of(ps, 2 * b, t), qk[b][:, 2 * t:2 * t + 2, :].rearrange("p a d -> p (a d)"),
                                          ident[:, :])
                    mm.then_inc(pp.sem, pp.step(f"turned_{b}"))
            te.wait_ge(pa.sem, pa.start(NT // 2))

            def scores(i):
                b, at_q = i // NT, (i % NT) * P
                if i % NT == 0:
                    te.wait_ge(h_in[b], 48 * j + 48)
                for c in range(2):
                    half = slice(64 * c, 64 * c + 64)
                    if i:
                        te.wait_ge(act.sem, act.at(f"exp{i - 1}_{c}", j))
                    for n in range(0, width(i), 512):
                        m = min(512, width(i) - n)
                        mm = te.matmul(ps[:, 2 * c + n // 512, 0:m], qh[b][half, at_q:at_q + P], kh[b][half, n:n + m],
                                       start=True, stop=True)
                    mm.then_inc(pe.sem, pe.step(f"scores{i}_{c}"))

            def output(i):
                te.wait_ge(act.sem, act.at(f"aT{i}", j))
                if i > 1:
                    te.wait_ge(dve.sem, dve.at(f"o{i - 2}", j))
                last = i % NT
                for k in range(last + 1):
                    mm = te.matmul(ps[:, 6 + i % 2, 0:AV], aT[i % 2][:, k * P:(k + 1) * P], vh[i // NT][:, k, :],
                                   start=(k == 0), stop=(k == last))
                mm.then_inc(pe.sem, pe.step(f"o{i}"))

            pe.begin(te)
            with te.Fori(0, AH // 2) as j:
                te.wait_ge(act.sem, act.start(j))
                te.sem_inc(passed, 1)
                te.wait_ge(dve.sem, dve.start(j))
                te.sem_inc(passed, 1)
                scores(0)
                for i in range(N):
                    if i + 1 < N:
                        scores(i + 1)
                    if i:
                        output(i - 1)
                    te.wait_ge(dve.sem, dve.at(f"attn{i}", j))
                    for k in range(i % NT + 1):
                        mm = te.transpose(block_of(ps, 4, k), at[i % 2][:, k * P:(k + 1) * P], ident[:, :])
                    mm.then_inc(pe.sem, pe.step(f"turned{i}"))
                output(N - 1)


SH, SP_, SG, SN = 16, 64, 2, 128
SW = SH * SP_
XBC = SW + 2 * SG * SN
NX = XBC // P
TAPS = 4
COL_Z, COL_XBC, COL_DT = 0, SW, SW + XBC
COL_Q = COL_DT + SH
COL_F, COL_I, COL_G = COL_Q + 512, COL_Q + 1024, COL_Q + 1536
COL_U, COL_SG = COL_Q + 2048, COL_Q + 2560


def ssd_masks():
    s, l = np.arange(P)[:, None], np.arange(P)[None, :]
    m = [s == l, s <= l, (s == P - 1) & (l >= 0)]
    sel = np.zeros((P, SH * P), np.float32)
    for h in range(SH):
        sel[h, h * P:(h + 1) * P] = 1
    return np.concatenate([a.astype(np.float32) for a in m] + [sel], axis=1)


def ssd(nc, proj, out, masks_d, g):
    with Phase(nc, "ssd") as ph:
        masks = ph.sb("masks", [P, (3 + SH) * P])
        ident, cum, last = (masks[:, i * P:(i + 1) * P] for i in range(3))
        sel = masks[0:SH, 3 * P:]
        cw = ph.sb("cw", [P, TAPS, NX])
        cb = ph.sb("cb", [P, NX])
        rows = ph.sb("rows", [P, 3, SH])
        nw = ph.sb("nw", [P, SW])
        dt = ph.sb("dt", [P, NT, SH])
        w8 = ph.sb("w8", [P, 8, NT * SH])
        acum = ph.sb("acum", [P, NT, SH])
        eac = ph.sb("eac", [P, NT, SH])
        dte = ph.sb("dte", [P, NT, SH])
        cdec = ph.sb("cdec", [P, NT, SH])
        z = ph.sb("z", [P, SW])
        xbc = ph.sb("xbc", [P, XBC])
        xF = ph.sb("xF", [P, NX, 3 + P])
        cF = ph.sb("cF", [P, NX, P])
        sF = ph.sb("sF", [P, NX, P])
        xs = ph.sb("xs", [P, SH, SP_])
        Bt = ph.sb("Bt", [P, SG, SN])
        a1 = ph.sb("a1", [P, SH])
        aT = ph.sb("aT", [SH, P])
        seg = ph.sb("seg", [P, SH, P])
        sm = ph.sb("sm", [P, SG, P])
        xdt = ph.sb("xdt", [P, SH, SP_])
        xdd = ph.sb("xdd", [P, SH, SP_])
        S = ph.sb("S", [P, SH, SP_])
        y = ph.sb("y", [P, SH, SP_])
        y2 = ph.sb("y2", [P, SH, SP_])
        gz = ph.sb("gz", [P, SW])
        ss = ph.sb("ss", [P, 4, SG])
        yo = ph.sb("yo", [P, SW])
        ps = ph.psum()
        const_in, x_in, y_st, passed = (ph.sem(n) for n in ("const_in", "x_in", "y_st", "passed"))
        pre_d = ph.marks("pre_dve", "biased dta acum diffs")
        pre_a = ph.marks("pre_act", "exps cum")
        pre_p = ph.marks("pre_pe", "acum last")
        act = ph.steps("act", "xF silu xs gate decay root")
        dve = ph.steps("dve", "halo conv aT xin seg masked state out1 mean out")
        pe = ph.steps("pe", "turned xturned rows sums")
        blk = ph.block()

        @blk.sync
        def _(sp):
            for dst, src in ((masks[:, :], masks_d),
                             (cw[:, :, :], g["ssd_conv_w_2"].rearrange("j (k p) -> p j k", p=P)),
                             (cb[:, :], g["ssd_conv_b_2"].rearrange("(k p) -> p k", p=P)),
                             (rows[:, 0, :], g["ssd_dt_bias_2"].partition_broadcast(P)),
                             (rows[:, 1, :], g["ssd_a_log_2"].partition_broadcast(P)),
                             (rows[:, 2, :], g["ssd_d_2"].partition_broadcast(P)),
                             (nw[:, :], g["ssd_norm_w_2"].partition_broadcast(P)),
                             (dt[:, :, :], proj[:, COL_DT:COL_DT + SH].rearrange("(t p) h -> p t h", p=P))):
                sp.dma_start(dst, src, allow_slow_non_contiguous=True).then_inc(const_in, 16)
            sp.sem_inc(y_st, 16)
            with sp.Fori(0, NT) as t:
                sp.wait_ge(dve.sem, dve.start(t))
                sp.dma_start(xbc[:, :], proj[bass.ds(t * P, P), COL_XBC:COL_XBC + XBC]).then_inc(x_in, 16)
                sp.dma_start(z[:, :], proj[bass.ds(t * P, P), COL_Z:COL_Z + SW]).then_inc(x_in, 16)
                sp.wait_ge(dve.sem, dve.at("out", t))
                sp.sem_inc(passed, 1)
                sp.dma_start(out[bass.ds(t * P, P), :], yo[:, :]).then_inc(y_st, 16)
            sp.wait_ge(y_st, 16 * (NT + 1))

        @blk.scalar
        def _(s):
            s.wait_ge(pre_d.sem, 1)
            s.activation(w8[:, 2, :], w8[:, 1, :], ACT.Exp, scale=-1.0)
            s.activation(w8[:, 7, 0:SH], rows[:, 1, :], ACT.Exp).then_inc(pre_a.sem, pre_a.step("exps"))
            s.wait_ge(pre_d.sem, 4)
            s.activation(eac[:, :, :], acum[:, :, :], ACT.Exp)
            s.activation(dte[:, :, :].rearrange("p t h -> p (t h)"), w8[:, 0, :], ACT.Exp)
            s.activation(cdec[:, :, :].rearrange("p t h -> p (t h)"), w8[:, 3, :], ACT.Exp)\
                .then_inc(pre_a.sem, pre_a.step("cum"))
            act.begin(s)
            with s.Fori(0, NT) as t:
                s.wait_ge(dve.sem, dve.at("halo", t))
                s.wait_ge(pe.sem, pe.at("turned", t))
                s.activation(xF[:, :, 3:], blocks(ps, 0, NX), ACT.Copy).then_inc(act.sem, act.step("xF"))
                s.wait_ge(dve.sem, dve.at("conv", t))
                s.activation(sF[:, :, :], cF[:, :, :], ACT.Silu).then_inc(act.sem, act.step("silu"))
                s.wait_ge(pe.sem, pe.at("xturned", t))
                s.activation(xs[:, :, :].rearrange("p h d -> p (h d)"), banks(ps, 0), ACT.Copy)
                s.activation(Bt[:, :, :], blocks(ps, 2, 2), ACT.Copy).then_inc(act.sem, act.step("xs"))
                s.activation(gz[:, :], z[:, :], ACT.Silu).then_inc(act.sem, act.step("gate"))
                s.wait_ge(dve.sem, dve.at("seg", t))
                s.activation(seg[:, :, :], seg[:, :, :], ACT.Exp).then_inc(act.sem, act.step("decay"))
                s.wait_ge(dve.sem, dve.at("mean", t))
                s.activation(ss[:, 2, :], ss[:, 1, :], ACT.Sqrt).then_inc(act.sem, act.step("root"))

        @blk.vector
        def _(ve):
            tt, ts, stt = ve.tensor_tensor, ve.tensor_scalar, ve.scalar_tensor_tensor
            ve.memset(S[:, :, :], 0.0)
            ve.memset(xF[:, :, P:], 0.0)
            ve.drain()
            ve.wait_ge(const_in, 128)
            v, av, e, zz, z2, pl, tmp, na = (w8[:, i, :] for i in range(8))
            dtf = dt[:, :, :].rearrange("p t h -> p (t h)")
            tt(v.rearrange("p (t h) -> p t h", h=SH), dt[:, :, :], over(rows[:, 0, :], NT), ALU.add)
            ve.drain()
            stt(av, v, -1.0, v, ALU.mult, ALU.max).then_inc(pre_d.sem, pre_d.step("biased"))
            ve.drain()
            ve.wait_ge(pre_a.sem, 1)
            ts(tmp, e, 2.0, None, ALU.add)
            ve.drain()
            ve.reciprocal(pl, tmp)
            ve.drain()
            tt(zz, e, pl, ALU.mult)
            ve.drain()
            tt(z2, zz, zz, ALU.mult)
            ve.drain()
            ts(pl, z2, 1.0 / 17, 1.0 / 15, ALU.mult, ALU.add)
            for n in (13, 11, 9, 7, 5, 3, 1):
                ve.drain()
                tt(pl, pl, z2, ALU.mult)
                ve.drain()
                ts(pl, pl, 1.0 / n, None, ALU.add)
            ve.drain()
            tt(pl, pl, zz, ALU.mult)
            ts(v, v, 0.0, None, ALU.max)
            ve.drain()
            stt(dtf, pl, 2.0, v, ALU.mult, ALU.add)
            ve.drain()
            tt(tmp.rearrange("p (t h) -> p t h", h=SH), dt[:, :, :], over(na[:, 0:SH], NT), ALU.mult)
            ve.drain()
            ts(tmp, tmp, -1.0, None, ALU.mult).then_inc(pre_d.sem, pre_d.step("dta"))
            ve.drain()
            ve.wait_ge(pre_p.sem, 1)
            acf = acum[:, :, :].rearrange("p t h -> p (t h)")
            ve.tensor_copy(acf, ps[:, 0, 0:P]).then_inc(pre_d.sem, pre_d.step("acum"))
            ve.drain()
            ve.wait_ge(pre_p.sem, 2)
            ve.tensor_copy(zz, ps[:, 1, 0:P])
            ve.drain()
            tt(v, zz, acf, ALU.subtract)
            ve.drain()
            ts(v, v, 0.0, None, ALU.min).then_inc(pre_d.sem, pre_d.step("diffs"))
            ve.drain()
            ve.wait_ge(pre_a.sem, 2)
            dve.begin(ve)
            with ve.Fori(0, NT) as t:
                th = bass.ds(t, 1)
                row = lambda z: z[:, th, :].rearrange("p o h -> p (o h)")
                ve.drain()
                ve.tensor_copy(xF[:, :, 0:3], xF[:, :, P:P + 3]).then_inc(dve.sem, dve.step("halo"))
                ve.tensor_copy(a1[:, :], row(acum))
                ve.drain()
                ve.wait_ge(act.sem, act.at("xF", t))
                for k in range(NX):
                    ts(cF[:, k, :], xF[:, k, 0:P], cw[:, 0, k:k + 1], cb[:, k:k + 1], ALU.mult, ALU.add)
                for j in range(1, TAPS):
                    ve.drain()
                    for k in range(NX):
                        ins = stt(cF[:, k, :], xF[:, k, j:j + P], cw[:, j, k:k + 1], cF[:, k, :], ALU.mult, ALU.add)
                ins.then_inc(dve.sem, dve.step("conv"))
                ve.drain()
                ve.wait_ge(pe.sem, pe.at("xturned", t))
                ve.tensor_copy(aT[:, :], ps[0:SH, 3, 0:P]).then_inc(dve.sem, dve.step("aT"))
                ve.drain()
                ve.wait_ge(act.sem, act.at("xs", t))
                tt(xdt[:, :, :], xs[:, :, :], bcast(row(dt), SP_), ALU.mult)
                ve.drain()
                tt(xdd[:, :, :], xdt[:, :, :], bcast(row(dte), SP_), ALU.mult).then_inc(dve.sem, dve.step("xin"))
                ve.drain()
                ve.wait_ge(pe.sem, pe.at("rows", t))
                for b in range(4):
                    tt(seg[:, 4 * b:4 * b + 4, :], blocks(ps, 3 + b, 4), bcast(a1[:, 4 * b:4 * b + 4], P), ALU.subtract)
                ve.drain()
                ts(seg[:, :, :], seg[:, :, :], 0.0, None, ALU.min).then_inc(dve.sem, dve.step("seg"))
                tt(sm[:, :, :], blocks(ps, 7, 2), over(cum, 2), ALU.mult)
                ve.drain()
                ve.wait_ge(act.sem, act.at("decay", t))
                for q in range(2):
                    ins = tt(seg[:, 8 * q:8 * q + 8, :], seg[:, 8 * q:8 * q + 8, :], over(sm[:, q, :], 8), ALU.mult)
                ins.then_inc(dve.sem, dve.step("masked"))
                ve.drain()
                ve.wait_ge(pe.sem, pe.at("sums", t))
                tt(S[:, :, :], S[:, :, :], bcast(row(cdec), SP_), ALU.mult)
                h64 = lambda b: banks(ps, b).rearrange("p (h d) -> p h d", d=SP_)
                tt(y[:, :, :], h64(2), bcast(row(eac), SP_), ALU.mult)
                tt(y2[:, :, :], xs[:, :, :], bcast(rows[:, 2, :], SP_), ALU.mult)
                ve.drain()
                tt(S[:, :, :], S[:, :, :], h64(4), ALU.add).then_inc(dve.sem, dve.step("state"))
                tt(y[:, :, :], y[:, :, :], h64(0), ALU.add).then_inc(dve.sem, dve.step("out1"))
                ve.drain()
                tt(y[:, :, :], y[:, :, :], y2[:, :, :], ALU.add)
                ve.drain()
                yf = y[:, :, :].rearrange("p h d -> p (h d)")
                y2f = y2[:, :, :].rearrange("p (g h) d -> p g (h d)", g=SG)
                yg = y[:, :, :].rearrange("p (g h) d -> p g (h d)", g=SG)
                tt(yf, yf, gz[:, :], ALU.mult)
                ve.drain()
                tt(y2f, yg, yg, ALU.mult)
                ve.drain()
                ve.tensor_reduce(ss[:, 0, :], y2f, AX, ALU.add)
                ve.drain()
                ts(ss[:, 1, :], ss[:, 0, :], 1.0 / 512, EPS, ALU.mult, ALU.add).then_inc(dve.sem, dve.step("mean"))
                ve.drain()
                ve.wait_ge(act.sem, act.at("root", t))
                ve.reciprocal(ss[:, 3, :], ss[:, 2, :])
                ve.drain()
                tt(yg, yg, bcast(ss[:, 3, :], 512), ALU.mult)
                ve.drain()
                ve.wait_ge(y_st, 16 * t + 16)
                tt(yo[:, :], yf, nw[:, :], ALU.mult).then_inc(dve.sem, dve.step("out"))
                ve.drain()

        @blk.tensor
        def _(te):
            te.wait_ge(const_in, 128)
            te.wait_ge(pre_d.sem, 2)
            te.matmul(ps[:, 0, 0:P], cum, w8[:, 6, :], start=True, stop=True).then_inc(pre_p.sem, pre_p.step("acum"))
            te.wait_ge(pre_d.sem, 3)
            te.matmul(ps[:, 1, 0:P], last, acum[:, :, :].rearrange("p t h -> p (t h)"), start=True, stop=True)\
                .then_inc(pre_p.sem, pre_p.step("last"))
            te.wait_ge(pre_d.sem, 4)
            pe.begin(te)
            with te.Fori(0, NT) as t:
                te.wait_ge(dve.sem, dve.start(t))
                te.wait_ge(x_in, 32 * t + 32)
                for k in range(NX):
                    mm = te.transpose(block_of(ps, 0, k), xbc[:, k * P:(k + 1) * P], ident)
                mm.then_inc(pe.sem, pe.step("turned"))
                te.wait_ge(act.sem, act.at("silu", t))
                for k in range(10):
                    te.transpose(block_of(ps, 0, k), sF[:, k, :], ident)
                te.transpose(ps[0:SH, 3, 0:P], a1[:, :], ident).then_inc(pe.sem, pe.step("xturned"))
                te.wait_ge(dve.sem, dve.at("aT", t))
                for q in range(SG):
                    te.matmul(ps[:, 7, q * P:(q + 1) * P], sF[:, 8 + q, :], sF[:, 10 + q, :], start=True, stop=True)
                for h in range(SH):
                    mm = te.matmul(block_of(ps, 3, h), sel[:, h * P:(h + 1) * P], aT[:, :], start=True, stop=True)
                mm.then_inc(pe.sem, pe.step("rows"))
                te.wait_ge(dve.sem, dve.at("masked", t))
                for h in range(SH):
                    te.matmul(ps[:, h // 8, (h % 8) * 64:(h % 8 + 1) * 64], seg[:, h, :], xdt[:, h, :], start=True, stop=True)
                for q in range(SG):
                    hq = slice(8 * q, 8 * q + 8)
                    te.matmul(ps[:, 2 + q, :], sF[:, 10 + q, :], S[:, hq, :].rearrange("p h d -> p (h d)"),
                              start=True, stop=True)
                    mm = te.matmul(ps[:, 4 + q, :], Bt[:, q, :], xdd[:, hq, :].rearrange("p h d -> p (h d)"),
                                   start=True, stop=True)
                mm.then_inc(pe.sem, pe.step("sums"))


HH, HD = 4, 128


def hgrn_masks():
    t, l = np.arange(P)[:, None], np.arange(P)[None, :]
    same = lambda n: (t // n) == (l // n)
    b16 = l // 32 * 32 + 16
    lev = same(32) & np.where(l >= b16, (t >= b16) & (t <= l), (t > l) & (t < b16))
    b8 = l // 16 * 16 + 8
    mid = np.where(same(16) & (l >= b8) & (t >= b8) & (t <= l), 1, 0) - np.where(same(16) & (l < b8) & (t > l) & (t < b8), 1, 0)
    cum = same(32) & (t <= l)
    suf = same(32) & (t > l)
    cross = same(32) & ~same(16) & (t < l)
    diag = same(16) & (t <= l)
    return np.concatenate([a.astype(np.float32) for a in (t == l, lev, mid, cum, suf, cross, diag)], axis=1)


def hgrn(nc, proj, out, masks_d, g):
    W = HH * HD
    LIM = 85.0
    with Phase(nc, "hgrn") as ph:
        masks = ph.sb("masks", [P, 7 * P])
        ident, lev, mid, cum, suf, cross, diag = (masks[:, i * P:(i + 1) * P] for i in range(7))
        ind = ph.sb("ind", [P, 4])
        nw = ph.sb("nw", [P, W])
        x = ph.sb("x", [P, 4, W])
        lf = ph.sb("lf", [P, W])
        wk = ph.sb("wk", [P, 16, W])
        q, kf, ex, e1, e2, e2n, e3, e4, q1, k1, q2, k2, q3, k4, sp0, tmp = (wk[:, i, :] for i in range(16))
        gz = ph.sb("gz", [P, W])
        T = [ph.sb(f"T{i}", [P, HH, P]) for i in range(5)]
        at = ph.sb("at", [P, HH, P])
        a2 = ph.sb("a2", [P, HH, P])
        dec = ph.sb("dec", [P, HH, 4])
        kv = ph.sb("kv", [P, 4, W])
        S = ph.sb("S", [P, 5, W])
        y = ph.sb("y", [P, W])
        ss = ph.sb("ss", [P, 4, HH])
        yo = ph.sb("yo", [P, W])
        ps = ph.psum()
        const_in, x_in, y_st, passed = (ph.sem(n) for n in ("const_in", "x_in", "y_st", "passed"))
        act = ph.steps("act", "gates ln exps T34 root")
        dve = ph.steps("dve", "lf small scaled T at s mean out")
        pe = ph.steps("pe", "sums turned scores outs states")
        blk = ph.block()
        h4 = lambda z: z.rearrange("p (h d) -> p h d", d=HD)

        @blk.sync
        def _(sp):
            for dst, src in ((masks[:, :], masks_d), (ind[:, :], g["ind32"]), (nw[:, :], g["hgrn_norm_w_2"].partition_broadcast(P))):
                sp.dma_start(dst, src).then_inc(const_in, 16)
            sp.sem_inc(y_st, 16)
            with sp.Fori(0, NT) as t:
                sp.wait_ge(dve.sem, dve.start(t))
                sp.dma_start(x[:, :, :].rearrange("p a c -> p (a c)"), proj[bass.ds(t * P, P), COL_Q:COL_Q + 4 * W])\
                    .then_inc(x_in, 16)
                sp.wait_ge(dve.sem, dve.at("out", t))
                sp.sem_inc(passed, 1)
                sp.dma_start(out[bass.ds(t * P, P), :], yo[:, :]).then_inc(y_st, 16)
            sp.wait_ge(y_st, 16 * (NT + 1))

        @blk.scalar
        def _(s):
            act.begin(s)
            with s.Fori(0, NT) as t:
                s.wait_ge(dve.sem, dve.start(t))
                s.wait_ge(x_in, 16 * t + 16)
                s.activation(q, x[:, 0, :], ACT.Silu)
                s.activation(gz[:, :], x[:, 3, :], ACT.Silu)
                s.activation(kf, x[:, 1, :], ACT.Sigmoid, scale=-1.0)
                s.activation(tmp, x[:, 1, :], ACT.Abs)
                s.drain()
                s.activation(ex, tmp, ACT.Exp, scale=-1.0).then_inc(act.sem, act.step("gates"))
                s.drain()
                s.activation(sp0, ex, ACT.Ln, bias=1.0).then_inc(act.sem, act.step("ln"))
                s.wait_ge(pe.sem, pe.at("sums", t))
                s.activation(e1, ps[:, 0, :], ACT.Exp)
                s.activation(e3, ps[:, 2, :], ACT.Exp)
                s.activation(e4, ps[:, 3, :], ACT.Exp)
                s.activation(dec[:, :, :].rearrange("p h c -> p (h c)"), ps[:, 4, 0:16], ACT.Exp)
                s.wait_ge(dve.sem, dve.at("small", t))
                s.activation(e2, e2, ACT.Exp)
                s.activation(e2n, e2n, ACT.Exp).then_inc(act.sem, act.step("exps"))
                s.wait_ge(pe.sem, pe.at("turned", t))
                s.activation(T[4][:, :, :], blocks(ps, 5, 4), ACT.Copy)
                s.activation(T[3][:, :, :], blocks(ps, 3, 4), ACT.Copy).then_inc(act.sem, act.step("T34"))
                s.wait_ge(dve.sem, dve.at("mean", t))
                s.activation(ss[:, 2, :], ss[:, 1, :], ACT.Sqrt).then_inc(act.sem, act.step("root"))

        @blk.vector
        def _(ve):
            tt, ts, stt = ve.tensor_tensor, ve.tensor_scalar, ve.scalar_tensor_tensor
            ve.memset(S[:, :, :], 0.0)
            ve.memset(a2[:, :, :], 0.0)
            ve.drain()
            ve.wait_ge(const_in, 48)
            dve.begin(ve)
            with ve.Fori(0, NT) as t:
                ve.wait_ge(act.sem, act.at("ln", t))
                stt(lf[:, :], x[:, 1, :], 0.0, sp0, ALU.min, ALU.subtract).then_inc(dve.sem, dve.step("lf"))
                ve.drain()
                ve.tensor_copy(S[:, 0, :], S[:, 4, :])
                ve.drain()
                ve.wait_ge(pe.sem, pe.at("sums", t))
                ts(e2, ps[:, 1, :], LIM, -LIM, ALU.min, ALU.max)
                ve.drain()
                ts(e2n, e2, -1.0, None, ALU.mult).then_inc(dve.sem, dve.step("small"))
                ve.drain()
                ve.wait_ge(act.sem, act.at("exps", t))
                for o, a, b in ((q1, q, e1), (k1, kf, e1), (q2, q, e2), (k2, kf, e2n), (q3, q, e3), (k4, kf, e4)):
                    ins = tt(o, a, b, ALU.mult)
                ins.then_inc(dve.sem, dve.step("scaled"))
                ve.drain()
                ve.wait_ge(pe.sem, pe.at("turned", t))
                for i in range(3):
                    ins = ve.tensor_copy(T[i][:, :, :], blocks(ps, i, 4))
                ins.then_inc(dve.sem, dve.step("T"))
                ve.drain()
                ve.wait_ge(pe.sem, pe.at("scores", t))
                tt(at[:, :, :], blocks(ps, 6, 4), over(cross, 4), ALU.mult)
                ve.copy_predicated(a2[:, :, :], over(diag.bitcast(U32), 4), blocks(ps, 7, 4))
                ve.drain()
                tt(at[:, :, :], at[:, :, :], a2[:, :, :], ALU.add).then_inc(dve.sem, dve.step("at"))
                ve.drain()
                ve.wait_ge(pe.sem, pe.at("outs", t))
                ve.tensor_copy(y[:, :], ps[:, 0, :])
                for c in range(4):
                    ve.drain()
                    for h in range(HH):
                        hs = slice(h * HD, (h + 1) * HD)
                        ins = stt(S[:, c + 1, hs], S[:, c, hs], dec[:, h, c:c + 1], ps[:, 1 + c, hs], ALU.mult, ALU.add)
                ins.then_inc(dve.sem, dve.step("s"))
                ve.drain()
                ve.wait_ge(pe.sem, pe.at("states", t))
                tt(y[:, :], y[:, :], ps[:, 5, :], ALU.add)
                ve.drain()
                tt(tmp, y[:, :], y[:, :], ALU.mult)
                ve.drain()
                ve.tensor_reduce(ss[:, 0, :], h4(tmp), AX, ALU.add)
                ve.drain()
                ts(ss[:, 1, :], ss[:, 0, :], 1.0 / HD, EPS, ALU.mult, ALU.add).then_inc(dve.sem, dve.step("mean"))
                ve.drain()
                ve.wait_ge(act.sem, act.at("root", t))
                ve.reciprocal(ss[:, 3, :], ss[:, 2, :])
                ve.drain()
                tt(h4(y[:, :]), h4(y[:, :]), bcast(ss[:, 3, :], HD), ALU.mult)
                ve.drain()
                tt(y[:, :], y[:, :], nw[:, :], ALU.mult)
                ve.drain()
                ve.wait_ge(y_st, 16 * t + 16)
                tt(yo[:, :], y[:, :], gz[:, :], ALU.mult).then_inc(dve.sem, dve.step("out"))
                ve.drain()

        @blk.tensor
        def _(te):
            v = x[:, 2, :]
            te.wait_ge(const_in, 48)
            pe.begin(te)
            with te.Fori(0, NT) as t:
                te.wait_ge(dve.sem, dve.at("lf", t))
                for b, m in enumerate((lev, mid, cum, suf)):
                    te.matmul(ps[:, b, :], m, lf[:, :], start=True, stop=True)
                for h in range(HH):
                    mm = te.matmul(ps[:, 4, 4 * h:4 * h + 4], lf[:, h * HD:(h + 1) * HD], ind[:, :], start=True, stop=True)
                mm.then_inc(pe.sem, pe.step("sums"))
                te.wait_ge(dve.sem, dve.at("scaled", t))
                for b, z in ((0, q1), (1, k1), (2, q2), (3, k2), (5, q3)):
                    for h in range(HH):
                        mm = te.transpose(block_of(ps, b, h), z[:, h * HD:(h + 1) * HD], ident)
                mm.then_inc(pe.sem, pe.step("turned"))
                te.wait_ge(dve.sem, dve.at("T", t))
                for h in range(HH):
                    te.matmul(block_of(ps, 6, h), T[1][:, h, :], T[0][:, h, :], start=True, stop=True)
                te.wait_ge(act.sem, act.at("T34", t))
                for h in range(HH):
                    mm = te.matmul(block_of(ps, 7, h), T[3][:, h, :], T[2][:, h, :], start=True, stop=True)
                mm.then_inc(pe.sem, pe.step("scores"))
                te.wait_ge(dve.sem, dve.at("at", t))
                for h in range(HH):
                    te.matmul(block_of(ps, 0, h), at[:, h, :], v[:, h * HD:(h + 1) * HD], start=True, stop=True)
                for c in range(4):
                    o = slice(32 * c, 32 * c + 32)
                    for h in range(HH):
                        hs = slice(h * HD, (h + 1) * HD)
                        mm = te.matmul(ps[:, 1 + c, hs], k4[o, hs], v[o, hs], start=True, stop=True)
                mm.then_inc(pe.sem, pe.step("outs"))
                te.wait_ge(dve.sem, dve.at("s", t))
                te.sem_inc(passed, 1)
                for c in range(4):
                    o = slice(32 * c, 32 * c + 32)
                    for h in range(HH):
                        hs = slice(h * HD, (h + 1) * HD)
                        mm = te.matmul(ps[o, 5, hs], T[4][:, h, o], S[:, c, hs], start=True, stop=True)
                mm.then_inc(pe.sem, pe.step("states"))


GH, GP, NG = 16, 64, 32
S5W = GH * NG
NJ = NG // 2
JQ = NJ // 4


def s5(nc, proj, out, g):
    TWO_PI_HI, TWO_PI_LO = 6.28125, 2 * math.pi - 6.28125
    with Phase(nc, "s5") as ph:
        ident = ph.sb("ident", [P, P])
        prm = ph.sb("prm", [P, 24, NJ])
        ki = ph.sb("ki", [P, 2, NJ], I32)
        bc = ph.sb("bc", [P, 2, NJ, GH])
        bb = ph.sb("bb", [P, 2, NJ, GH])
        bt = ph.sb("bt", [P, 2, NJ, GH])
        bpad = ph.sb("bpad", [P, 2, NJ, 2 * GH])
        cpad = ph.sb("cpad", [P, 2, JQ, P])
        bT = ph.sb("bT", [P, 2, JQ, P])
        cT = ph.sb("cT", [P, 2, JQ, P])
        dcol = ph.sb("dcol", [P, JQ])
        ut = ph.sb("ut", [P, S5W])
        uT = ph.sb("uT", [P, JQ, SEQ])
        bq = ph.sb("bq", [P, 2, P])
        cq = ph.sb("cq", [P, 2, P])
        uq = ph.sb("uq", [P, SEQ])
        pq = ph.sb("pq", [P, 3, 4])
        tb = [ph.sb(f"tb{i}", [P, 2, SEQ]) for i in range(2)]
        w = ph.sb("w", [P, 2, SEQ])
        wt = ph.sb("wt", [P, 2, SEQ])
        z = [ph.sb(f"z{i}", [P, 2, SEQ]) for i in range(2)]
        s = ph.sb("s", [P, 2, SEQ])
        st = ph.sb("st", [P, 2, SEQ])
        yT = ph.sb("yT", [P, JQ, SEQ])
        gluw = ph.sb("gluw", [P, JQ, 2 * S5W])
        glub = ph.sb("glub", [P, 2 * S5W])
        nw = ph.sb("nw", [P, S5W])
        ycur = ph.sb("ycur", [P, JQ, P])
        gate = ph.sb("gate", [P, S5W])
        hg = ph.sb("hg", [P, 2 * S5W])
        yy = ph.sb("yy", [P, S5W])
        ss = ph.sb("ss", [P, 4])
        yo = ph.sb("yo", [P, S5W])
        ps = ph.psum()
        const_in, c_in, pad_set, x_in, g_in, y_st, passed = (ph.sem(n) for n in (
            "const_in", "c_in", "pad_set", "x_in", "g_in", "y_st", "passed"))
        pre_a = ph.marks("pre_act", "step mag sin bTcT")
        pre_d = ph.marks("pre_dve", "lr angles bpad")
        pre_p = ph.marks("pre_pe", "turned")
        ud = ph.steps("u_dve", "uT")
        up = ph.steps("u_pe", "turned")
        act = ph.steps("act", "cur gelu")
        dve = ph.steps("dve", " ".join(f"w{i} z{i}" for i in range(4)) + " sums cubic yT")
        pool_s = ph.steps("pool", " ".join(f"s{i}" for i in range(4)))
        pe = ph.steps("pe", "bu0 bu1 y0 bu2 y1 bu3 y2 y3")
        act2 = ph.steps("act2", "ycur gates root")
        dve2 = ph.steps("dve2", "hg mean out")
        pe2 = ph.steps("pe2", "sums")
        blk = ph.block()
        C = lambda i: prm[:, i, :]

        @blk.sync
        def _(sp):
            ls = g["s5_log_step_2"].rearrange("(j g) -> g j", g=2)
            jobs = [(ident[:, :], g["ident"]),
                    (dcol[:, :], g["s5_d_2"].rearrange("(k p) -> p k", p=P)),
                    (gluw[:, :, :], g["s5_glu_w_2"].rearrange("(k p) n -> p k n", p=P)),
                    (glub[:, :], g["s5_glu_b_2"].partition_broadcast(P)),
                    (nw[:, :], g["s5_norm_w_2"].partition_broadcast(P))]
            for k in range(2):
                half = slice(64 * k, 64 * k + 64)
                jobs += [(prm[half, 2, :], ls[k, :].partition_broadcast(64)),
                         (prm[half, 0, :], g["s5_lambda_re_2"].rearrange("(j g) p -> g p j", g=2)[k]),
                         (prm[half, 1, :], g["s5_lambda_im_2"].rearrange("(j g) p -> g p j", g=2)[k]),
                         (bc[half, 0, :, :], g["s5_b_re_2"].rearrange("(j g) p h -> g p j h", g=2)[k]),
                         (bc[half, 1, :, :], g["s5_b_im_2"].rearrange("(j g) p h -> g p j h", g=2)[k])]
            assert len(jobs) == 15
            for dst, src in jobs:
                sp.dma_start(dst, src, allow_slow_non_contiguous=True).then_inc(const_in, 16)
            sp.wait_ge(pad_set, 1)
            for i, name in enumerate(("s5_c_re_2", "s5_c_im_2")):
                c_v = g[name].rearrange("(J j g) h p -> j g h J p", j=4, g=2)
                for jj in range(4):
                    for k in range(2):
                        r0 = 32 * jj + 16 * k
                        sp.dma_start(cpad[r0:r0 + 16, i, :, 64 * k:64 * k + 64], c_v[jj, k]).then_inc(c_in, 16)
            with sp.Fori(0, NT) as t:
                sp.wait_ge(ud.sem, ud.start(t))
                sp.dma_start(ut[:, :], proj[bass.ds(t * P, P), COL_U:COL_U + S5W]).then_inc(x_in, 16)
            sp.sem_inc(y_st, 16)
            with sp.Fori(0, NT) as t:
                sp.wait_ge(dve2.sem, dve2.start(t))
                sp.dma_start(gate[:, :], proj[bass.ds(t * P, P), COL_SG:COL_SG + S5W]).then_inc(g_in, 16)
                sp.wait_ge(dve2.sem, dve2.at("out", t))
                sp.sem_inc(passed, 1)
                sp.dma_start(out[bass.ds(t * P, P), :], yo[:, :]).then_inc(y_st, 16)
            sp.wait_ge(y_st, 16 * (NT + 1))

        @blk.gpsimd
        def _(pool):
            pool.memset(cpad[:, :, :, :], 0.0).then_inc(pad_set, 1)
            tt = pool.tensor_tensor
            pool_s.begin(pool)
            with pool.Fori(0, JQ) as J:
                for i in range(4):
                    zz, t2 = z[i % 2], tb[i % 2]
                    pool.wait_ge(dve.sem, dve.at(f"z{i}", J))
                    tt(st[:, 0, :], zz[:, 1, :], t2[:, 1, :], ALU.mult)
                    tt(st[:, 1, :], zz[:, 1, :], t2[:, 0, :], ALU.mult)
                    if i:
                        pool.wait_ge(pe.sem, pe.at(f"y{i - 1}", J))
                    else:
                        pool.wait_ge(pe.sem, pe.start(J))
                    tt(s[:, 0, :], zz[:, 0, :], t2[:, 0, :], ALU.mult)
                    tt(s[:, 1, :], zz[:, 0, :], t2[:, 1, :], ALU.mult)
                    pool.drain()
                    tt(s[:, 0, :], s[:, 0, :], st[:, 0, :], ALU.subtract)
                    tt(s[:, 1, :], s[:, 1, :], st[:, 1, :], ALU.add).then_inc(pool_s.sem, pool_s.step(f"s{i}"))
                    pool.drain()

        @blk.scalar
        def _(a):
            a.wait_ge(const_in, 240)
            a.activation(C(3), C(2), ACT.Exp).then_inc(pre_a.sem, pre_a.step("step"))
            a.wait_ge(pre_d.sem, 1)
            a.activation(C(5), C(4), ACT.Exp).then_inc(pre_a.sem, pre_a.step("mag"))
            a.wait_ge(pre_d.sem, 2)
            a.activation(C(8), C(6), ACT.Sin)
            a.activation(C(9), C(7), ACT.Sin).then_inc(pre_a.sem, pre_a.step("sin"))
            a.wait_ge(pre_p.sem, 1)
            a.activation(bT[:, :, :, :].rearrange("p a j c -> p (a j) c"), blocks(ps, 0, 8), ACT.Copy)
            a.activation(cT[:, 0, :, :], blocks(ps, 2, 4), ACT.Copy)
            a.activation(cT[:, 1, :, :], blocks(ps, 3, 4), ACT.Copy, scale=-1.0).then_inc(pre_a.sem, pre_a.step("bTcT"))
            a.drain()
            a.wait_ge(ud.sem, ud.start(NT))
            act.begin(a)
            with a.Fori(0, JQ) as J:
                one = bass.ds(J, 1)
                a.wait_ge(dve.sem, dve.start(J))
                for k in range(2):
                    a.activation(bq[:, k, :], bT[:, k, one, :].rearrange("p o c -> p (o c)"), ACT.Copy)
                    a.activation(cq[:, k, :], cT[:, k, one, :].rearrange("p o c -> p (o c)"), ACT.Copy)
                a.activation(uq[:, :], uT[:, one, :].rearrange("p o c -> p (o c)"), ACT.Copy)\
                    .then_inc(act.sem, act.step("cur"))
                a.wait_ge(dve.sem, dve.at("cubic", J))
                a.activation(wt[:, 1, :], wt[:, 0, :], ACT.Sigmoid, scale=2 * math.sqrt(2 / math.pi))\
                    .then_inc(act.sem, act.step("gelu"))
            act2.begin(a)
            with a.Fori(0, NT) as t:
                a.wait_ge(pe2.sem, pe2.start(t))
                a.wait_ge(dve.sem, dve.start(JQ))
                a.activation(ycur[:, :, :], yT[:, :, bass.ds(t * P, P)], ACT.Copy).then_inc(act2.sem, act2.step("ycur"))
                a.wait_ge(dve2.sem, dve2.at("hg", t))
                a.wait_ge(g_in, 16 * t + 16)
                a.activation(hg[:, S5W:], hg[:, S5W:], ACT.Sigmoid)
                a.activation(gate[:, :], gate[:, :], ACT.Silu).then_inc(act2.sem, act2.step("gates"))
                a.wait_ge(dve2.sem, dve2.at("mean", t))
                a.activation(ss[:, 2:3], ss[:, 1:2], ACT.Sqrt).then_inc(act2.sem, act2.step("root"))

        @blk.vector
        def _(ve):
            tt, ts, stt = ve.tensor_tensor, ve.tensor_scalar, ve.scalar_tensor_tensor
            ve.memset(bpad[:, :, :, :], 0.0)
            ve.drain()
            ve.wait_ge(pre_a.sem, 1)
            ts(C(10), C(0), -1e-4, None, ALU.min)
            ve.drain()
            tt(C(4), C(10), C(3), ALU.mult).then_inc(pre_d.sem, pre_d.step("lr"))
            tt(C(11), C(1), C(3), ALU.mult)
            ve.drain()
            ts(C(12), C(11), math.pi / 2, None, ALU.add)
            for k, src, dst in ((0, 11, 6), (1, 12, 7)):
                ve.drain()
                ts(C(13), C(src), 1 / (2 * math.pi), None, ALU.mult)
                ve.drain()
                ve.tensor_copy(ki[:, k, :], C(13))
                ve.drain()
                ve.tensor_copy(C(14), ki[:, k, :])
                ve.drain()
                stt(C(13), C(14), -TWO_PI_HI, C(src), ALU.mult, ALU.add)
                ve.drain()
                stt(C(15), C(14), -TWO_PI_LO, C(13), ALU.mult, ALU.add)
                for sign, cmp in ((-1, ALU.is_gt), (1, ALU.is_lt)):
                    ve.drain()
                    ts(C(16), C(15), -sign * math.pi, sign * 2 * math.pi, cmp, ALU.mult)
                    ve.drain()
                    tt(C(15), C(15), C(16), ALU.add)
                ve.drain()
                last = ts(C(dst), C(15), math.pi, -math.pi, ALU.min, ALU.max)
            last.then_inc(pre_d.sem, pre_d.step("angles"))
            ve.drain()
            ve.wait_ge(pre_a.sem, 3)
            sn, cs, mag, lr, li = C(8), C(9), C(5), C(10), C(1)
            tt(C(13), mag, cs, ALU.mult)
            tt(C(14), mag, sn, ALU.mult)
            tt(C(15), lr, lr, ALU.mult)
            tt(C(16), li, li, ALU.mult)
            ve.drain()
            ts(C(13), C(13), -1.0, None, ALU.add)
            tt(C(15), C(15), C(16), ALU.add)
            ve.drain()
            ve.reciprocal(C(16), C(15))
            tt(C(17), C(13), lr, ALU.mult)
            tt(C(18), C(14), li, ALU.mult)
            tt(C(19), C(14), lr, ALU.mult)
            tt(C(20), C(13), li, ALU.mult)
            ve.drain()
            tt(C(17), C(17), C(18), ALU.add)
            tt(C(19), C(19), C(20), ALU.subtract)
            ve.drain()
            tt(C(17), C(17), C(16), ALU.mult)
            tt(C(19), C(19), C(16), ALU.mult)
            ve.drain()
            for k, (i, j, op) in enumerate(((0, 1, ALU.subtract), (1, 0, ALU.add))):
                tt(bb[:, k, :, :], bc[:, i, :, :], bcast(C(17), GH), ALU.mult)
                tt(bt[:, k, :, :], bc[:, j, :, :], bcast(C(19), GH), ALU.mult)
                ve.drain()
                for q in range(2):
                    half = slice(64 * q, 64 * q + 64)
                    last = tt(bpad[half, k, :, q * GH:(q + 1) * GH], bb[half, k, :, :], bt[half, k, :, :], op)
            last.then_inc(pre_d.sem, pre_d.step("bpad"))
            ve.drain()
            ve.wait_ge(pre_a.sem, 4)
            ud.begin(ve)
            with ve.Fori(0, NT) as t:
                ve.wait_ge(up.sem, up.start(t + 1))
                ve.tensor_copy(uT[:, :, bass.ds(t * P, P)], blocks(ps, 4, 4)).then_inc(ud.sem, ud.step("uT"))
            dve.begin(ve)
            with ve.Fori(0, JQ) as J:
                for k, src in enumerate((9, 8, 5)):
                    ve.tensor_copy(pq[:, k, :], prm[:, src, bass.ds(J * 4, 4)])
                for i in range(4):
                    c, sn_ = tb[i % 2][:, 0, :], tb[i % 2][:, 1, :]
                    ve.drain()
                    if i >= 2:
                        ve.drain()
                        ve.wait_ge(pool_s.sem, pool_s.at(f"s{i - 2}", J))
                    else:
                        ve.drain()
                        ve.wait_ge(pool_s.sem, pool_s.start(J))
                    ve.tensor_copy(c[:, 0:1], pq[:, 0, i:i + 1])
                    ve.tensor_copy(sn_[:, 0:1], pq[:, 1, i:i + 1])
                    n = 1
                    while n < SEQ:
                        ve.drain()
                        cn, sc = c[:, n - 1:n], sn_[:, n - 1:n]
                        ts(wt[:, 0, 0:n], sn_[:, 0:n], sc, None, ALU.mult)
                        ts(wt[:, 1, 0:n], c[:, 0:n], sc, None, ALU.mult)
                        ve.drain()
                        stt(c[:, n:2 * n], c[:, 0:n], cn, wt[:, 0, 0:n], ALU.mult, ALU.subtract)
                        stt(sn_[:, n:2 * n], sn_[:, 0:n], cn, wt[:, 1, 0:n], ALU.mult, ALU.add)
                        n *= 2
                    ve.drain()
                    ve.wait_ge(pe.sem, pe.at(f"bu{i}", J))
                    tt(w[:, 0, :], banks(ps, 0), c, ALU.mult)
                    tt(wt[:, 0, :], banks(ps, 2), sn_, ALU.mult)
                    tt(w[:, 1, :], banks(ps, 2), c, ALU.mult)
                    tt(wt[:, 1, :], banks(ps, 0), sn_, ALU.mult).then_inc(dve.sem, dve.step(f"w{i}"))
                    ve.drain()
                    tt(w[:, 0, :], w[:, 0, :], wt[:, 0, :], ALU.add)
                    tt(w[:, 1, :], w[:, 1, :], wt[:, 1, :], ALU.subtract)
                    ve.drain()
                    for k in range(2):
                        last = ve.tensor_tensor_scan(z[i % 2][:, k, :], pq[:, 2, i:i + 1].to_broadcast([P, SEQ]),
                                                     w[:, k, :], 0.0, ALU.mult, ALU.add)
                    last.then_inc(dve.sem, dve.step(f"z{i}"))
                ve.drain()
                ve.wait_ge(pe.sem, pe.at("y3", J))
                stt(w[:, 0, :], uq[:, :], dcol[:, bass.ds(J, 1)], banks(ps, 4), ALU.mult, ALU.add)\
                    .then_inc(dve.sem, dve.step("sums"))
                ve.drain()
                tt(w[:, 1, :], w[:, 0, :], w[:, 0, :], ALU.mult)
                ve.drain()
                ts(w[:, 1, :], w[:, 1, :], 0.044715, 1.0, ALU.mult, ALU.add)
                ve.drain()
                tt(wt[:, 0, :], w[:, 1, :], w[:, 0, :], ALU.mult).then_inc(dve.sem, dve.step("cubic"))
                ve.drain()
                ve.wait_ge(act.sem, act.at("gelu", J))
                tt(yT[:, bass.ds(J, 1), :].rearrange("p o c -> p (o c)"), wt[:, 1, :], w[:, 0, :], ALU.mult)\
                    .then_inc(dve.sem, dve.step("yT"))
                ve.drain()
            dve2.begin(ve)
            with ve.Fori(0, NT) as t:
                ve.wait_ge(pe2.sem, pe2.start(t + 1))
                tt(hg[:, :], banks(ps, 6), glub[:, :], ALU.add).then_inc(dve2.sem, dve2.step("hg"))
                ve.drain()
                ve.wait_ge(act2.sem, act2.at("gates", t))
                tt(yy[:, :], hg[:, 0:S5W], hg[:, S5W:], ALU.mult)
                ve.drain()
                tt(yy[:, :], yy[:, :], gate[:, :], ALU.mult)
                ve.drain()
                tt(hg[:, 0:S5W], yy[:, :], yy[:, :], ALU.mult)
                ve.drain()
                ve.tensor_reduce(ss[:, 0:1], hg[:, 0:S5W], AX, ALU.add)
                ve.drain()
                ts(ss[:, 1:2], ss[:, 0:1], 1.0 / S5W, EPS, ALU.mult, ALU.add).then_inc(dve2.sem, dve2.step("mean"))
                ve.drain()
                ve.wait_ge(act2.sem, act2.at("root", t))
                ve.reciprocal(ss[:, 3:4], ss[:, 2:3])
                ve.drain()
                ve.wait_ge(y_st, 16 * t + 16)
                stt(yo[:, :], yy[:, :], ss[:, 3:4], nw[:, :], ALU.mult, ALU.mult).then_inc(dve2.sem, dve2.step("out"))
                ve.drain()

        @blk.tensor
        def _(te):
            te.wait_ge(const_in, 240)
            te.wait_ge(pre_d.sem, 3)
            te.wait_ge(c_in, 256)
            for k in range(2):
                for j in range(JQ):
                    te.transpose(block_of(ps, k, j),
                                 bpad[:, k, 4 * j:4 * j + 4, :].rearrange("p j c -> p (j c)"), ident[:, :])
                    mm = te.transpose(block_of(ps, 2 + k, j), cpad[:, k, j, :], ident[:, :])
            mm.then_inc(pre_p.sem, pre_p.step("turned"))
            up.begin(te)
            with te.Fori(0, NT) as t:
                te.wait_ge(ud.sem, ud.start(t))
                te.wait_ge(x_in, 16 * t + 16)
                for j in range(JQ):
                    mm = te.transpose(block_of(ps, 4, j), ut[:, j * P:(j + 1) * P], ident[:, :])
                mm.then_inc(up.sem, up.step("turned"))
            te.wait_ge(pre_a.sem, 4)
            pe.begin(te)
            with te.Fori(0, JQ) as J:
                def bu(i):
                    rows = slice(32 * i, 32 * i + 32)
                    for k in range(2):
                        for n in range(2):
                            mm = te.matmul(ps[:, 2 * k + n, :], bq[rows, k, :], uq[rows, n * 512:(n + 1) * 512],
                                           start=True, stop=True)
                    mm.then_inc(pe.sem, pe.step(f"bu{i}"))

                te.wait_ge(act.sem, act.at("cur", J))
                bu(0)
                for i in range(4):
                    if i < 3:
                        te.wait_ge(dve.sem, dve.at(f"w{i}", J))
                        bu(i + 1)
                    te.wait_ge(pool_s.sem, pool_s.at(f"s{i}", J))
                    rows = slice(32 * i, 32 * i + 32)
                    for n in range(2):
                        for k in range(2):
                            mm = te.matmul(ps[rows, 4 + n, :], cq[:, k, rows], s[:, k, n * 512:(n + 1) * 512],
                                           start=(k == 0), stop=(k == 1))
                    mm.then_inc(pe.sem, pe.step(f"y{i}"))
            pe2.begin(te)
            with te.Fori(0, NT) as t:
                te.wait_ge(dve2.sem, dve2.start(t))
                te.wait_ge(act2.sem, act2.at("ycur", t))
                for n in range(2):
                    for k in range(JQ):
                        mm = te.matmul(ps[:, 6 + n, :], ycur[:, k, :], gluw[:, k, n * 512:(n + 1) * 512],
                                       start=(k == 0), stop=(k == JQ - 1))
                mm.then_inc(pe2.sem, pe2.step("sums"))


NGRP, EPG = 4, 8
NE = NGRP * EPG
FF = 512
KF = FF // P
N_BLOCKS = (2 * SEQ + NE * P) // P
BIG = 1e30


def route_consts():
    t, l = np.arange(P)[:, None], np.arange(P)[None, :]
    io = np.broadcast_to(np.arange(EPG, dtype=np.float32), (P, EPG))
    return np.concatenate([(t == l).astype(np.float32), (t < l).astype(np.float32), np.ones((P, P), np.float32), io,
                           (t * P).astype(np.float32)], axis=1)


def token_ids():
    return (np.arange(NT)[None, :] * P + np.arange(P)[:, None]).astype(np.int32)


def route(nc, x, hbuf, buf_tok, ybuf, dests, weights, blk_e, n_pairs, consts_d, ids_d, g):
    with Phase(nc, "route") as ph:
        cst = ph.sb("cst", [P, 3 * P + EPG + 1])
        ident, strict, ones = (cst[:, i * P:(i + 1) * P] for i in range(3))
        iota, bcol = cst[:, 3 * P:3 * P + EPG], cst[:, 3 * P + EPG:]
        ids = ph.sb("ids", [P, NT], I32)
        gain = ph.sb("gain", [P, D])
        wr = ph.sb("wr", [P, KD, NGRP + NE])
        bias = ph.sb("bias", [P, NGRP + NE])
        xt = ph.sb("xt", [P, D])
        junk = ph.sb("junk", [P, D])
        ss = ph.sb("ss", [P, 4])
        h0 = ph.sb("h0", [P, D])
        h = ph.sb("h", [P, D])
        hT = ph.sb("hT", [P, KD, P])
        L = ph.sb("L", [P, NT, NGRP + NE])
        sc = ph.sb("sc", [P, 16, NT])
        og = ph.sb("og", [P, NT, NGRP])
        o8 = ph.sb("o8", [P, 2, NT, EPG])
        t8 = ph.sb("t8", [P, NT, EPG])
        t4 = ph.sb("t4", [P, NT, NGRP])
        es = ph.sb("es", [P, NT, EPG])
        e2 = ph.sb("e2", [P, NT, EPG])
        O = ph.sb("O", [P, 2, NT, NE])
        A = ph.sb("A", [P, NT, NE])
        pre = ph.sb("pre", [P, NT + 1, NE])
        Dst = ph.sb("Dst", [P, NT, NE])
        cnt = ph.sb("cnt", [P, 6, NE])
        cnti = ph.sb("cnti", [P, 2, NE], I32)
        di = ph.sb("di", [P, 2, NT], I32)
        wts = ph.sb("wts", [P, 2, NT])
        be = ph.sb("be", [P, 2])
        bei = ph.sb("bei", [P, 1], I32)
        npi = ph.sb("npi", [P, 2], I32)
        zero = ph.sb("zero", [P, N_BLOCKS + 2], I32)
        zrow = ph.sb("zrow", [P, D])
        ps = ph.psum()
        const_in, x_in, h_st, fill_st, tok_st, meta_st, passed = (ph.sem(n) for n in (
            "const_in", "x_in", "h_st", "fill_st", "tok_st", "meta_st", "passed"))
        act = ph.steps("act", "square root")
        dve = ph.steps("dve", "mean normed hT logits")
        pe = ph.steps("pe", "turned logits")
        d2 = ph.marks("dve2", "shifted diff counted rows")
        a2 = ph.marks("act2", "gexp eexp")
        p2 = ph.marks("pe2", "counts")
        blk = ph.block()

        @blk.sync
        def _(sp):
            for dst, src in ((cst[:, :], consts_d), (ids[:, :], ids_d), (gain[:, :], g["norm_ffn"].partition_broadcast(P)),
                             (wr[:, :, 0:NGRP], g["w_group"].rearrange("(k p) n -> p k n", p=P)),
                             (wr[:, :, NGRP:], g["w_expert_router"].rearrange("(k p) n -> p k n", p=P)),
                             (bias[:, 0:NGRP], g["b_group"].partition_broadcast(P)),
                             (bias[:, NGRP:], g["b_expert_router"].partition_broadcast(P))):
                sp.dma_start(dst, src, allow_slow_non_contiguous=True).then_inc(const_in, 16)
            sp.sem_inc(h_st, 16)
            with sp.Fori(0, NT) as t:
                sp.wait_ge(dve.sem, dve.start(t))
                sp.dma_start(xt[:, :], x[bass.ds(t * P, P), :]).then_inc(x_in, 16)
                sp.wait_ge(dve.sem, dve.at("normed", t))
                sp.sem_inc(passed, 1)
                sp.dma_start(hbuf[bass.ds(t * P, P), :], h[:, :]).then_inc(h_st, 16)
            sp.wait_ge(h_st, 16 * (NT + 1))
            sp.wait_ge(d2.sem, 4)
            sp.dma_start(dests, di[:, :, :]).then_inc(meta_st, 16)
            sp.dma_start(weights, wts[:, :, :]).then_inc(meta_st, 16)
            sp.dma_start(blk_e, bei[0:N_BLOCKS, :]).then_inc(meta_st, 16)
            sp.dma_start(n_pairs, npi[0:1, 1:2]).then_inc(meta_st, 16)
            sp.wait_ge(meta_st, 64)

        @blk.gpsimd
        def _(pool):
            pool.memset(zero[:, :], 0)
            pool.memset(zrow[:, :], 0.0)
            pool.drain()
            pool.dma_start(buf_tok.rearrange("(p b) o -> p (b o)", p=P), zero[:, :]).then_inc(fill_st, 16)
            full = 2 * SEQ // P
            pool.dma_start(ybuf[full * P:, :].rearrange("(b p) d -> p b d", p=P), over(zrow[:, :], N_BLOCKS - full))\
                .then_inc(fill_st, 16)
            pool.wait_ge(fill_st, 32)
            pool.wait_ge(d2.sem, 4)
            for k in range(2):
                for t in range(NT):
                    pool.indirect_dma_start(out=buf_tok, out_offset=bass.IndirectOffsetOnAxis(
                        ap=di[:, k, t:t + 1].bitcast(U32), axis=0), in_=ids[:, t:t + 1], in_offset=None).then_inc(tok_st, 16)
            pool.wait_ge(tok_st, 16 * 2 * NT)

        @blk.scalar
        def _(s):
            act.begin(s)
            with s.Fori(0, NT) as t:
                s.wait_ge(x_in, 16 * t + 16)
                s.activation(junk[:, :], xt[:, :], ACT.Square, accum_out=ss[:, 0:1]).then_inc(act.sem, act.step("square"))
                s.wait_ge(dve.sem, dve.at("mean", t))
                s.activation(ss[:, 2:3], ss[:, 1:2], ACT.Sqrt).then_inc(act.sem, act.step("root"))
            s.wait_ge(d2.sem, 1)
            s.activation(t4[:, :, :], t4[:, :, :], ACT.Exp).then_inc(a2.sem, a2.step("gexp"))
            s.wait_ge(d2.sem, 2)
            s.activation(sc[:, 9, :], sc[:, 8, :], ACT.Exp).then_inc(a2.sem, a2.step("eexp"))

        @blk.vector
        def _(ve):
            tt, ts, stt = ve.tensor_tensor, ve.tensor_scalar, ve.scalar_tensor_tensor
            ve.drain()
            ve.wait_ge(const_in, 112)
            dve.begin(ve)
            with ve.Fori(0, NT) as t:
                ve.wait_ge(act.sem, act.at("square", t))
                ts(ss[:, 1:2], ss[:, 0:1], 1.0 / D, EPS, ALU.mult, ALU.add).then_inc(dve.sem, dve.step("mean"))
                ve.drain()
                ve.wait_ge(act.sem, act.at("root", t))
                ve.reciprocal(ss[:, 3:4], ss[:, 2:3])
                ve.drain()
                ve.wait_ge(h_st, 16 * t + 16)
                stt(h[:, :], xt[:, :], ss[:, 3:4], gain[:, :], ALU.mult, ALU.mult).then_inc(dve.sem, dve.step("normed"))
                ve.drain()
                ve.wait_ge(pe.sem, pe.at("turned", t))
                ve.tensor_copy(hT[:, :, :], blocks(ps, 0, 8)).then_inc(dve.sem, dve.step("hT"))
                ve.drain()
                ve.wait_ge(pe.sem, pe.at("logits", t))
                tt(L[:, bass.ds(t, 1), :].rearrange("p o c -> p (o c)"), ps[:, 2, 0:NGRP + NE], bias[:, :], ALU.add)\
                    .then_inc(dve.sem, dve.step("logits"))
                ve.drain()

            def first_max(onehot, values, top, n, tmp):
                ve.tensor_reduce(top, values, AX, ALU.max)
                ve.drain()
                tt(tmp, values, bcast(top, n), ALU.is_lt)
                ve.drain()
                stt(tmp, tmp, BIG, iota[:, 0:n].unsqueeze(1).to_broadcast([P, NT, n]), ALU.mult, ALU.add)
                ve.drain()
                ve.tensor_reduce(sc[:, 15, :], tmp, AX, ALU.min)
                ve.drain()
                tt(onehot, tmp, bcast(sc[:, 15, :], n), ALU.is_equal)

            G = L[:, :, 0:NGRP]
            E = L[:, :, NGRP:].rearrange("p t (g e) -> p t g e", g=NGRP)
            first_max(og[:, :, :], G, sc[:, 0, :], NGRP, t4[:, :, :])
            ve.drain()
            tt(t4[:, :, :], G, bcast(sc[:, 0, :], NGRP), ALU.subtract).then_inc(d2.sem, d2.step("shifted"))
            prod = A[:, :, :].rearrange("p t (g e) -> p t g e", g=NGRP)
            tt(prod, E, og[:, :, :].unsqueeze(3).to_broadcast([P, NT, NGRP, EPG]), ALU.mult)
            ve.drain()
            ve.tensor_reduce(es[:, :, :], prod.rearrange("p t g e -> p t e g"), AX, ALU.add)
            ve.drain()
            first_max(o8[:, 0, :, :], es[:, :, :], sc[:, 1, :], EPG, t8[:, :, :])
            ve.drain()
            stt(e2[:, :, :], o8[:, 0, :, :], -BIG, es[:, :, :], ALU.mult, ALU.add)
            ve.drain()
            first_max(o8[:, 1, :, :], e2[:, :, :], sc[:, 2, :], EPG, t8[:, :, :])
            ve.drain()
            tt(sc[:, 8, :], sc[:, 2, :], sc[:, 1, :], ALU.subtract).then_inc(d2.sem, d2.step("diff"))
            for k in range(2):
                tt(O[:, k, :, :].rearrange("p t (g e) -> p t g e", g=NGRP),
                   og[:, :, :].unsqueeze(3).to_broadcast([P, NT, NGRP, EPG]),
                   o8[:, k, :, :].unsqueeze(2).to_broadcast([P, NT, NGRP, EPG]), ALU.mult)
            ve.drain()
            tt(A[:, :, :], O[:, 0, :, :], O[:, 1, :, :], ALU.add)
            ve.memset(pre[:, 0, :], 0.0)
            for t in range(NT):
                ve.drain()
                last = tt(pre[:, t + 1, :], pre[:, t, :], A[:, t, :], ALU.add)
            last.then_inc(d2.sem, d2.step("counted"))
            ve.drain()
            ve.wait_ge(a2.sem, 2)
            ve.tensor_reduce(sc[:, 3, :], t4[:, :, :], AX, ALU.add)
            ts(sc[:, 4, :], sc[:, 9, :], 1.0, None, ALU.add)
            ve.drain()
            tt(sc[:, 5, :], sc[:, 3, :], sc[:, 4, :], ALU.mult)
            ve.drain()
            ve.reciprocal(wts[:, 0, :], sc[:, 5, :])
            ve.drain()
            tt(wts[:, 1, :], wts[:, 0, :], sc[:, 9, :], ALU.mult)
            ve.drain()
            ve.wait_ge(p2.sem, 1)
            c = lambda i: cnt[:, i, :]
            ts(c(0), ps[:, 1, 0:NE], float(P - 1), None, ALU.add)
            ve.memset(c(3), 1.0)
            ve.drain()
            ve.tensor_copy(cnti[:, 0, :], c(0))
            ve.drain()
            ts(cnti[:, 1, :], cnti[:, 0, :], 7, 7, ALU.logical_shift_right, ALU.logical_shift_left)
            ve.drain()
            ve.tensor_copy(c(1), cnti[:, 1, :])
            ve.drain()
            ve.tensor_tensor_scan(c(2), c(3), c(1), 0.0, ALU.mult, ALU.add)
            ve.drain()
            tt(c(4), c(2), c(1), ALU.subtract)
            ts(c(5), c(2), bcol, None, ALU.is_le)
            ve.drain()
            ve.tensor_reduce(be[:, 0:1], c(5), AX, ALU.add)
            tt(Dst[:, :, :], ps[:, 0, 0:NT * NE].rearrange("p (t e) -> p t e", e=NE), over(c(4), NT), ALU.add)
            ve.drain()
            ts(be[:, 1:2], be[:, 0:1], float(NE - 1), None, ALU.min)
            ve.drain()
            ve.tensor_copy(bei[:, :], be[:, 1:2])
            ts(npi[:, 0:1], cnt[:, 2, NE - 1:NE], float(P), None, ALU.add)
            ve.drain()
            ts(npi[:, 1:2], npi[:, 0:1], 8, None, ALU.logical_shift_right)
            for k in range(2):
                tt(A[:, :, :], O[:, k, :, :], Dst[:, :, :], ALU.mult)
                ve.drain()
                ve.tensor_reduce(sc[:, 10 + k, :], A[:, :, :], AX, ALU.add)
                ve.drain()
            ve.tensor_copy(di[:, :, :], sc[:, 10:12, :]).then_inc(d2.sem, d2.step("rows"))

        @blk.tensor
        def _(te):
            te.wait_ge(const_in, 112)
            pe.begin(te)
            with te.Fori(0, NT) as t:
                te.wait_ge(dve.sem, dve.at("normed", t))
                for j in range(8):
                    mm = te.transpose(block_of(ps, 0, j), h[:, j * P:(j + 1) * P], ident)
                mm.then_inc(pe.sem, pe.step("turned"))
                te.wait_ge(dve.sem, dve.at("hT", t))
                for k in range(KD):
                    mm = te.matmul(ps[:, 2, 0:NGRP + NE], hT[:, k, :], wr[:, k, :], start=(k == 0), stop=(k == KD - 1))
                mm.then_inc(pe.sem, pe.step("logits"))
            te.wait_ge(d2.sem, 3)
            te.matmul(ps[:, 0, 0:NT * NE], strict, A[:, :, :].rearrange("p t e -> p (t e)"), start=True, stop=False)
            te.matmul(ps[:, 0, 0:NT * NE], ones, pre[:, 0:NT, :].rearrange("p t e -> p (t e)"), start=False, stop=True)
            te.matmul(ps[:, 1, 0:NE], ones, pre[:, NT, :], start=True, stop=True).then_inc(p2.sem, p2.step("counts"))


def experts(nc, hbuf, buf_tok, blk_e, n_pairs, ybuf, ident_d, g):
    NB = N_BLOCKS
    with Phase(nc, "moe") as ph:
        ident = ph.sb("ident", [P, P])
        idx_all = ph.sb("idx_all", [P, NB + 2], I32)
        be = ph.sb("be", [1, NB + 1], I32)
        idx = [ph.sb(f"idx{b}", [P, 1], I32) for b in range(2)]
        xb = [ph.sb(f"xb{b}", [P, D]) for b in range(2)]
        wg = [ph.sb(f"wg{b}", [P, KD, FF]) for b in range(2)]
        wu = [ph.sb(f"wu{b}", [P, KD, FF]) for b in range(2)]
        wd = [ph.sb(f"wd{b}", [P, KF, D]) for b in range(2)]
        xT = [ph.sb(f"xT{b}", [P, KD, P]) for b in range(2)]
        sg = ph.sb("sg", [P, FF])
        a = ph.sb("a", [P, FF])
        aT = ph.sb("aT", [P, KF, P])
        yb = [ph.sb(f"yb{b}", [P, D]) for b in range(2)]
        ps = ph.psum()
        const_in = ph.sem("const_in")
        w_in = [ph.sem(f"w_in{b}") for b in range(2)]
        x_in = [ph.sem(f"x_in{b}") for b in range(2)]
        y_st = [ph.sem(f"y_st{b}") for b in range(2)]
        passed = ph.sem("passed")
        xt_ps = ph.sem("xt_ps")
        xt_sb = ph.sem("xt_sb")
        gu = ph.sem("gu")
        silu = ph.sem("silu")
        a_ok = ph.sem("a_ok")
        at_ps = ph.sem("at_ps")
        at_sb = ph.sem("at_sb")
        down = ph.sem("down")
        y_act = ph.sem("y_act")
        y_dve = ph.sem("y_dve")
        idx_ok = ph.sem("idx_ok")
        blk = ph.block()

        def turns_of(eng):
            eng.wait_ge(const_in, 64)
            return eng.value_load(be[0:1, NB:NB + 1], min_val=8, max_val=NB // 2)

        @blk.sync
        def _(sp):
            sp.dma_start(ident[:, :], ident_d).then_inc(const_in, 16)
            sp.dma_start(idx_all[:, :], buf_tok.rearrange("(b p) o -> p (b o)", p=P), allow_slow_non_contiguous=True)\
                .then_inc(const_in, 16)
            sp.dma_start(be[0:1, 0:NB], blk_e.rearrange("b o -> o b"), allow_slow_non_contiguous=True).then_inc(const_in, 16)
            sp.dma_start(be[0:1, NB:NB + 1], n_pairs).then_inc(const_in, 16)
            turns = turns_of(sp)
            with sp.Fori(0, turns) as j:
                for b in range(2):
                    e = sp.value_load(be[0:1, bass.ds(2 * j + b, 1)], min_val=0, max_val=NE - 1)
                    sp.wait_ge(down, 2 * j + b + 1)
                    sp.dma_start(wg[b][:, :, :], g["w_gate"][bass.ds(e, 1), :, :].rearrange("o (k p) f -> p (o k) f", p=P))\
                        .then_inc(w_in[b], 16)
                    sp.dma_start(wu[b][:, :, :], g["w_up"][bass.ds(e, 1), :, :].rearrange("o (k p) f -> p (o k) f", p=P))\
                        .then_inc(w_in[b], 16)
                    sp.dma_start(wd[b][:, :, :], g["w_down"][bass.ds(e, 1), :, :].rearrange("o (k p) f -> p (o k) f", p=P))\
                        .then_inc(w_in[b], 16)

        @blk.gpsimd
        def _(pool):
            def gather(n, b):
                pool.tensor_copy(idx[b][:, :], idx_all[:, bass.ds(n, 1)] if not isinstance(n, int) else idx_all[:, n:n + 1])
                pool.drain()
                pool.indirect_dma_start(out=xb[b][:, :], out_offset=None, in_=hbuf, in_offset=bass.IndirectOffsetOnAxis(
                    ap=idx[b][:, :].bitcast(U32), axis=0)).then_inc(x_in[b], 16)

            turns = turns_of(pool)
            gather(0, 0)
            gather(1, 1)
            with pool.Fori(0, turns) as j:
                for b in range(2):
                    pool.wait_ge(xt_ps, 2 * j + b + 1)
                    pool.sem_inc(passed, 1)
                    pool.wait_ge(x_in[b], 16 * j + 16)
                    gather(2 * j + b + 2, b)
            for b in range(2):
                pool.wait_ge(x_in[b], 16 * (turns + 1))

        @blk.scalar
        def _(s):
            turns = turns_of(s)
            s.wait_ge(xt_ps, 1)
            s.activation(xT[0][:, :, :], blocks(ps, 0, 8), ACT.Copy).then_inc(xt_sb, 1)
            s.sem_inc(y_act, 1)
            for b in range(2):
                s.sem_inc(y_st[b], 16)
            with s.Fori(0, turns) as j:
                for b in range(2):
                    n = 2 * j + b
                    s.wait_ge(gu, n + 1)
                    s.activation(sg[:, :], ps[:, 2, :], ACT.Silu).then_inc(silu, 1)
                    s.wait_ge(xt_ps, n + 2)
                    s.activation(xT[1 - b][:, :, :], blocks(ps, 0, 8), ACT.Copy).then_inc(xt_sb, 1)
                    s.wait_ge(y_st[b], 16 * j + 16)
                    s.wait_ge(down, n + 3)
                    s.activation(yb[b][:, 0:512], ps[:, 5, :], ACT.Copy).then_inc(y_act, 1)
                    s.wait_ge(y_act, n + 2)
                    s.wait_ge(y_dve, n + 2)
                    s.sem_inc(passed, 1)
                    s.dma_start(ybuf[bass.ds(n * P, P), :], yb[b][:, :]).then_inc(y_st[b], 16)
            for b in range(2):
                s.wait_ge(y_st[b], 16 * (turns + 1))
                s.sem_inc(passed, 1)

        @blk.vector
        def _(ve):
            turns = turns_of(ve)
            ve.sem_inc(a_ok, 1)
            ve.sem_inc(y_dve, 1)
            with ve.Fori(0, turns) as j:
                for b in range(2):
                    n = 2 * j + b
                    ve.drain()
                    ve.wait_ge(silu, n + 1)
                    ve.tensor_tensor(a[:, :], sg[:, :], ps[:, 3, :], ALU.mult).then_inc(a_ok, 1)
                    ve.drain()
                    ve.wait_ge(at_ps, n + 1)
                    ve.tensor_copy(aT[:, :, :], blocks(ps, 4, 4)).then_inc(at_sb, 1)
                    ve.drain()
                    ve.wait_ge(y_st[b], 16 * j + 16)
                    ve.wait_ge(down, n + 3)
                    ve.tensor_copy(yb[b][:, 512:], ps[:, 6, :]).then_inc(y_dve, 1)

        @blk.tensor
        def _(te):
            def turn(b):
                for k in range(KD):
                    mm = te.transpose(block_of(ps, 0, k), xb[b][:, k * P:(k + 1) * P], ident[:, :])
                mm.then_inc(xt_ps, 1)

            te.sem_inc(down, 2)
            turns = turns_of(te)
            te.wait_ge(x_in[0], 16)
            turn(0)
            with te.Fori(0, turns) as j:
                for b in range(2):
                    n = 2 * j + b
                    te.wait_ge(xt_sb, n + 1)
                    te.wait_ge(a_ok, n + 1)
                    te.wait_ge(w_in[b], 48 * j + 48)
                    for bank, w in ((2, wg), (3, wu)):
                        for k in range(KD):
                            mm = te.matmul(ps[:, bank, :], xT[b][:, k, :], w[b][:, k, :], start=(k == 0), stop=(k == KD - 1))
                    mm.then_inc(gu, 1)
                    te.wait_ge(x_in[1 - b], 16 * (j + b) + 16)
                    turn(1 - b)
                    te.wait_ge(a_ok, n + 2)
                    for k in range(KF):
                        mm = te.transpose(block_of(ps, 4, k), a[:, k * P:(k + 1) * P], ident[:, :])
                    mm.then_inc(at_ps, 1)
                    te.wait_ge(at_sb, n + 1)
                    te.wait_ge(y_act, n + 1)
                    te.wait_ge(y_dve, n + 1)
                    for m in range(2):
                        for k in range(KF):
                            mm = te.matmul(ps[:, 5 + m, :], aT[:, k, :], wd[b][:, k, m * 512:(m + 1) * 512],
                                           start=(k == 0), stop=(k == KF - 1))
                    mm.then_inc(down, 1)


def combine(nc, x, ybuf, dests, weights, out, g):
    with Phase(nc, "comb") as ph:
        di = ph.sb("di", [P, 2, NT], I32)
        wts = ph.sb("wts", [P, 2, NT])
        idx = ph.sb("idx", [P, 2], I32)
        xt = ph.sb("xt", [P, D])
        y = [ph.sb(f"y{k}", [P, D]) for k in range(2)]
        acc = ph.sb("acc", [P, D])
        o = ph.sb("o", [P, D])
        const_in, x_in, y_in, o_st, passed = (ph.sem(n) for n in ("const_in", "x_in", "y_in", "o_st", "passed"))
        dve = ph.steps("dve", "sum")
        blk = ph.block()

        @blk.sync
        def _(sp):
            sp.dma_start(di[:, :, :], dests).then_inc(const_in, 16)
            sp.dma_start(wts[:, :, :], weights).then_inc(const_in, 16)
            sp.sem_inc(o_st, 16)
            with sp.Fori(0, NT) as t:
                sp.wait_ge(dve.sem, dve.start(t))
                sp.dma_start(xt[:, :], x[bass.ds(t * P, P), :]).then_inc(x_in, 16)
                sp.wait_ge(dve.sem, dve.at("sum", t))
                sp.sem_inc(passed, 1)
                sp.dma_start(out[bass.ds(t * P, P), :], o[:, :]).then_inc(o_st, 16)
            sp.wait_ge(o_st, 16 * (NT + 1))

        @blk.gpsimd
        def _(pool):
            pool.wait_ge(const_in, 32)
            with pool.Fori(0, NT) as t:
                pool.wait_ge(dve.sem, dve.start(t))
                pool.tensor_copy(idx[:, :], di[:, :, bass.ds(t, 1)].rearrange("p k o -> p (k o)"))
                pool.drain()
                for k in range(2):
                    pool.indirect_dma_start(out=y[k][:, :], out_offset=None, in_=ybuf, in_offset=bass.IndirectOffsetOnAxis(
                        ap=idx[:, k:k + 1].bitcast(U32), axis=0)).then_inc(y_in, 16)
                pool.wait_ge(y_in, 32 * t + 32)

        @blk.vector
        def _(ve):
            ve.wait_ge(const_in, 32)
            dve.begin(ve)
            with ve.Fori(0, NT) as t:
                one = bass.ds(t, 1)
                ve.drain()
                ve.wait_ge(x_in, 16 * t + 16)
                ve.wait_ge(y_in, 32 * t + 32)
                ve.scalar_tensor_tensor(acc[:, :], y[0][:, :], wts[:, 0, one], xt[:, :], ALU.mult, ALU.add)
                ve.drain()
                ve.wait_ge(o_st, 16 * t + 16)
                ve.scalar_tensor_tensor(o[:, :], y[1][:, :], wts[:, 1, one], acc[:, :], ALU.mult, ALU.add)\
                    .then_inc(dve.sem, dve.step("sum"))
                ve.drain()


RWKV_IN, DIFF_IN = 0, RWKV_COLS
GATES_IN = RWKV_COLS + 3 * 512


def build_program(nc, g, out):
    def scratch(name, shape, dt=F32):
        return nc.dram_tensor(f"scratch_{name}", shape, dt).ap()

    x0 = g["x"]
    w_in, w_in2 = g["w_in"], g["w_in_2"]
    proj = scratch("proj", (1 + SEQ, w_in.shape[1]))
    norm_project(nc, "pin", x0, g["norm_mix"], w_in, 448, proj, 1, g["ident"])
    tokens = proj[1:, :]
    o_rwkv = scratch("o_rwkv", (SEQ, RW))
    o_diff = scratch("o_diff", (SEQ, AH * AV))
    rwkv(nc, proj, o_rwkv, g["rwkv_masks"], g)
    attention(nc, tokens, DIFF_IN, o_diff, g)
    x1 = scratch("x1", (SEQ, D))
    mix_branches(nc, x0, tokens, GATES_IN, o_rwkv, o_diff, x1, g)

    hbuf = scratch("hbuf", (SEQ, D))
    buf_tok = scratch("buf_tok", ((N_BLOCKS + 2) * P, 1), I32)
    dests = scratch("dests", (P, 2, NT), I32)
    weights = scratch("weights", (P, 2, NT))
    blk_e = scratch("blk_e", (N_BLOCKS, 1), I32)
    n_pairs = scratch("n_pairs", (1, 1), I32)
    ybuf = scratch("ybuf", (N_BLOCKS * P, D))
    x2 = scratch("x2", (SEQ, D))
    route(nc, x1, hbuf, buf_tok, ybuf, dests, weights, blk_e, n_pairs, g["route_consts"], g["token_ids"], g)
    experts(nc, hbuf, buf_tok, blk_e, n_pairs, ybuf, g["ident"], g)
    combine(nc, x1, ybuf, dests, weights, x2, g)
    x3 = scratch("x3", (SEQ, D))
    ple(nc, x2, g["p"], x3, g)

    proj2 = scratch("proj2", (SEQ, w_in2.shape[1]))
    norm_project(nc, "pin2", x3, g["pre_norm_w_2"], w_in2, 353, proj2, 0, g["ident"])
    y_ssd = scratch("y_ssd", (SEQ, SW))
    y_hgrn = scratch("y_hgrn", (SEQ, HH * HD))
    y_s5 = scratch("y_s5", (SEQ, S5W))
    ssd(nc, proj2, y_ssd, g["ssd_masks"], g)
    hgrn(nc, proj2, y_hgrn, g["hgrn_masks"], g)
    s5(nc, proj2, y_s5, g)
    mix_out(nc, x3, [y_ssd, y_hgrn, y_s5], out, g)


def constants():
    rows, cols = np.arange(P)[:, None], np.arange(P)[None, :]
    return {
        "ident": np.eye(P, dtype=np.float32),
        "causal": np.where(cols <= rows, 0, NEG).astype(np.float32),
        "rope": rope_consts(),
        "rwkv_masks": rwkv_masks()[1],
        "ind64": (rows // 64 == np.arange(2)).astype(np.float32),
        "ssd_masks": ssd_masks(),
        "hgrn_masks": hgrn_masks(),
        "ind32": (rows // 32 == np.arange(4)).astype(np.float32),
        "route_consts": route_consts(),
        "token_ids": token_ids(),
    }


def kernel(**inputs):
    import concourse.bacc as bacc
    from concourse.bass_utils import run_bass_kernel_spmd

    nc = bacc.Bacc("TRN2", target_bir_lowering=False, num_devices=1)
    arrays, g = {}, {}
    inputs = {n: a for n, a in inputs.items() if n != "hgrn_lower_bounds_2"}
    for source, own in ((inputs, False), (constants(), True)):
        for name, a in source.items():
            a = np.ascontiguousarray(a)
            if not own:
                a = a[0, 0] if name == "p" else a[0]
            key = f"in_{name}"
            arrays[key] = a
            g[name] = nc.dram_tensor(key, a.shape, mybir.dt.from_np(a.dtype), kind="ExternalInput").ap()
    out = nc.dram_tensor("out_0", (SEQ, D), F32, kind="ExternalOutput").ap()
    build_program(nc, g, out)
    r = run_bass_kernel_spmd(nc, [arrays], core_ids=[0])
    return r.results[0]["out_0"].reshape(1, SEQ, D)
```

```python
import math
from contextlib import ExitStack

import numpy as np
import concourse.bass as bass
from concourse import mybir

F32 = mybir.dt.float32
F32R = mybir.dt.float32r
I32 = mybir.dt.int32
U32 = mybir.dt.uint32
ALU = mybir.AluOpType
ACT = mybir.ActivationFunctionType
AX = mybir.AxisListType.X

P = 128
D = 1024
SEQ = 1024
NT = SEQ // P
KD = D // P
EPS = 1e-6


class Steps:

    def __init__(self, sem, names, base):
        self.base = base
        self.sem = sem
        self.names = names.split() if isinstance(names, str) else list(names)
        assert len(set(self.names)) == len(self.names)
        self.last = -1

    def step(self, name):
        self.last += 1
        assert self.names[self.last % len(self.names)] == name, (self.names[self.last % len(self.names)], name)
        return 1

    def at(self, name, turn=0):
        return turn * len(self.names) + (self.names.index(name) + 1 + self.base)

    def begin(self, eng):
        assert self.base == 1
        eng.sem_inc(self.sem, 1)

    def start(self, turn):
        return turn * len(self.names) + self.base


class Count:

    def __init__(self, sem):
        self.sem = sem

    def begin(self, eng):
        eng.sem_inc(self.sem, 2)

    def done(self, t):
        return t + 3


def each_tile(eng, body):
    body(0, 0, 0)
    with eng.Fori(0, NT // 2 - 1) as j:
        body(2 * j + 1, 1, j)
        body(2 * j + 2, 0, j + 1)
    body(NT - 1, 1, NT // 2 - 1)


def first(t):
    return isinstance(t, int) and t == 0


def last(t):
    return isinstance(t, int) and t == NT - 1


class Phase:

    def __init__(self, nc, name):
        self.nc, self.name, self.ctx, self.sems = nc, name, ExitStack(), []

    def __enter__(self):
        self.ctx.__enter__()
        return self

    def __exit__(self, *a):
        self.ctx.__exit__(*a)
        self.nc.clear_and_free_semaphores(self.sems)
        self.nc.all_engine_barrier()

    def sb(self, name, shape, dt=F32):
        return self.ctx.enter_context(self.nc.sbuf_tensor(f"{self.name}_sb_{name}", shape, dt))

    def psum(self, name="psum"):
        return self.ctx.enter_context(self.nc.psum_tensor(f"{self.name}_{name}", [P, 8, 512], F32))

    def sem(self, name):
        self.sems.append(self.nc.alloc_semaphore(f"{self.name}_{name}"))
        return self.sems[-1]

    def steps(self, name, names):
        return Steps(self.sem(name), names, 1)

    def marks(self, name, names):
        return Steps(self.sem(name), names, 0)

    def count(self, name):
        return Count(self.sem(name))

    def block(self):
        return self.ctx.enter_context(self.nc.Block())


def bcast(ap, n):
    p, a = ap.shape
    return ap.unsqueeze(2).to_broadcast([p, a, n])


def over(ap, n):
    p, a = ap.shape
    return ap.unsqueeze(1).to_broadcast([p, n, a])


def banks(ps, b, n=2):
    return ps[:, b:b + n, :].rearrange("p b c -> p (b c)")


def blocks(ps, b, n):
    return ps[:, b:b + (n + 3) // 4, :].rearrange("p b (k c) -> p (b k) c", c=P)[:, 0:n, :]


def block_of(ps, b, j):
    return ps[:, b + j // 4, (j % 4) * P:(j % 4 + 1) * P]


def norm_project(nc, name, x, gain, w, width, out, pad_rows, ident_d):
    cols = width + width % 2
    n_cols = w.shape[1]
    pairs = n_cols // (2 * width)
    assert pairs * 2 * width == n_cols
    with Phase(nc, name) as ph:
        ident = ph.sb("ident", [P, P])
        gcol = ph.sb("gcol", [P, KD])
        xt = ph.sb("xt", [P, NT, D])
        h = [ph.sb(f"h{b}", [P, D]) for b in range(2)]
        hg = [ph.sb(f"hg{b}", [P, KD, P]) for b in range(2)]
        junk = hg[0][:, :, :].rearrange("p k c -> p (k c)")
        ss = ph.sb("ss", [P, 4, NT])
        hT = [ph.sb(f"hT{part}", [P, KD, SEQ], F32R) for part in range(2)]
        raw = [ph.sb(f"raw{b}", [P, KD, cols]) for b in range(2)]
        wt = [[ph.sb(f"w{b}{part}", [P, KD, cols], F32R) for part in range(2)] for b in range(2)]
        og = [xt[:, :, 512 * b:512 * b + width] for b in range(2)]
        zero = ph.sb("zero", [P, n_cols // P]) if pad_rows else None
        ps = ph.psum()
        const_in = ph.sem("const_in")
        x_in = [ph.sem(f"x_in{t}") for t in range(NT)]
        w_in = [ph.sem(f"w_in{b}") for b in range(2)]
        out_st = [ph.sem(f"out_st{b}") for b in range(2)]
        zero_set = ph.sem("zero_set")
        zero_st = ph.sem("zero_st")
        passed = ph.sem("passed")
        squared, mean, root, inverse = (ph.sem(n) for n in ("squared", "mean", "root", "inverse"))
        normed, turned, gained, high, low = (ph.count(n) for n in ("normed", "turned", "gained", "high", "low"))
        split = ph.count("split")
        bank_full = ph.sem("bank_full")
        act_free = ph.sem("act_free")
        dve_free = ph.sem("dve_free")
        chunks = out[pad_rows:pad_rows + SEQ, :].rearrange("(t p) n -> p t n", p=P)
        w_v = w.rearrange("(k p) n -> p k n", p=P)
        blk = ph.block()

        @blk.sync
        def _(sp):
            for t in range(NT):
                sp.dma_start(xt[:, t, :], x[t * P:(t + 1) * P, :]).then_inc(x_in[t], 16)
            sp.dma_start(ident[:, :], ident_d).then_inc(const_in, 16)
            sp.dma_start(gcol[:, :], gain.rearrange("(k p) -> p k", p=P),
                         allow_slow_non_contiguous=True).then_inc(const_in, 16)
            with sp.Fori(0, pairs) as j:
                for b in range(2):
                    sp.wait_ge(split.sem, split.done(2 * j + b - 2))
                    sp.dma_start(raw[b][:, :, 0:width], w_v[:, :, bass.ds((2 * j + b) * width, width)])\
                        .then_inc(w_in[b], 16)

        @blk.gpsimd
        def _(pool):
            if pad_rows:
                pool.memset(zero[:, :], 0.0).then_inc(zero_set, 1)
                pool.wait_ge(zero_set, 1)
                for i in range(pad_rows):
                    pool.dma_start(out[i:i + 1, :].rearrange("o (p c) -> p (o c)", p=P), zero[:, :]).then_inc(zero_st, 16)
            if cols > width:
                for b in range(2):
                    pool.memset(raw[b][:, :, width:], 0.0)
                pool.drain()
            split.begin(pool)
            with pool.Fori(0, pairs) as j:
                for b in range(2):
                    pool.wait_ge(w_in[b], 16 * j + 16)
                    pool.sem_inc(passed, 1)
                    pool.wait_ge(bank_full, 8 * (2 * j + b) + 8)
                    pool.sem_inc(passed, 1)
                    pool.tensor_copy(wt[b][0][:, :, :], raw[b][:, :, :])
                    pool.drain()
                    pool.tensor_tensor(wt[b][1][:, :, :], raw[b][:, :, :], wt[b][0][:, :, :].bitcast(F32), ALU.subtract)\
                        .then_inc(split.sem, 1)
            if pad_rows:
                pool.wait_ge(zero_st, 16 * pad_rows)

        @blk.scalar
        def _(a):
            for t in range(NT):
                a.drain()
                a.wait_ge(x_in[t], 16)
                a.activation(junk[:, :], xt[:, t, :], ACT.Square, accum_out=ss[:, 0, t:t + 1]).then_inc(squared, 1)
            a.wait_ge(mean, 1)
            a.activation(ss[:, 2, :], ss[:, 1, :], ACT.Sqrt).then_inc(root, 1)
            a.wait_ge(inverse, 1)

            def norm(t, b, n):
                a.wait_ge(turned.sem, turned.done(t - 2))
                one = t if isinstance(t, int) else None
                row = xt[:, t, :] if one is not None else xt[:, bass.ds(t, 1), :].rearrange("p o d -> p (o d)")
                rstd = ss[:, 3, t:t + 1] if one is not None else ss[:, 3, bass.ds(t, 1)]
                a.activation(h[b][:, :], row, ACT.Copy, scale=rstd).then_inc(normed.sem, 1)

            def norm_and_round(t, b, n):
                if not last(t):
                    norm(t + 1, 1 - b, n)
                a.wait_ge(gained.sem, gained.done(t))
                a.activation(hT[0][:, :, bass.ds(t * P, P)], hg[b][:, :, :], ACT.Copy).then_inc(high.sem, 1)

            for c in (normed, high):
                c.begin(a)
            norm(0, 0, 0)
            each_tile(a, norm_and_round)
            a.sem_inc(act_free, 4)
            for b in range(2):
                a.sem_inc(out_st[b], 16)
            with a.Fori(0, pairs) as j:
                for b in range(2):
                    a.wait_ge(out_st[b], 16 * j + 16)
                    for t in range(0, NT, 2):
                        a.wait_ge(bank_full, 8 * (2 * j + b) + 16 + t + 1)
                        a.activation(og[b][:, t, :], ps[:, t, 0:width], ACT.Copy).then_inc(act_free, 1)
                    a.wait_ge(act_free, 4 * (2 * j + b) + 8)
                    a.wait_ge(dve_free, 4 * (2 * j + b) + 8)
                    a.dma_start(chunks[:, :, bass.ds((2 * j + b) * width, width)], og[b][:, :, :])\
                        .then_inc(out_st[b], 16)
            for b in range(2):
                a.wait_ge(out_st[b], 16 * (pairs + 1))

        @blk.vector
        def _(v):
            v.wait_ge(const_in, 32)
            v.wait_ge(squared, NT)
            v.tensor_scalar(ss[:, 1, :], ss[:, 0, :], 1.0 / D, EPS, ALU.mult, ALU.add).then_inc(mean, 1)
            v.wait_ge(root, 1)
            v.reciprocal(ss[:, 3, :], ss[:, 2, :]).then_inc(inverse, 1)

            def rest(t, b):
                v.wait_ge(high.sem, high.done(t))
                v.tensor_tensor(hT[1][:, :, bass.ds(t * P, P)], hg[b][:, :, :],
                                hT[0][:, :, bass.ds(t * P, P)].bitcast(F32), ALU.subtract).then_inc(low.sem, 1)

            def copy(t, b, n):
                v.drain()
                v.wait_ge(turned.sem, turned.done(t))
                v.tensor_tensor(hg[b][:, :, :], blocks(ps, 2 * b, 8), bcast(gcol[:, :], P), ALU.mult)\
                    .then_inc(gained.sem, 1)
                if not first(t):
                    rest(t - 1, 1 - b)

            for c in (gained, low):
                c.begin(v)
            each_tile(v, copy)
            rest(NT - 1, 1)
            v.sem_inc(dve_free, 4)
            with v.Fori(0, pairs) as j:
                for b in range(2):
                    v.wait_ge(out_st[b], 16 * j + 16)
                    for t in range(1, NT, 2):
                        v.wait_ge(bank_full, 8 * (2 * j + b) + 16 + t + 1)
                        v.tensor_copy(og[b][:, t, :], ps[:, t, 0:width]).then_inc(dve_free, 1)

        @blk.tensor
        def _(te):
            te.sem_inc(bank_full, 16)
            te.wait_ge(const_in, 32)
            def turn(t, b, n):
                te.wait_ge(normed.sem, normed.done(t))
                te.wait_ge(gained.sem, gained.done(t - 2))
                for k in range(KD):
                    mm = te.transpose(block_of(ps, 2 * b, k), h[b][:, k * P:(k + 1) * P], ident[:, :])
                mm.then_inc(turned.sem, 1)

            turned.begin(te)
            each_tile(te, turn)
            te.wait_ge(low.sem, low.done(NT - 1))
            with te.Fori(0, pairs) as j:
                for b in range(2):
                    te.wait_ge(split.sem, split.done(2 * j + b))
                    for t in range(NT):
                        te.wait_ge(dve_free if t % 2 else act_free, 4 * (2 * j + b) + t // 2 + 1)
                        for k in range(KD):
                            for n, (a_part, w_part) in enumerate(((0, 0), (0, 1), (1, 0))):
                                mm = te.matmul(ps[:, t, 0:cols], hT[a_part][:, k, t * P:(t + 1) * P],
                                               wt[b][w_part][:, k, :], start=(k == 0 and n == 0),
                                               stop=(k == KD - 1 and n == 2))
                        mm.then_inc(bank_full, 1)


def mix_branches(nc, x, proj, gcol, o_rwkv, o_diff, out, g):
    with Phase(nc, "mix") as ph:
        ident = ph.sb("ident", [P, P])
        wr = ph.sb("wr", [P, 4, D])
        wd = ph.sb("wd", [P, 4, D])
        wo = ph.sb("wo", [P, KD, D])
        two = lambda n, shape: [ph.sb(f"{n}{b}", shape) for b in range(2)]
        ob = two("ob", [P, 2, 512])
        gt = two("gt", [P, 2 * D])
        xt = two("xt", [P, D])
        sg = two("sg", [P, 2 * D])
        oT = ph.sb("oT", [P, KD, P])
        m = ph.sb("m", [P, D])
        m2 = ph.sb("m2", [P, D])
        mT = ph.sb("mT", [P, KD, P])
        y = two("y", [P, D])
        ps = ph.psum()
        const_in, passed = ph.sem("const_in"), ph.sem("passed")
        o_in, g_in, x_in, y_st = ([ph.sem(f"{n}{b}") for b in range(2)] for n in ("o_in", "g_in", "x_in", "y_st"))
        gates, turned, copied, branches, mixed, mturned, mcopied, summed, added = (ph.count(n) for n in (
            "gates", "turned", "copied", "branches", "mixed", "mturned", "mcopied", "summed", "added"))
        blk = ph.block()

        @blk.sync
        def _(sp):
            for dst, src in ((ident[:, :], g["ident"]),
                             (wr[:, :, :], g["w_branch_rwkv"].rearrange("(k p) n -> p k n", p=P)),
                             (wd[:, :, :], g["w_branch_diff"].rearrange("(k p) n -> p k n", p=P)),
                             (wo[:, :, :], g["w_out"].rearrange("(k p) n -> p k n", p=P))):
                sp.dma_start(dst, src).then_inc(const_in, 16)

            def load_branches(t, b):
                sp.dma_start(ob[b][:, 0, :], o_rwkv[bass.ds(t * P, P), :]).then_inc(o_in[b], 16)
                sp.dma_start(ob[b][:, 1, :], o_diff[bass.ds(t * P, P), :]).then_inc(o_in[b], 16)
                sp.dma_start(gt[b][:, :], proj[bass.ds(t * P, P), gcol:gcol + 2 * D]).then_inc(g_in[b], 16)

            def load_x(t, b):
                sp.dma_start(xt[b][:, :], x[bass.ds(t * P, P), :]).then_inc(x_in[b], 16)

            def store(t, b):
                sp.wait_ge(added.sem, added.done(t))
                sp.dma_start(out[bass.ds(t * P, P), :], y[b][:, :]).then_inc(y_st[b], 16)

            for b in range(2):
                sp.sem_inc(y_st[b], 16)
                load_branches(b, b)
                load_x(b, b)
            with sp.Fori(0, NT // 2 - 1) as j:
                for b in range(2):
                    t = 2 * j + b
                    sp.wait_ge(turned.sem, turned.done(t))
                    sp.sem_inc(passed, 1)
                    sp.wait_ge(gates.sem, gates.done(t))
                    load_branches(t + 2, b)
                    store(t, b)
                    load_x(t + 2, b)
            for b in range(2):
                store(NT - 2 + b, b)
            for b in range(2):
                sp.wait_ge(y_st[b], 16 * (NT // 2 + 1))

        @blk.scalar
        def _(s):
            def body(t, b, n):
                s.wait_ge(g_in[b], 16 * n + 16)
                s.wait_ge(mixed.sem, mixed.done(t - 2))
                s.activation(sg[b][:, :], gt[b][:, :], ACT.Sigmoid).then_inc(gates.sem, 1)

            gates.begin(s)
            each_tile(s, body)

        @blk.vector
        def _(ve):
            tt = ve.tensor_tensor

            def turn_inputs(t):
                ve.drain()
                ve.wait_ge(turned.sem, turned.done(t))
                ve.tensor_copy(oT[:, :, :], blocks(ps, 0, 8)).then_inc(copied.sem, 1)

            def turn_mix(t):
                ve.drain()
                ve.wait_ge(mturned.sem, mturned.done(t))
                ve.tensor_copy(mT[:, :, :], blocks(ps, 0, 8)).then_inc(mcopied.sem, 1)

            def add(t, b, n):
                ve.drain()
                ve.wait_ge(summed.sem, summed.done(t))
                ve.wait_ge(x_in[b], 16 * n + 16)
                ve.wait_ge(y_st[b], 16 * n + 16)
                tt(y[b][:, :], xt[b][:, :], banks(ps, 6), ALU.add).then_inc(added.sem, 1)

            def body(t, b, n):
                if not first(t):
                    turn_mix(t - 1)
                ve.drain()
                ve.wait_ge(gates.sem, gates.done(t))
                ve.wait_ge(branches.sem, branches.done(t))
                tt(m[:, :], sg[b][:, 0:D], banks(ps, 2), ALU.mult)
                tt(m2[:, :], sg[b][:, D:2 * D], banks(ps, 4), ALU.mult)
                ve.drain()
                tt(m[:, :], m[:, :], m2[:, :], ALU.add).then_inc(mixed.sem, 1)
                if not last(t):
                    turn_inputs(t + 1)
                if not first(t):
                    add(t - 1, 1 - b, n - 1 + b)

            for c in (copied, mixed, mcopied, added):
                c.begin(ve)
            turn_inputs(0)
            each_tile(ve, body)
            turn_mix(NT - 1)
            add(NT - 1, 1, NT // 2 - 1)

        @blk.tensor
        def _(te):
            def turn_inputs(t, b, n):
                te.wait_ge(o_in[b], 32 * n + 32)
                te.wait_ge(mcopied.sem, mcopied.done(t - 2))
                for i in range(8):
                    mm = te.transpose(block_of(ps, 0, i), ob[b][:, i // 4, (i % 4) * P:(i % 4 + 1) * P], ident[:, :])
                mm.then_inc(turned.sem, 1)

            def out_product(t):
                te.wait_ge(mcopied.sem, mcopied.done(t))
                te.wait_ge(added.sem, added.done(t - 1))
                for n in range(2):
                    for k in range(KD):
                        mm = te.matmul(ps[:, 6 + n, :], mT[:, k, :], wo[:, k, n * 512:(n + 1) * 512],
                                       start=(k == 0), stop=(k == KD - 1))
                mm.then_inc(summed.sem, 1)

            def body(t, b, n):
                te.wait_ge(copied.sem, copied.done(t))
                te.wait_ge(mixed.sem, mixed.done(t - 1))
                for bank, w, k0 in ((2, wr, 0), (4, wd, 4)):
                    for h in range(2):
                        for k in range(4):
                            mm = te.matmul(ps[:, bank + h, :], oT[:, k0 + k, :], w[:, k, h * 512:(h + 1) * 512],
                                           start=(k == 0), stop=(k == 3))
                mm.then_inc(branches.sem, 1)
                if not last(t):
                    turn_inputs(t + 1, 1 - b, n + b)
                if not first(t):
                    out_product(t - 1)
                te.wait_ge(mixed.sem, mixed.done(t))
                if not last(t):
                    te.wait_ge(copied.sem, copied.done(t + 1))
                for i in range(8):
                    mm = te.transpose(block_of(ps, 0, i), m[:, i * P:(i + 1) * P], ident[:, :])
                mm.then_inc(mturned.sem, 1)

            for c in (turned, branches, mturned, summed):
                c.begin(te)
            te.wait_ge(const_in, 64)
            turn_inputs(0, 0, 0)
            each_tile(te, body)
            out_product(NT - 1)


def ple(nc, x, p, out, g):
    with Phase(nc, "ple") as ph:
        ident = ph.sb("ident", [P, P])
        gcol = ph.sb("gcol", [P, KD])
        wg = ph.sb("wg", [P, KD, D])
        wp = ph.sb("wp", [P, 2, D])
        two = lambda n, shape: [ph.sb(f"{n}{b}", shape) for b in range(2)]
        xt = two("xt", [P, D])
        pt = two("pt", [P, 2, P])
        junk = ph.sb("junk", [P, D])
        ss = two("ss", [P, 4])
        h = ph.sb("h", [P, D])
        hT = ph.sb("hT", [P, KD, P])
        pT = two("pT", [P, 2, P])
        sg = ph.sb("sg", [P, D])
        m = ph.sb("m", [P, D])
        y = two("y", [P, D])
        ps = ph.psum()
        const_in = ph.sem("const_in")
        x_in, y_st = ([ph.sem(f"{n}{b}") for b in range(2)] for n in ("x_in", "y_st"))
        squared, mean, root, normed, turned, copied, gate_sums, proj_sums, gates, added = (ph.count(n) for n in (
            "squared", "mean", "root", "normed", "turned", "copied", "gate_sums", "proj_sums", "gates", "added"))
        blk = ph.block()

        @blk.sync
        def _(sp):
            for dst, src in ((ident[:, :], g["ident"]), (gcol[:, :], g["norm_ple"].rearrange("(k p) -> p k", p=P)),
                             (wg[:, :, :], g["w_ple_gate"].rearrange("(k p) n -> p k n", p=P)),
                             (wp[:, :, :], g["w_ple_proj"].rearrange("(k p) n -> p k n", p=P))):
                sp.dma_start(dst, src, allow_slow_non_contiguous=True).then_inc(const_in, 16)

            def load(t, b):
                sp.dma_start(xt[b][:, :], x[bass.ds(t * P, P), :]).then_inc(x_in[b], 16)
                sp.dma_start(pt[b][:, :, :].rearrange("p a c -> p (a c)"), p[bass.ds(t * P, P), :]).then_inc(x_in[b], 16)

            def store(t, b):
                sp.wait_ge(added.sem, added.done(t))
                sp.dma_start(out[bass.ds(t * P, P), :], y[b][:, :]).then_inc(y_st[b], 16)

            for b in range(2):
                sp.sem_inc(y_st[b], 16)
                load(b, b)
            with sp.Fori(0, NT // 2 - 1) as j:
                for b in range(2):
                    store(2 * j + b, b)
                    load(2 * j + b + 2, b)
            for b in range(2):
                store(NT - 2 + b, b)
            for b in range(2):
                sp.wait_ge(y_st[b], 16 * (NT // 2 + 1))

        @blk.scalar
        def _(s):
            def norm(t, b, n):
                s.wait_ge(x_in[b], 32 * n + 32)
                s.wait_ge(normed.sem, normed.done(t - 1))
                s.activation(junk[:, :], xt[b][:, :], ACT.Square, accum_out=ss[b][:, 0:1]).then_inc(squared.sem, 1)
                s.wait_ge(mean.sem, mean.done(t))
                s.activation(ss[b][:, 2:3], ss[b][:, 1:2], ACT.Sqrt).then_inc(root.sem, 1)

            def body(t, b, n):
                if not last(t):
                    norm(t + 1, 1 - b, n + b)
                s.wait_ge(gate_sums.sem, gate_sums.done(t))
                s.wait_ge(added.sem, added.done(t - 1))
                s.activation(sg[:, :], banks(ps, 4), ACT.Sigmoid).then_inc(gates.sem, 1)

            for c in (squared, root, gates):
                c.begin(s)
            norm(0, 0, 0)
            each_tile(s, body)

        @blk.vector
        def _(ve):
            tt = ve.tensor_tensor

            def norm(t, b, n):
                ve.drain()
                ve.wait_ge(squared.sem, squared.done(t))
                ve.tensor_scalar(ss[b][:, 1:2], ss[b][:, 0:1], 1.0 / D, EPS, ALU.mult, ALU.add).then_inc(mean.sem, 1)
                ve.drain()
                ve.wait_ge(root.sem, root.done(t))
                ve.reciprocal(ss[b][:, 3:4], ss[b][:, 2:3])
                ve.drain()
                ve.wait_ge(turned.sem, turned.done(t - 1))
                ve.tensor_scalar(h[:, :], xt[b][:, :], ss[b][:, 3:4], None, ALU.mult).then_inc(normed.sem, 1)

            def copy(t, b, n):
                ve.drain()
                ve.wait_ge(turned.sem, turned.done(t))
                ve.tensor_copy(pT[b][:, :, :], blocks(ps, 2, 2))
                tt(hT[:, :, :], blocks(ps, 0, 8), bcast(gcol[:, :], P), ALU.mult).then_inc(copied.sem, 1)

            def body(t, b, n):
                if not last(t):
                    norm(t + 1, 1 - b, n + b)
                    copy(t + 1, 1 - b, n + b)
                ve.drain()
                ve.wait_ge(gates.sem, gates.done(t))
                ve.wait_ge(proj_sums.sem, proj_sums.done(t))
                tt(m[:, :], sg[:, :], banks(ps, 6), ALU.mult)
                ve.drain()
                ve.wait_ge(y_st[b], 16 * n + 16)
                tt(y[b][:, :], xt[b][:, :], m[:, :], ALU.add).then_inc(added.sem, 1)

            for c in (mean, normed, copied, added):
                c.begin(ve)
            ve.wait_ge(const_in, 64)
            norm(0, 0, 0)
            copy(0, 0, 0)
            each_tile(ve, body)

        @blk.tensor
        def _(te):
            def turn(t, b, n):
                te.wait_ge(normed.sem, normed.done(t))
                for i in range(8):
                    te.transpose(block_of(ps, 0, i), h[:, i * P:(i + 1) * P], ident[:, :])
                for i in range(2):
                    mm = te.transpose(block_of(ps, 2, i), pt[b][:, i, :], ident[:, :])
                mm.then_inc(turned.sem, 1)

            def product(bank, a, w, n_k):
                for h in range(2):
                    for k in range(n_k):
                        mm = te.matmul(ps[:, bank + h, :], a[:, k, :], w[:, k, h * 512:(h + 1) * 512],
                                       start=(k == 0), stop=(k == n_k - 1))
                return mm

            def body(t, b, n):
                te.wait_ge(copied.sem, copied.done(t))
                te.wait_ge(gates.sem, gates.done(t - 1))
                product(4, hT, wg, KD).then_inc(gate_sums.sem, 1)
                if not last(t):
                    turn(t + 1, 1 - b, n + b)
                te.wait_ge(added.sem, added.done(t - 1))
                product(6, pT[b], wp, 2).then_inc(proj_sums.sem, 1)

            for c in (turned, gate_sums, proj_sums):
                c.begin(te)
            te.wait_ge(const_in, 64)
            turn(0, 0, 0)
            each_tile(te, body)


def mix_out(nc, x, mixes, out, g):
    KM = 16
    with Phase(nc, "fin") as ph:
        ident = ph.sb("ident", [P, P])
        w = ph.sb("w", [P, KM, D])
        post = ph.sb("post", [P, D])
        two = lambda n, shape: [ph.sb(f"{n}{b}", shape) for b in range(2)]
        mt = two("mt", [P, KM * P])
        xt = two("xt", [P, D])
        mT = two("mT", [P, KM, P])
        z = ph.sb("z", [P, D])
        junk = ph.sb("junk", [P, D])
        ss = ph.sb("ss", [P, 4])
        y = two("y", [P, D])
        ps = ph.psum()
        const_in, passed = ph.sem("const_in"), ph.sem("passed")
        mix_in, x_in, y_st = ([ph.sem(f"{n}{b}") for b in range(2)] for n in ("mix_in", "x_in", "y_st"))
        turned, copied, summed, squared, mean, root, scaled, added = (ph.count(n) for n in (
            "turned", "copied", "summed", "squared", "mean", "root", "scaled", "added"))
        blk = ph.block()

        @blk.sync
        def _(sp):
            for dst, src in ((ident[:, :], g["ident"]), (post[:, :], g["post_norm_w_2"].partition_broadcast(P))):
                sp.dma_start(dst, src).then_inc(const_in, 16)

            def load_mix(t, b):
                at = 0
                for mix in mixes:
                    n = mix.shape[1]
                    sp.dma_start(mt[b][:, at:at + n], mix[bass.ds(t * P, P), :]).then_inc(mix_in[b], 16)
                    at += n

            def load_x(t, b):
                sp.dma_start(xt[b][:, :], x[bass.ds(t * P, P), :]).then_inc(x_in[b], 16)

            def store(t, b):
                sp.wait_ge(added.sem, added.done(t))
                sp.dma_start(out[bass.ds(t * P, P), :], y[b][:, :]).then_inc(y_st[b], 16)

            for b in range(2):
                sp.sem_inc(y_st[b], 16)
                load_mix(b, b)
                load_x(b, b)
            with sp.Fori(0, NT // 2 - 1) as j:
                for b in range(2):
                    t = 2 * j + b
                    sp.wait_ge(turned.sem, turned.done(t))
                    sp.sem_inc(passed, 1)
                    load_mix(t + 2, b)
                    store(t, b)
                    load_x(t + 2, b)
            for b in range(2):
                store(NT - 2 + b, b)
            for b in range(2):
                sp.wait_ge(y_st[b], 16 * (NT // 2 + 1))

        @blk.scalar
        def _(s):
            def body(t, b, n):
                s.wait_ge(summed.sem, summed.done(t))
                s.wait_ge(scaled.sem, scaled.done(t - 1))
                s.activation(junk[:, :], banks(ps, 4 + 2 * b), ACT.Square, accum_out=ss[:, 0:1]).then_inc(squared.sem, 1)
                s.wait_ge(mean.sem, mean.done(t))
                s.activation(ss[:, 2:3], ss[:, 1:2], ACT.Sqrt).then_inc(root.sem, 1)

            s.dma_start(w[:, :, :], g["w_out_2"].rearrange("(k p) n -> p k n", p=P)).then_inc(const_in, 16)
            for c in (squared, root):
                c.begin(s)
            each_tile(s, body)

        @blk.vector
        def _(ve):
            def copy(t, b):
                ve.drain()
                ve.wait_ge(turned.sem, turned.done(t))
                ve.wait_ge(summed.sem, summed.done(t - 2))
                ve.tensor_copy(mT[b][:, :, :], blocks(ps, 0, KM)).then_inc(copied.sem, 1)

            def body(t, b, n):
                if not last(t):
                    copy(t + 1, 1 - b)
                ve.drain()
                ve.wait_ge(squared.sem, squared.done(t))
                ve.tensor_scalar(ss[:, 1:2], ss[:, 0:1], 1.0 / D, EPS, ALU.mult, ALU.add).then_inc(mean.sem, 1)
                ve.drain()
                ve.wait_ge(root.sem, root.done(t))
                ve.reciprocal(ss[:, 3:4], ss[:, 2:3])
                ve.drain()
                ve.scalar_tensor_tensor(z[:, :], banks(ps, 4 + 2 * b), ss[:, 3:4], post[:, :], ALU.mult, ALU.mult)\
                    .then_inc(scaled.sem, 1)
                ve.drain()
                ve.wait_ge(x_in[b], 16 * n + 16)
                ve.wait_ge(y_st[b], 16 * n + 16)
                ve.tensor_tensor(y[b][:, :], xt[b][:, :], z[:, :], ALU.add).then_inc(added.sem, 1)

            for c in (copied, mean, scaled, added):
                c.begin(ve)
            ve.wait_ge(const_in, 48)
            copy(0, 0)
            each_tile(ve, body)

        @blk.tensor
        def _(te):
            def turn(t, b, n):
                te.wait_ge(mix_in[b], 48 * n + 48)
                te.wait_ge(copied.sem, copied.done(t - 1))
                for i in range(KM):
                    mm = te.transpose(block_of(ps, 0, i), mt[b][:, i * P:(i + 1) * P], ident[:, :])
                mm.then_inc(turned.sem, 1)

            def body(t, b, n):
                if not last(t):
                    turn(t + 1, 1 - b, n + b)
                te.wait_ge(copied.sem, copied.done(t))
                te.wait_ge(scaled.sem, scaled.done(t - 2))
                for h in range(2):
                    for k in range(KM):
                        mm = te.matmul(ps[:, 4 + 2 * b + h, :], mT[b][:, k, :], w[:, k, h * 512:(h + 1) * 512],
                                       start=(k == 0), stop=(k == KM - 1))
                mm.then_inc(summed.sem, 1)

            for c in (turned, summed):
                c.begin(te)
            te.wait_ge(const_in, 48)
            turn(0, 0, 0)
            each_tile(te, body)


RH, RD = 8, 64
RW = RH * RD
RWKV_COLS = 1792
GN_EPS = 64e-5
CH = 64


def rwkv_masks():
    s, t = np.arange(P)[:, None], np.arange(P)[None, :]
    same = lambda n: (s // n) == (t // n)
    up = s < t
    m = dict(
        ident=s == t,
        cum=same(64) & (s <= t),
        suf=same(64) & (s > t),
        m16=same(16) & up, n16=same(16) & (s > t),
        strict=same(64) & up, incl=same(64) & (s <= t),
        n32=same(32) & ~same(16) & (s > t),
        n64=same(64) & ~same(32) & (s > t),
    )
    return list(m), np.concatenate([v.astype(np.float32) for v in m.values()], axis=1)


def rwkv(nc, pr, out, masks_d, g):
    mnames, _ = rwkv_masks()
    with Phase(nc, "rwkv") as ph:
        masks = ph.sb("masks", [P, len(mnames) * P])
        M = {n: masks[:, i * P:(i + 1) * P] for i, n in enumerate(mnames)}
        ind = ph.sb("ind", [P, 2])
        mu = ph.sb("mu", [P, RWKV_COLS])
        rows = ph.sb("rows", [P, 7, RW])
        w0, a0, k_k, k_a, r_k, ln_w, ln_b = (rows[:, i, :] for i in range(7))
        w2 = ph.sb("w2", [64, RW])
        a2 = ph.sb("a2", [64, RW])
        g2 = ph.sb("g2", [P, RW])
        x = ph.sb("x", [P, RWKV_COLS])
        prev = ph.sb("prev", [P, RWKV_COLS])
        xs = [ph.sb(f"xs{b}", [P, RWKV_COLS]) for b in range(2)]
        r, k, v = ([x_[:, i * RW:(i + 1) * RW] for x_ in xs] for i in range(3))
        xw, xa, xg = ([x_[:, c] for x_ in xs] for c in (slice(1536, 1600), slice(1600, 1664), slice(1664, 1792)))
        lo = ph.sb("lo", [P, 2, P])
        loT = ph.sb("loT", [P, 3, P])
        wide = ph.sb("wide", [P, 21, RW])
        wp, ap_, gg0, sw, a, ld, kk, sq, km, tmp, eL, enL, eS, eLm, al, rh, be, ka, bE, kE, gg1 = (
            wide[:, i, :] for i in range(21))
        gg = [gg0, gg1]
        small = ph.sb("small", [P, 6, RH])
        gn = ph.sb("gn", [P, 4, RH])
        sqy = ph.sb("sqy", [P, RW])
        arT = ph.sb("arT", [P, 4, 2, P])
        beT = ph.sb("beT", [P, 4, P])
        kaT = ph.sb("kaT", [P, 4, P])
        pend = ph.sb("pend", [64, RH, 2])
        G4 = [P, 4, P]
        two = lambda n, shape: [ph.sb(f"{n}{q}", shape) for q in range(2)]
        M1, N1, X, XT, M2, N2, M4, N4, N32, N64, QB, Km, QK = (two(n, G4) for n in (
            "M1", "N1", "X", "XT", "M2", "N2", "M4", "N4", "N32", "N64", "QB", "Km", "QK"))
        M8, Z = M2, N2
        aKV = two("aKV", [P, 4, 2, 64])
        AG = two("AG", [P, 4, 2, 64])
        side = ph.sb("side", [P, 4, RW])
        bon, bk, lg, bg = (side[:, i, :] for i in range(4))
        bsum = ph.sb("bsum", [P, RH])
        ET = ph.sb("ET", [64, RH, P])
        F = ph.sb("F", [P, RH, 64])
        HT = ph.sb("HT", [64, RH, 2, 64])
        J = ph.sb("J", [64, RH, 2, 64])
        S = ph.sb("S", [64, RH, 64])
        y = ph.sb("y", [P, RH, 64])
        yo = ph.sb("yo", [P, RH, 64])
        ps = ph.psum()
        const_in, x_in, o_st = ph.sem("const_in"), ph.sem("x_in"), ph.sem("o_st")
        passed = ph.sem("passed")

        groups = range(2)
        both = lambda names: " ".join(f"{n}_{q}" for n in names.split() for q in groups)
        fa = ph.steps("front_act", "lora_in decays norm gate exps lmexp")
        fd = ph.steps("front_dve", "xs loT lora ld lm scaled")
        fp = ph.steps("front_pe", "lora_t lora_wa lora_g sums")
        act = ph.steps("act", "arT " + both("p2 x2 x4 z32 z64 ag eh"))
        dve = ph.steps("dve", "bkT " + both("masked") + " " + both("x1") + " "
                       + both("p2") + " bsum " + both("x2 x4 x8 x32 x64 eh") + " s0 s1")
        pe = ph.steps("pe", "turned " + both("scores p2 qk x2 x4 x8 z32 x32 z64 x64 ag eh") + " y0 y1")
        pool = ph.steps("pool", "diag alpha rk bonus")
        shift = ph.steps("shift", "done")
        na = ph.steps("norm_act", "root")
        nd = ph.steps("norm_dve", "var out")
        blk = ph.block()

        def pg(b, n=P):
            return ps[:, b, 0:4 * n].rearrange("p (h c) -> p h c", c=n)

        @blk.sync
        def _(sp):
            for dst, src in ((masks[:, :], masks_d), (ind[:, :], g["ind64"]),
                             (mu[:, :], g["rwkv_mu"].partition_broadcast(P)),
                             (w0, g["rwkv_w0"].partition_broadcast(P)), (a0, g["rwkv_a0"].partition_broadcast(P)),
                             (k_k, g["rwkv_k_k"].partition_broadcast(P)), (k_a, g["rwkv_k_a"].partition_broadcast(P)),
                             (r_k, g["rwkv_r_k"].rearrange("h d -> (h d)").partition_broadcast(P)),
                             (ln_w, g["rwkv_ln_w"].partition_broadcast(P)),
                             (ln_b, g["rwkv_ln_b"].partition_broadcast(P)),
                             (w2[:, :], g["rwkv_w2"]), (a2[:, :], g["rwkv_a2"]), (g2[:, :], g["rwkv_g2"])):
                sp.dma_start(dst, src).then_inc(const_in, 16)
            sp.sem_inc(o_st, 16)

            def load(t):
                sp.dma_start(x[:, :], pr[bass.ds(t * P + 1, P), 0:RWKV_COLS]).then_inc(x_in, 16)
                sp.dma_start(prev[:, :], pr[bass.ds(t * P, P), 0:RWKV_COLS]).then_inc(x_in, 16)

            def store(t):
                sp.wait_ge(nd.sem, nd.at("out", t))
                sp.dma_start(out[bass.ds(t * P, P), :], yo[:, :, :].rearrange("p h d -> p (h d)")).then_inc(o_st, 16)

            load(0)
            sp.wait_ge(fd.sem, fd.at("xs", 0))
            load(1)
            with sp.Fori(0, NT - 2) as t:
                sp.wait_ge(fd.sem, fd.at("xs", t + 1))
                load(t + 2)
                store(t)
            store(NT - 2)
            store(NT - 1)
            sp.wait_ge(o_st, 16 * (NT + 1))

        @blk.scalar
        def _(s):
            def lora_in(t, b):
                s.wait_ge(fd.sem, fd.at("xs", t))
                s.activation(lo[:, 0, 0:64], xw[b], ACT.Tanh)
                s.activation(lo[:, 1, :], xg[b], ACT.Sigmoid).then_inc(fa.sem, fa.step("lora_in"))

            def decays(t):
                s.wait_ge(fd.sem, fd.at("lora", t))
                s.activation(sw, wp, ACT.Sigmoid)
                s.activation(a, ap_, ACT.Sigmoid).then_inc(fa.sem, fa.step("decays"))
                s.activation(small[:, 1, :], small[:, 0, :], ACT.Sqrt).then_inc(fa.sem, fa.step("norm"))

            def gate(t, b):
                s.wait_ge(fp.sem, fp.at("lora_g", t))
                s.activation(gg[b], ps[:, 7, :], ACT.Copy).then_inc(fa.sem, fa.step("gate"))

            def exps(t):
                s.wait_ge(fp.sem, fp.at("sums", t))
                s.activation(eL, ps[:, 4, :], ACT.Exp)
                s.activation(enL, ps[:, 4, :], ACT.Exp, scale=-1.0)
                s.activation(eS, ps[:, 5, :], ACT.Exp)
                s.activation(pend[:, :, :].rearrange("p h c -> p (h c)"), ps[0:64, 3, 0:16], ACT.Exp)\
                    .then_inc(fa.sem, fa.step("exps"))
                s.wait_ge(fd.sem, fd.at("lm", t))
                s.activation(eLm, tmp, ACT.Exp).then_inc(fa.sem, fa.step("lmexp"))

            def copies(t, stage, outs):
                for q in groups:
                    s.wait_ge(pe.sem, pe.at(f"{stage}_{q}", t))
                    for bank, dst in outs:
                        copy = s.activation(dst[q][:, :, :], pg(4 * q + bank), ACT.Copy)
                    copy.then_inc(act.sem, act.step(f"{stage}_{q}"))

            def root(t):
                s.wait_ge(nd.sem, nd.at("var", t))
                s.activation(gn[:, 3, :], gn[:, 2, :], ACT.Sqrt).then_inc(na.sem, na.step("root"))

            def body(t, b, n):
                s.wait_ge(pe.sem, pe.at("turned", t))
                s.activation(arT[:, :, 0, :], pg(0), ACT.Copy)
                s.activation(arT[:, :, 1, :], pg(1), ACT.Copy).then_inc(act.sem, act.step("arT"))
                if not first(t):
                    root(t - 1)
                copies(t, "p2", ((0, M2), (1, N2)))
                copies(t, "x2", ((2, M4), (3, N4)))
                if not last(t):
                    lora_in(t + 1, 1 - b)
                copies(t, "x4", ((2, M8),))
                copies(t, "z32", ((2, Z),))
                copies(t, "z64", ((2, Z),))
                if not last(t):
                    decays(t + 1)
                    gate(t + 1, 1 - b)
                for q in groups:
                    s.wait_ge(pe.sem, pe.at(f"ag_{q}", t))
                    s.activation(AG[q][:, :, :, :].rearrange("p h a c -> p h (a c)"), pg(4 * q + 1), ACT.Copy)\
                        .then_inc(act.sem, act.step(f"ag_{q}"))
                for q in groups:
                    s.wait_ge(pe.sem, pe.at(f"eh_{q}", t))
                    s.activation(ET[:, slice(q, RH, 2), :], ps[0:64, 4 * q, :].rearrange("p (h c) -> p h c", c=P), ACT.Copy)
                    s.activation(F[:, slice(q, RH, 2), :], pg(4 * q + 1, 64), ACT.Copy).then_inc(act.sem, act.step(f"eh_{q}"))
                if not last(t):
                    exps(t + 1)

            for c in (fa, act, na):
                c.begin(s)
            lora_in(0, 0)
            decays(0)
            gate(0, 0)
            exps(0)
            each_tile(s, body)
            root(NT - 1)

        @blk.gpsimd
        def _(po):
            h8 = lambda z: z.rearrange("p (h d) -> p h d", d=RD)
            tt = po.tensor_tensor

            def shift_in(t):
                po.drain()
                po.wait_ge(x_in, 32 * t + 32)
                tt(prev[:, :], prev[:, :], x[:, :], ALU.subtract)
                po.drain()
                tt(prev[:, :], prev[:, :], mu[:, :], ALU.mult).then_inc(shift.sem, shift.step("done"))

            def body(t, b, n):
                po.drain()
                po.wait_ge(pe.sem, pe.start(t))
                po.wait_ge(fa.sem, fa.at("exps", t))
                for c in range(2):
                    ins = tt(HT[:, :, c, :], bcast(pend[:, :, c], 64), over(M["ident"][0:64, 0:64], RH), ALU.mult)
                ins.then_inc(pool.sem, pool.step("diag"))
                po.drain()
                po.wait_ge(fd.sem, fd.at("scaled", t))
                tt(bon, r[b], km, ALU.mult)
                for q in groups:
                    ins = po.tensor_copy(aKV[q][:, :, 0, :], h8(al)[:, slice(q, RH, 2), :])
                ins.then_inc(pool.sem, pool.step("alpha"))
                po.drain()
                tt(bon, bon, r_k, ALU.mult).then_inc(pool.sem, pool.step("rk"))
                if not last(t):
                    shift_in(t + 1)
                po.drain()
                if not first(t):
                    po.wait_ge(nd.sem, nd.at("out", t - 1))
                tt(lg, ln_w, gg[b], ALU.mult)
                po.drain()
                po.wait_ge(dve.sem, dve.at("bsum", t))
                tt(h8(bk), h8(v[b]), bcast(bsum[:, :], RD), ALU.mult)
                po.drain()
                tt(bon, bk, ln_b, ALU.add)
                po.drain()
                tt(bg, bon, gg[b], ALU.mult).then_inc(pool.sem, pool.step("bonus"))

            po.wait_ge(const_in, 16 * 13)
            for c in (pool, shift):
                c.begin(po)
            shift_in(0)
            each_tile(po, body)

        @blk.vector
        def _(ve):
            h8 = lambda z: z.rearrange("p (h d) -> p h d", d=RD)

            def tt(o, i0, i1, op):
                return ve.tensor_tensor(o, i0, i1, op)

            def shifted(t, b):
                ve.drain()
                ve.wait_ge(shift.sem, shift.at("done", t))
                tt(xs[b][:, :], prev[:, :], x[:, :], ALU.add).then_inc(fd.sem, fd.step("xs"))

            def direction(b):
                ve.drain()
                tt(kk, k[b], k_k, ALU.mult)
                ve.drain()
                tt(sq, kk, kk, ALU.mult)
                ve.drain()
                ve.tensor_reduce(small[:, 0, :], h8(sq), AX, ALU.add)

            def lora_turned(t):
                ve.drain()
                ve.wait_ge(fp.sem, fp.at("lora_t", t))
                ve.tensor_copy(loT[0:64, 0:2, :], ps[0:64, 3, 0:2 * P].rearrange("p (a c) -> p a c", c=P))
                ve.tensor_copy(loT[:, 2, :], ps[:, 3, 2 * P:3 * P]).then_inc(fd.sem, fd.step("loT"))

            def lora_out(t):
                ve.drain()
                ve.wait_ge(fp.sem, fp.at("lora_wa", t))
                tt(wp, ps[:, 7, :], w0, ALU.add)
                tt(ap_, ps[:, 3, :], a0, ALU.add).then_inc(fd.sem, fd.step("lora"))

            def decays(t, b):
                ve.drain()
                ve.wait_ge(fa.sem, fa.at("decays", t))
                ve.tensor_scalar(ld, sw, -math.exp(-0.5), None, ALU.mult).then_inc(fd.sem, fd.step("ld"))
                ve.drain()
                ve.wait_ge(fa.sem, fa.at("norm", t))
                ve.tensor_scalar(small[:, 4, :], small[:, 1, :], 1e-12, None, ALU.max)
                ve.scalar_tensor_tensor(km, a, 1.0, k_a, ALU.subtract, ALU.mult)
                ve.drain()
                ve.reciprocal(small[:, 5, :], small[:, 4, :])
                ve.scalar_tensor_tensor(km, km, 1.0, k[b], ALU.add, ALU.mult)
                ve.drain()
                tt(h8(kk), h8(kk), bcast(small[:, 5, :], RD), ALU.mult)
                ve.drain()
                ve.scalar_tensor_tensor(sq, kk, -1.0, a, ALU.mult, ALU.mult)

            def scale(t, b):
                ve.drain()
                ve.wait_ge(fa.sem, fa.at("exps", t))
                tt(tmp, ps[:, 4, :], ld, ALU.subtract).then_inc(fd.sem, fd.step("lm"))
                tt(rh, r[b], eL, ALU.mult)
                tt(be, sq, enL, ALU.mult)
                tt(ka, km, enL, ALU.mult)
                tt(bE, sq, eS, ALU.mult)
                tt(kE, km, eS, ALU.mult)
                ve.drain()
                ve.wait_ge(fa.sem, fa.at("lmexp", t))
                tt(al, kk, eLm, ALU.mult).then_inc(fd.sem, fd.step("scaled"))

            def variance(t):
                ve.drain()
                ve.tensor_reduce(gn[:, 0, :], y[:, :, :], AX, ALU.add)
                ve.drain()
                ve.tensor_scalar(gn[:, 0, :], gn[:, 0, :], 1.0 / RD, None, ALU.mult)
                ve.drain()
                tt(y[:, :, :], y[:, :, :], bcast(gn[:, 0, :], RD), ALU.subtract)
                ve.drain()
                tt(h8(sqy[:, :]), y[:, :, :], y[:, :, :], ALU.mult)
                ve.drain()
                ve.tensor_reduce(gn[:, 1, :], h8(sqy[:, :]), AX, ALU.add)
                ve.drain()
                ve.tensor_scalar(gn[:, 2, :], gn[:, 1, :], 1.0 / RD, GN_EPS, ALU.mult, ALU.add)\
                    .then_inc(nd.sem, nd.step("var"))

            def output(t):
                ve.drain()
                ve.wait_ge(na.sem, na.at("root", t))
                ve.reciprocal(gn[:, 0, :], gn[:, 3, :])
                ve.drain()
                tt(y[:, :, :], y[:, :, :], bcast(gn[:, 0, :], RD), ALU.mult)
                ve.drain()
                ve.wait_ge(pool.sem, pool.at("bonus", t))
                tt(y[:, :, :], y[:, :, :], h8(lg), ALU.mult)
                ve.drain()
                ve.wait_ge(o_st, 16 * t + 16)
                tt(yo[:, :, :], y[:, :, :], h8(bg), ALU.add).then_inc(nd.sem, nd.step("out"))

            def masks_of(t):
                for q in groups:
                    ve.drain()
                    ve.wait_ge(pe.sem, pe.at(f"scores_{q}", t))
                    tt(M1[q][:, :, :], pg(4 * q), m4("m16"), ALU.mult)
                    tt(N1[q][:, :, :], pg(4 * q + 1), m4("n16"), ALU.mult)
                    tt(Km[q][:, :, :], pg(4 * q + 2), m4("strict"), ALU.mult)
                    tt(N32[q][:, :, :], pg(4 * q + 1), m4("n32"), ALU.mult)
                    tt(N64[q][:, :, :], pg(4 * q + 1), m4("n64"), ALU.mult).then_inc(dve.sem, dve.step(f"masked_{q}"))
                for q in groups:
                    ve.drain()
                    tt(QB[q][:, :, :], pg(4 * q + 3), m4("incl"), ALU.mult)
                    tt(X[q][:, :, :], M1[q][:, :, :], m4("ident"), ALU.add)
                    tt(XT[q][:, :, :], N1[q][:, :, :], m4("ident"), ALU.add).then_inc(dve.sem, dve.step(f"x1_{q}"))
                for q in groups:
                    ve.wait_ge(pe.sem, pe.at(f"qk_{q}", t))
                    ve.tensor_copy(aKV[q][:, :, 1, :], pg(4 * q + 2, 64))
                    tt(QK[q][:, :, :], pg(4 * q + 3), m4("incl"), ALU.mult).then_inc(dve.sem, dve.step(f"p2_{q}"))

            def grow(t, stage):
                for q in groups:
                    ve.drain()
                    ve.wait_ge(pe.sem, pe.at(f"{stage}_{q}", t))
                    ins = tt(X[q][:, :, :], X[q][:, :, :], pg(4 * q), ALU.add)
                    if stage != "x64":
                        ins = tt(XT[q][:, :, :], XT[q][:, :, :], pg(4 * q + 1), ALU.add)
                    ins.then_inc(dve.sem, dve.step(f"{stage}_{q}"))

            def body(t, b, n):
                more = not last(t)
                ve.drain()
                ve.wait_ge(pe.sem, pe.at("turned", t))
                ve.tensor_copy(beT[:, :, :], pg(2))
                ve.tensor_copy(kaT[:, :, :], pg(3)).then_inc(dve.sem, dve.step("bkT"))
                if not first(t):
                    variance(t - 1)
                masks_of(t)
                if not first(t):
                    output(t - 1)
                ve.drain()
                ve.wait_ge(pool.sem, pool.at("rk", t))
                ve.tensor_reduce(bsum[:, :], h8(bon), AX, ALU.add).then_inc(dve.sem, dve.step("bsum"))
                grow(t, "x2")
                if more:
                    shifted(t + 1, 1 - b)
                grow(t, "x4")
                if more:
                    direction(1 - b)
                grow(t, "x8")
                if more:
                    lora_turned(t + 1)
                    lora_out(t + 1)
                grow(t, "x32")
                grow(t, "x64")
                if more:
                    decays(t + 1, 1 - b)
                for q in groups:
                    hs = slice(q, RH, 2)
                    half = lambda c, at: ps[0:64, 4 * q + 2 + c, at:at + 256].rearrange("p (h c) -> p h c", c=64)
                    ve.drain()
                    ve.wait_ge(pool.sem, pool.at("diag", t))
                    ve.wait_ge(pe.sem, pe.at(f"eh_{q}", t))
                    for c in range(2):
                        tt(HT[:, hs, c, :], HT[:, hs, c, :], half(c, 0), ALU.add)
                    for c in range(2):
                        ins = ve.tensor_copy(J[:, hs, c, :], half(c, 256))
                    ins.then_inc(dve.sem, dve.step(f"eh_{q}"))
                for c in range(2):
                    ve.drain()
                    ve.wait_ge(pe.sem, pe.at(f"y{c}", t))
                    tt(S[:, :, :], J[:, :, c, :], ps[0:64, 7, :].rearrange("p (h c) -> p h c", c=64), ALU.add)\
                        .then_inc(dve.sem, dve.step(f"s{c}"))
                tt(y[:, :, :], F[:, :, :], ps[:, 6, :].rearrange("p (h c) -> p h c", c=64), ALU.add)
                if more:
                    scale(t + 1, 1 - b)

            m4 = lambda n: over(M[n], 4)
            ve.memset(S[:, :, :], 0.0)
            ve.drain()
            ve.wait_ge(const_in, 16 * 13)
            for c in (fd, dve, nd):
                c.begin(ve)
            shifted(0, 0)
            direction(0)
            lora_turned(0)
            lora_out(0)
            decays(0, 0)
            scale(0, 0)
            each_tile(ve, body)
            variance(NT - 1)
            output(NT - 1)

        @blk.tensor
        def _(te):
            I = M["ident"]
            hd = lambda z, h: z[:, h * RD:(h + 1) * RD]
            def lora_turn(t, b):
                te.wait_ge(fa.sem, fa.at("lora_in", t))
                te.transpose(ps[:, 3, 2 * P:3 * P], lo[:, 1, :], I)
                te.transpose(ps[0:64, 3, 0:P], lo[:, 0, 0:64], I)
                te.transpose(ps[0:64, 3, P:2 * P], xa[b], I).then_inc(fp.sem, fp.step("lora_t"))

            def lora_decays(t):
                te.wait_ge(fd.sem, fd.at("loT", t))
                te.sem_inc(passed, 1)
                te.matmul(ps[:, 7, :], loT[0:64, 0, :], w2[:, :], start=True, stop=True)
                te.matmul(ps[:, 3, :], loT[0:64, 1, :], a2[:, :], start=True, stop=True).then_inc(fp.sem, fp.step("lora_wa"))

            def lora_gate(t):
                te.wait_ge(fd.sem, fd.at("lora", t))
                te.matmul(ps[:, 7, :], loT[:, 2, :], g2[:, :], start=True, stop=True).then_inc(fp.sem, fp.step("lora_g"))

            def sums(t):
                te.wait_ge(fd.sem, fd.at("ld", t))
                te.matmul(ps[:, 4, :], M["cum"], ld, start=True, stop=True)
                te.matmul(ps[:, 5, :], M["suf"], ld, start=True, stop=True)
                for h in range(RH):
                    mm = te.matmul(ps[0:64, 3, 2 * h:2 * h + 2], hd(ld, h), ind[:, :], start=True, stop=True)
                mm.then_inc(fp.sem, fp.step("sums"))

            def body(t, b, n):
                te.wait_ge(fd.sem, fd.at("scaled", t))
                for bank, z in enumerate((al, rh, be, ka)):
                    for j in range(4):
                        mm = te.transpose(ps[:, bank, j * P:(j + 1) * P], z[:, j * P:(j + 1) * P], I)
                mm.then_inc(pe.sem, pe.step("turned"))
                te.wait_ge(act.sem, act.at("arT", t))
                te.wait_ge(dve.sem, dve.at("bkT", t))

                def four(q, bank, lhsT, rhs, n=P):
                    for i in range(4):
                        mm = te.matmul(ps[:, 4 * q + bank, i * n:(i + 1) * n], lhsT[q][:, i, :], rhs(q, i),
                                       start=True, stop=True)
                    return mm

                of = lambda z: lambda q, i: z[q][:, i, :]
                for q in groups:
                    o = slice(64 * q, 64 * q + 64)
                    for i in range(4):
                        for bank, lhsT, rhs in ((0, beT[o, i, :], arT[o, i, 0, :]), (1, arT[o, i, 0, :], beT[o, i, :]),
                                             (2, kaT[o, i, :], arT[o, i, 0, :]), (3, beT[o, i, :], arT[o, i, 1, :])):
                            mm = te.matmul(ps[:, 4 * q + bank, i * P:(i + 1) * P], lhsT, rhs, start=True, stop=True)
                    mm.then_inc(pe.sem, pe.step(f"scores_{q}"))
                for q in groups:
                    te.wait_ge(dve.sem, dve.at(f"masked_{q}", t))
                    four(q, 0, N1, of(M1))
                    four(q, 1, M1, of(N1))
                    four(q, 2, Km, lambda q, i: hd(v[b], 2 * i + q), 64).then_inc(pe.sem, pe.step(f"p2_{q}"))
                for q in groups:
                    o = slice(64 * q, 64 * q + 64)
                    te.wait_ge(dve.sem, dve.at(f"x1_{q}", t))
                    te.sem_inc(passed, 1)
                    for i in range(4):
                        mm = te.matmul(ps[:, 4 * q + 3, i * P:(i + 1) * P], kaT[o, i, :], arT[o, i, 1, :],
                                       start=True, stop=True)
                    mm.then_inc(pe.sem, pe.step(f"qk_{q}"))
                for q in groups:
                    te.wait_ge(act.sem, act.at(f"p2_{q}", t))
                    te.wait_ge(dve.sem, dve.at(f"p2_{q}", t))
                    four(q, 0, XT, of(M2))
                    four(q, 1, M2, of(XT))
                    four(q, 2, N2, of(M2))
                    four(q, 3, M2, of(N2)).then_inc(pe.sem, pe.step(f"x2_{q}"))
                for q in groups:
                    te.wait_ge(act.sem, act.at(f"x2_{q}", t))
                    te.wait_ge(dve.sem, dve.at(f"x2_{q}", t))
                    four(q, 0, XT, of(M4))
                    four(q, 1, M4, of(XT))
                    four(q, 2, N4, of(M4)).then_inc(pe.sem, pe.step(f"x4_{q}"))
                for q in groups:
                    te.wait_ge(act.sem, act.at(f"x4_{q}", t))
                    te.wait_ge(dve.sem, dve.at(f"x4_{q}", t))
                    four(q, 0, XT, of(M8))
                    four(q, 1, M8, of(XT)).then_inc(pe.sem, pe.step(f"x8_{q}"))
                if not last(t):
                    lora_turn(t + 1, 1 - b)
                before = "x8"
                for n, off in ((32, N32), (64, N64)):
                    for q in groups:
                        te.wait_ge(dve.sem, dve.at(f"{before}_{q}", t))
                        four(q, 2, off, of(X)).then_inc(pe.sem, pe.step(f"z{n}_{q}"))
                    if n == 32 and not last(t):
                        lora_decays(t + 1)
                    for q in groups:
                        te.wait_ge(act.sem, act.at(f"z{n}_{q}", t))
                        mm = four(q, 0, XT, of(Z))
                        if n == 32:
                            mm = four(q, 1, Z, of(XT))
                        mm.then_inc(pe.sem, pe.step(f"x{n}_{q}"))
                    if n == 32 and not last(t):
                        lora_gate(t + 1)
                    before = f"x{n}"
                te.wait_ge(pool.sem, pool.at("alpha", t))
                for q in groups:
                    te.wait_ge(dve.sem, dve.at(f"x64_{q}", t))
                    four(q, 1, X, lambda q, i: aKV[q][:, i, :, :].rearrange("p a c -> p (a c)"))\
                        .then_inc(pe.sem, pe.step(f"ag_{q}"))
                for q in groups:
                    if q and not last(t):
                        te.wait_ge(fa.sem, fa.at("gate", t + 1))
                    te.wait_ge(act.sem, act.at(f"ag_{q}", t))
                    for i in range(4):
                        h = 2 * i + q
                        e = ps[0:64, 4 * q, i * P:(i + 1) * P]
                        te.matmul(e, hd(rh, h), I, start=True, stop=False)
                        te.matmul(e, AG[q][:, i, 0, :], QB[q][:, i, :], start=False, stop=True)
                        f = ps[:, 4 * q + 1, i * 64:(i + 1) * 64]
                        te.matmul(f, QK[q][:, i, :], hd(v[b], h), start=True, stop=False)
                        te.matmul(f, QB[q][:, i, :], AG[q][:, i, 1, :], start=False, stop=True)
                        for c in range(2):
                            o, n, bank = slice(64 * c, 64 * c + 64), 64 * i, 4 * q + 2 + c
                            te.matmul(ps[0:64, bank, n:n + 64], AG[q][o, i, 0, :], hd(bE, h)[o, :], start=True, stop=True)
                            n += 256
                            te.matmul(ps[0:64, bank, n:n + 64], hd(kE, h)[o, :], hd(v[b], h)[o, :], start=True, stop=False)
                            mm = te.matmul(ps[0:64, bank, n:n + 64], hd(bE, h)[o, :], AG[q][o, i, 1, :], start=False, stop=True)
                    mm.then_inc(pe.sem, pe.step(f"eh_{q}"))
                for c in range(2):
                    if c and not last(t):
                        sums(t + 1)
                    te.wait_ge(dve.sem, dve.at("s0" if c else "eh_1", t))
                    te.sem_inc(passed, 1)
                    te.wait_ge(act.sem, act.at("eh_1", t))
                    te.sem_inc(passed, 1)
                    o = slice(64 * c, 64 * c + 64)
                    for h in range(RH):
                        te.matmul(ps[o, 6, h * 64:(h + 1) * 64], ET[:, h, o], S[:, h, :], start=True, stop=True)
                        mm = te.matmul(ps[0:64, 7, h * 64:(h + 1) * 64], HT[:, h, c, :], S[:, h, :], start=True, stop=True)
                    mm.then_inc(pe.sem, pe.step(f"y{c}"))

            te.wait_ge(const_in, 16 * 13)
            for c in (fp, pe):
                c.begin(te)
            lora_turn(0, 0)
            lora_decays(0)
            lora_gate(0)
            sums(0)
            each_tile(te, body)


AH, AD = 4, 64
AV = 2 * AD
LAM_INIT = 0.8 - 0.6 * math.exp(-0.3 * 0)
NEG = -1e30


def rope_consts():
    inv = np.float32(10000.0) ** (-np.arange(0, AD, 2, dtype=np.float32) / np.float32(AD))
    ang = np.arange(SEQ, dtype=np.float32)[:, None] * inv[None, :].astype(np.float32)
    c, s = np.cos(ang), np.sin(ang)
    return np.concatenate([c, c, -s, s], axis=1).astype(np.float32)


def attention(nc, proj, col, out, g):
    with Phase(nc, "att") as ph:
        ident = ph.sb("ident", [P, P])
        causal = ph.sb("causal", [P, P])
        gains = ph.sb("gains", [P, 2, AD])
        subw = ph.sb("subw", [P, AV])
        lq = ph.sb("lq", [P, 4, AD])
        lam = ph.sb("lam", [P, 8])
        rope = ph.sb("rope", [P, NT, 2, AD])
        rg = ph.sb("rg", [P, NT, 2, 2, AD])
        pair = range(2)
        two = lambda n, shape: [ph.sb(f"{n}{b}", shape) for b in pair]
        qk = two("qk", [P, 16, AD])
        sq = two("sq", [P, 16, AD])
        n16 = two("n16", [P, 4, 16])
        qkT = ph.sb("qkT", [P, 2, AH, SEQ])
        qh = two("qh", [P, SEQ])
        kh = two("kh", [P, SEQ])
        vh = two("vh", [P, NT, AV])
        e = [two(f"e{c}_", [P, SEQ]) for c in range(2)]
        at = two("at", [P, SEQ])
        aT = two("aT", [P, SEQ])
        mx = two("mx", [P, 2, 2])
        sm = two("sm", [P, 2])
        rs = two("rs", [P, 3])
        o = two("o", [P, NT, AV])
        o2 = ph.sb("o2", [P, NT, AV])
        on = two("on", [P, NT, AV])
        n8 = ph.sb("n8", [P, 4, NT])
        ps = ph.psum()
        const_in, passed = ph.sem("const_in"), ph.sem("passed")
        x_in = [ph.sem(f"x_in{b}") for b in pair]
        h_in = [ph.sem(f"h_in{b}") for b in pair]
        o_st = ph.sem("o_st")
        lams = ph.marks("lam", "dots exps")
        tab = ph.marks("tab", "gains")
        pa = ph.steps("prep_act", "root_0 root_1 qkT_0 qkT_1")
        pd = ph.steps("prep_dve", "mean_0 mean_1 roped_0 roped_1")
        pp = ph.steps("prep_pe", "turned_0 turned_1")
        N = 2 * NT
        act = ph.steps("act", " ".join(f"exp{s}_0 exp{s}_1 aT{s - 1}" if s else "exp0_0 exp0_1" for s in range(N))
                       + f" aT{N - 1} root_0 root_1")
        dve = ph.steps("dve", "max0_0 max0_1 " + " ".join(
            f"attn{s}" + (f" max{s + 1}_0 max{s + 1}_1" if s < N - 1 else "") + (f" o{s - 1}" if s else "") for s in range(N))
            + f" o{N - 1} mean_0 mean_1 out_0 out_1")
        pe = ph.steps("pe", "scores0_0 scores0_1 " + " ".join(
            (f"scores{s + 1}_0 scores{s + 1}_1 " if s < N - 1 else "") + (f"o{s - 1} " if s else "") + f"turned{s}"
            for s in range(N)) + f" o{N - 1}")
        blk = ph.block()
        width = lambda i: (i % NT + 1) * P
        row = lambda b: banks(ps, b)
        SC = AD ** -0.5

        @blk.sync
        def _(sp):
            for dst, src in ((ident[:, :], g["ident"]), (causal[:, :], g["causal"]),
                             (rope[:, :, :, :].rearrange("p t a d -> p t (a d)"), g["rope"].rearrange("(t p) c -> p t c", p=P)),
                             (gains[:, 0, :], g["q_norm"].partition_broadcast(P)),
                             (gains[:, 1, :], g["k_norm"].partition_broadcast(P)),
                             (subw[:, :], g["subln_w"].partition_broadcast(P)),
                             (lq[:, 0, :], g["lambda_q1"].partition_broadcast(P)),
                             (lq[:, 1, :], g["lambda_q2"].partition_broadcast(P)),
                             (lq[:, 2, :], g["lambda_k1"].partition_broadcast(P)),
                             (lq[:, 3, :], g["lambda_k2"].partition_broadcast(P))):
                sp.dma_start(dst, src).then_inc(const_in, 16)
            def load(t, b):
                sp.dma_start(qk[b][:, :, :].rearrange("p g d -> p (g d)"), proj[bass.ds(t * P, P), col:col + 1024])\
                    .then_inc(x_in[b], 16)

            for b in pair:
                load(b, b)
            with sp.Fori(0, NT // 2 - 1) as j:
                for b in pair:
                    sp.wait_ge(pp.sem, pp.at(f"turned_{b}", j))
                    sp.sem_inc(passed, 1)
                    load(2 * j + 2 + b, b)
            sp.wait_ge(pa.sem, pa.start(NT // 2))

            def load_head(h):
                sp.dma_start(qh[h % 2][:, :], qkT[:, 0, h:h + 1, :]).then_inc(h_in[h % 2], 16)
                sp.dma_start(kh[h % 2][:, :], qkT[:, 1, h:h + 1, :]).then_inc(h_in[h % 2], 16)
                sp.dma_start(vh[h % 2][:, :, :], proj[:, h * AV + col + 1024:(h + 1) * AV + col + 1024]
                             .rearrange("(t p) d -> p t d", p=P)).then_inc(h_in[h % 2], 16)

            for h in range(2):
                load_head(h)
            for h in range(AH):
                if h + 2 < AH:
                    sp.wait_ge(pe.sem, pe.at(f"o{NT * (h % 2 + 1) - 1}", h // 2))
                    load_head(h + 2)
            sp.wait_ge(o_st, 16 * (AH + 1))

        @blk.gpsimd
        def _(po):
            po.wait_ge(const_in, 160)
            for a in range(2):
                po.tensor_tensor(rg[:, :, a, 0, :], rope[:, :, 0, :], over(gains[:, a, :], NT), ALU.mult)
                for lo, hi in ((slice(0, 32), slice(32, 64)), (slice(32, 64), slice(0, 32))):
                    last = po.tensor_tensor(rg[:, :, a, 1, lo], rope[:, :, 1, lo], over(gains[:, a, hi], NT), ALU.mult)
            last.then_inc(tab.sem, tab.step("gains"))

        @blk.scalar
        def _(s):
            s.wait_ge(lams.sem, 1)
            s.activation(lam[:, 2:4], lam[:, 0:2], ACT.Exp).then_inc(lams.sem, lams.step("dots"))
            pa.begin(s)
            with s.Fori(0, NT // 2) as j:
                for b in pair:
                    s.wait_ge(pd.sem, pd.at(f"mean_{b}", j))
                    s.activation(n16[b][:, 1, :], n16[b][:, 0, :], ACT.Sqrt).then_inc(pa.sem, pa.step(f"root_{b}"))
                for b in pair:
                    s.wait_ge(pp.sem, pp.at(f"turned_{b}", j))
                    s.activation(qkT[:, :, :, bass.ds((2 * j + b) * P, P)].rearrange("p a h c -> p (a h) c"),
                                 ps[:, 2 * b:2 * b + 2, :].rearrange("p b (h c) -> p (b h) c", c=P), ACT.Copy)\
                        .then_inc(pa.sem, pa.step(f"qkT_{b}"))
            act.begin(s)
            s.sem_inc(o_st, 16)

            def turn(i):
                s.wait_ge(pe.sem, pe.at(f"turned{i}", j))
                s.activation(aT[i % 2][:, 0:width(i)], row(4)[:, 0:width(i)], ACT.Copy).then_inc(act.sem, act.step(f"aT{i}"))

            with s.Fori(0, AH // 2) as j:
                for i in range(N):
                    for c in range(2):
                        s.wait_ge(dve.sem, dve.at(f"max{i}_{c}", j))
                        s.activation(e[c][i % 2][:, 0:width(i)], row(2 * c)[:, 0:width(i)], ACT.Exp,
                                     bias=mx[i % 2][:, 1, c:c + 1], scale=SC, accum_out=sm[i % 2][:, c:c + 1])\
                            .then_inc(act.sem, act.step(f"exp{i}_{c}"))
                    if i:
                        turn(i - 1)
                turn(N - 1)
                for b in pair:
                    s.wait_ge(dve.sem, dve.at(f"mean_{b}", j))
                    s.activation(n8[:, 2 * b + 1, :], n8[:, 2 * b, :], ACT.Sqrt).then_inc(act.sem, act.step(f"root_{b}"))
                for b in pair:
                    s.wait_ge(dve.sem, dve.at(f"out_{b}", j))
                    s.sem_inc(passed, 1)
                    s.dma_start(out[:, bass.ds((2 * j + b) * AV, AV)].rearrange("(t p) d -> p t d", p=P),
                                on[b][:, :, :]).then_inc(o_st, 16)

        @blk.vector
        def _(ve):
            tt = ve.tensor_tensor
            ve.wait_ge(const_in, 160)
            tt(lq[:, 0:2, :], lq[:, 0:2, :], lq[:, 2:4, :], ALU.mult)
            ve.drain()
            ve.tensor_reduce(lam[:, 0:2], lq[:, 0:2, :], AX, ALU.add).then_inc(lams.sem, 1)
            ve.drain()
            ve.wait_ge(lams.sem, 2)
            tt(lam[:, 4:5], lam[:, 3:4], lam[:, 2:3], ALU.subtract)
            ve.drain()
            ve.tensor_scalar(lam[:, 5:6], lam[:, 4:5], LAM_INIT, None, ALU.subtract)
            ve.drain()
            ve.wait_ge(tab.sem, 1)
            pd.begin(ve)
            with ve.Fori(0, NT // 2) as j:
                for b in pair:
                    ve.drain()
                    ve.wait_ge(x_in[b], 16 * j + 16)
                    tt(sq[b][:, :, :], qk[b][:, :, :], qk[b][:, :, :], ALU.mult)
                    ve.drain()
                    ve.tensor_reduce(n16[b][:, 2, :], sq[b][:, :, :], AX, ALU.add)
                    ve.drain()
                    ve.tensor_scalar(n16[b][:, 0, :], n16[b][:, 2, :], 1.0 / AD, EPS, ALU.mult, ALU.add)\
                        .then_inc(pd.sem, pd.step(f"mean_{b}"))
                for b in pair:
                    q, s2 = qk[b], sq[b]
                    ve.drain()
                    ve.wait_ge(pa.sem, pa.at(f"root_{b}", j))
                    ve.reciprocal(n16[b][:, 3, :], n16[b][:, 1, :])
                    ve.drain()
                    tt(q[:, :, :], q[:, :, :], bcast(n16[b][:, 3, :], AD), ALU.mult)
                    ve.drain()
                    table = rg[:, bass.ds(2 * j + b, 1), :, :, :].rearrange("p o a c d -> p (o a) c d")
                    for a in range(2):
                        part, cs, sn = slice(8 * a, 8 * a + 8), table[:, a, 0, :], table[:, a, 1, :]
                        tt(s2[:, part, 0:32], q[:, part, 32:64], over(sn[:, 0:32], 8), ALU.mult)
                        tt(s2[:, part, 32:64], q[:, part, 0:32], over(sn[:, 32:64], 8), ALU.mult)
                    ve.drain()
                    for a in range(2):
                        part, cs = slice(8 * a, 8 * a + 8), table[:, a, 0, :]
                        tt(q[:, part, :], q[:, part, :], over(cs, 8), ALU.mult)
                    ve.drain()
                    tt(q[:, :, :], q[:, :, :], s2[:, :, :], ALU.add).then_inc(pd.sem, pd.step(f"roped_{b}"))

            def largest(i):
                W = width(i)
                for c in range(2):
                    ve.drain()
                    ve.wait_ge(pe.sem, pe.at(f"scores{i}_{c}", j))
                    sc = row(2 * c)
                    tt(sc[:, W - P:W], sc[:, W - P:W], causal[:, :], ALU.add)
                    ve.drain()
                    ve.tensor_reduce(mx[i % 2][:, 0, c:c + 1], sc[:, 0:W], AX, ALU.max)
                    ve.drain()
                    ve.tensor_scalar(mx[i % 2][:, 1, c:c + 1], mx[i % 2][:, 0, c:c + 1], -SC, None, ALU.mult)\
                        .then_inc(dve.sem, dve.step(f"max{i}_{c}"))

            def output(i):
                ve.drain()
                ve.wait_ge(pe.sem, pe.at(f"o{i}", j))
                ve.tensor_scalar(o[i // NT][:, i % NT, :], ps[:, 6 + i % 2, 0:AV], rs[i % 2][:, 0:1], None, ALU.mult)\
                    .then_inc(dve.sem, dve.step(f"o{i}"))

            dve.begin(ve)
            with ve.Fori(0, AH // 2) as j:
                largest(0)
                for i in range(N):
                    W, b = width(i), i % 2
                    ve.drain()
                    ve.wait_ge(act.sem, act.at(f"exp{i}_1", j))
                    ve.reciprocal(rs[b][:, 0:2], sm[b][:, :])
                    ve.drain()
                    ve.scalar_tensor_tensor(rs[b][:, 2:3], rs[b][:, 1:2], sm[b][:, 0:1], lam[:, 5:6], ALU.mult, ALU.mult)
                    ve.drain()
                    ve.scalar_tensor_tensor(at[b][:, 0:W], e[1][b][:, 0:W], rs[b][:, 2:3], e[0][b][:, 0:W], ALU.mult, ALU.add)\
                        .then_inc(dve.sem, dve.step(f"attn{i}"))
                    if i + 1 < N:
                        largest(i + 1)
                    if i:
                        output(i - 1)
                output(N - 1)
                for b in pair:
                    ve.drain()
                    tt(o2[:, :, :], o[b][:, :, :], o[b][:, :, :], ALU.mult)
                    ve.drain()
                    ve.tensor_reduce(n8[:, 2 * b + 1, :], o2[:, :, :], AX, ALU.add)
                    ve.drain()
                    ve.tensor_scalar(n8[:, 2 * b, :], n8[:, 2 * b + 1, :], 1.0 / AV, EPS, ALU.mult, ALU.add)\
                        .then_inc(dve.sem, dve.step(f"mean_{b}"))
                for b in pair:
                    ve.drain()
                    ve.wait_ge(act.sem, act.at(f"root_{b}", j))
                    ve.reciprocal(n8[:, 2 * b, :], n8[:, 2 * b + 1, :])
                    ve.drain()
                    ve.tensor_scalar(n8[:, 2 * b + 1, :], n8[:, 2 * b, :], 1.0 - LAM_INIT, None, ALU.mult)
                    ve.drain()
                    tt(o2[:, :, :], o[b][:, :, :], bcast(n8[:, 2 * b + 1, :], AV), ALU.mult)
                    ve.drain()
                    ve.wait_ge(o_st, 32 * j + 16)
                    tt(on[b][:, :, :], o2[:, :, :], over(subw[:, :], NT), ALU.mult).then_inc(dve.sem, dve.step(f"out_{b}"))

        @blk.tensor
        def _(te):
            te.wait_ge(const_in, 160)
            pp.begin(te)
            with te.Fori(0, NT // 2) as j:
                for b in pair:
                    te.wait_ge(pd.sem, pd.at(f"roped_{b}", j))
                    te.wait_ge(pa.sem, pa.start(j))
                    for t in range(8):
                        mm = te.transpose(block_of(ps, 2 * b, t), qk[b][:, 2 * t:2 * t + 2, :].rearrange("p a d -> p (a d)"),
                                          ident[:, :])
                    mm.then_inc(pp.sem, pp.step(f"turned_{b}"))
            te.wait_ge(pa.sem, pa.start(NT // 2))

            def scores(i):
                b, at_q = i // NT, (i % NT) * P
                if i % NT == 0:
                    te.wait_ge(h_in[b], 48 * j + 48)
                for c in range(2):
                    half = slice(64 * c, 64 * c + 64)
                    if i:
                        te.wait_ge(act.sem, act.at(f"exp{i - 1}_{c}", j))
                    for n in range(0, width(i), 512):
                        m = min(512, width(i) - n)
                        mm = te.matmul(ps[:, 2 * c + n // 512, 0:m], qh[b][half, at_q:at_q + P], kh[b][half, n:n + m],
                                       start=True, stop=True)
                    mm.then_inc(pe.sem, pe.step(f"scores{i}_{c}"))

            def output(i):
                te.wait_ge(act.sem, act.at(f"aT{i}", j))
                if i > 1:
                    te.wait_ge(dve.sem, dve.at(f"o{i - 2}", j))
                last = i % NT
                for k in range(last + 1):
                    mm = te.matmul(ps[:, 6 + i % 2, 0:AV], aT[i % 2][:, k * P:(k + 1) * P], vh[i // NT][:, k, :],
                                   start=(k == 0), stop=(k == last))
                mm.then_inc(pe.sem, pe.step(f"o{i}"))

            pe.begin(te)
            with te.Fori(0, AH // 2) as j:
                te.wait_ge(act.sem, act.start(j))
                te.sem_inc(passed, 1)
                te.wait_ge(dve.sem, dve.start(j))
                te.sem_inc(passed, 1)
                scores(0)
                for i in range(N):
                    if i + 1 < N:
                        scores(i + 1)
                    if i:
                        output(i - 1)
                    te.wait_ge(dve.sem, dve.at(f"attn{i}", j))
                    for k in range(i % NT + 1):
                        mm = te.transpose(block_of(ps, 4, k), at[i % 2][:, k * P:(k + 1) * P], ident[:, :])
                    mm.then_inc(pe.sem, pe.step(f"turned{i}"))
                output(N - 1)


SH, SP_, SG, SN = 16, 64, 2, 128
SW = SH * SP_
XBC = SW + 2 * SG * SN
NX = XBC // P
TAPS = 4
COL_Z, COL_XBC, COL_DT = 0, SW, SW + XBC
COL_Q = COL_DT + SH
COL_F, COL_I, COL_G = COL_Q + 512, COL_Q + 1024, COL_Q + 1536
COL_U, COL_SG = COL_Q + 2048, COL_Q + 2560


def ssd_masks():
    s, l = np.arange(P)[:, None], np.arange(P)[None, :]
    m = [s == l, s <= l, (s == P - 1) & (l >= 0)]
    sel = np.zeros((P, SH * P), np.float32)
    for h in range(SH):
        sel[h, h * P:(h + 1) * P] = 1
    return np.concatenate([a.astype(np.float32) for a in m] + [sel], axis=1)


def ssd(nc, proj, out, masks_d, g):
    HG = SH // SG
    NB = 10
    with Phase(nc, "ssd") as ph:
        two = lambda n, shape: [ph.sb(f"{n}{b}", shape) for b in range(2)]
        masks = ph.sb("masks", [P, (3 + SH) * P])
        ident, cum, last_row = (masks[:, i * P:(i + 1) * P] for i in range(3))
        sel = masks[0:SH, 3 * P:]
        cw = ph.sb("cw", [P, TAPS, NX])
        cb = ph.sb("cb", [P, NX])
        rows = ph.sb("rows", [P, 3, SH])
        nw = ph.sb("nw", [P, SW])
        dt = ph.sb("dt", [P, NT, SH])
        w8 = ph.sb("w8", [P, 8, NT * SH])
        acum = ph.sb("acum", [P, NT, SH])
        eac = ph.sb("eac", [P, NT, SH])
        dte = ph.sb("dte", [P, NT, SH])
        cdec = ph.sb("cdec", [P, NT, SH])
        aT = ph.sb("aT", [SH, SEQ])
        z = ph.sb("z", [P, NT, SW])
        xbc = ph.sb("xbc", [P, NT, XBC])
        xF = two("xF", [P, 3 + SEQ])
        cF = two("cF", [P, SEQ])
        sF = two("sF", [P, SEQ])
        BC = ph.sb("BC", [P, 4, SEQ])
        cur = two("cur", [P, 4, P])
        Bt = two("Bt", [P, SG, SN])
        a1 = ph.sb("a1", [P, SH])
        seg = two("seg", [P, HG, P])
        sm = two("sm", [P, P])
        xdt = two("xdt", [P, SH, SP_])
        xdd = two("xdd", [P, SH, SP_])
        xd = two("xd", [P, SH, SP_])
        S = ph.sb("S", [P, SH, SP_])
        y = two("y", [P, HG, SP_])
        junk = ph.sb("junk", [P, HG * SP_])
        ss = ph.sb("ss", [P, 4, NT * SG])
        ps = ph.psum()
        const_in, x_in, z_in, y_st, passed = (ph.sem(n) for n in ("const_in", "x_in", "z_in", "y_st", "passed"))
        pre_d = ph.marks("pre_dve", "biased dta acum diffs")
        pre_a = ph.marks("pre_act", "exps cum")
        pre_p = ph.marks("pre_pe", "acum last aT")
        turned, held, tap, conv, silu, back, put = (ph.count(n) for n in (
            "turned", "held", "tap", "conv", "silu", "back", "put"))
        zeroed, gated = ph.sem("zeroed"), ph.sem("gated")
        prepared = ph.count("prepared")
        rowed, seged, decayed, masked, summed, stated, outed, gates, squared = (
            [ph.count(f"{n}{q}") for q in range(SG)]
            for n in ("rowed", "seged", "decayed", "masked", "summed", "stated", "outed", "gates", "squared"))
        mean, root, inverse, normed = (ph.sem(n) for n in ("mean", "root", "inverse", "normed"))
        blk = ph.block()
        groups = range(SG)
        heads = lambda q: slice(HG * q, HG * q + HG)
        cols = lambda q: slice(HG * SP_ * q, HG * SP_ * (q + 1))

        def pairs_of_tiles(eng, body):
            with eng.Fori(0, NT // 2) as j:
                for b in range(2):
                    body(2 * j + b, b)

        @blk.sync
        def _(sp):
            for dst, src in ((masks[:, :], masks_d),
                             (cw[:, :, :], g["ssd_conv_w_2"].rearrange("j (k p) -> p j k", p=P)),
                             (cb[:, :], g["ssd_conv_b_2"].rearrange("(k p) -> p k", p=P)),
                             (rows[:, 0, :], g["ssd_dt_bias_2"].partition_broadcast(P)),
                             (rows[:, 1, :], g["ssd_a_log_2"].partition_broadcast(P)),
                             (rows[:, 2, :], g["ssd_d_2"].partition_broadcast(P)),
                             (nw[:, :], g["ssd_norm_w_2"].partition_broadcast(P)),
                             (dt[:, :, :], proj[:, COL_DT:COL_DT + SH].rearrange("(t p) h -> p t h", p=P))):
                sp.dma_start(dst, src, allow_slow_non_contiguous=True).then_inc(const_in, 16)
            sp.dma_start(xbc[:, :, :], proj[:, COL_XBC:COL_XBC + XBC].rearrange("(t p) c -> p t c", p=P)).then_inc(x_in, 16)
            sp.dma_start(z[:, :, :], proj[:, COL_Z:COL_Z + SW].rearrange("(t p) c -> p t c", p=P)).then_inc(z_in, 16)
            for t in range(NT):
                sp.wait_ge(normed, t + 1)
                sp.dma_start(out[t * P:(t + 1) * P, :], z[:, t, :]).then_inc(y_st, 16)
            sp.wait_ge(y_st, 16 * NT)

        @blk.gpsimd
        def _(po):
            tt = po.tensor_tensor
            tap.begin(po)
            for b in range(2):
                last_set = po.memset(xF[b][:, 0:3], 0.0)
            last_set.then_inc(zeroed, 1)
            po.drain()
            po.wait_ge(const_in, 128)
            for k in range(NX):
                po.wait_ge(held.sem, held.done(k))
                po.tensor_scalar(cF[k % 2][:, :], xF[k % 2][:, 0:SEQ], cw[:, 0, k:k + 1], cb[:, k:k + 1],
                                 ALU.mult, ALU.add).then_inc(tap.sem, 1)
            po.drain()
            po.wait_ge(put.sem, put.done(NB - 1))
            po.wait_ge(silu.sem, silu.done(NX - 1))
            prepared.begin(po)

            def prepare(t, b):
                one = bass.ds(t, 1)
                row = lambda s: s[:, one, :].rearrange("p o h -> p (o h)")
                xs = xbc[:, one, 0:SW].rearrange("p o (h d) -> p (o h) d", d=SP_)
                po.drain()
                po.wait_ge(summed[0].sem, summed[0].done(t - 2))
                po.sem_inc(passed, 1)
                po.wait_ge(summed[1].sem, summed[1].done(t - 2))
                po.sem_inc(passed, 1)
                po.tensor_copy(cur[b][:, :, :], BC[:, :, bass.ds(t * P, P)])
                po.tensor_copy(Bt[b][:, :, :].rearrange("p g n -> p (g n)"),
                               xbc[:, one, SW:SW + SG * SN].rearrange("p o c -> p (o c)"))
                tt(xdt[b][:, :, :], xs, bcast(row(dt), SP_), ALU.mult)
                po.drain()
                tt(xdd[b][:, :, :], xdt[b][:, :, :], bcast(row(dte), SP_), ALU.mult)
                po.drain()
                po.wait_ge(outed[1].sem, outed[1].done(t - 2))
                po.sem_inc(passed, 1)
                tt(xd[b][:, :, :], xs, bcast(rows[:, 2, :], SP_), ALU.mult).then_inc(prepared.sem, 1)

            pairs_of_tiles(po, prepare)

        @blk.scalar
        def _(s):
            s.wait_ge(pre_d.sem, 1)
            s.activation(w8[:, 2, :], w8[:, 1, :], ACT.Exp, scale=-1.0)
            s.activation(w8[:, 7, 0:SH], rows[:, 1, :], ACT.Exp).then_inc(pre_a.sem, pre_a.step("exps"))
            s.wait_ge(pre_d.sem, 4)
            s.activation(eac[:, :, :], acum[:, :, :], ACT.Exp)
            s.activation(dte[:, :, :].rearrange("p t h -> p (t h)"), w8[:, 0, :], ACT.Exp)
            s.activation(cdec[:, :, :].rearrange("p t h -> p (t h)"), w8[:, 3, :], ACT.Exp)\
                .then_inc(pre_a.sem, pre_a.step("cum"))

            def hold(k):
                s.wait_ge(turned.sem, turned.done(k))
                s.wait_ge(conv.sem, conv.done(k - 2))
                s.activation(xF[k % 2][:, 3:], banks(ps, 2 * (k % 2)), ACT.Copy).then_inc(held.sem, 1)

            def gate(k):
                s.wait_ge(conv.sem, conv.done(k))
                s.wait_ge(back.sem, back.done(min(k - 2, NB - 1)))
                s.activation(BC[:, k - 8, :] if k >= 8 else sF[k % 2][:, :], cF[k % 2][:, :], ACT.Silu).then_inc(silu.sem, 1)

            def put_back(k):
                s.wait_ge(back.sem, back.done(k))
                s.activation(xbc[:, :, k * P:(k + 1) * P], blocks(ps, 4 + 2 * (k % 2), 8), ACT.Copy).then_inc(put.sem, 1)

            for c in (held, silu, put):
                c.begin(s)
            s.drain()
            s.wait_ge(zeroed, 1)
            for k in range(NX + 2):
                if k < NX:
                    hold(k)
                if 1 <= k <= NX:
                    gate(k - 1)
                if 2 <= k < NB + 2:
                    put_back(k - 2)
            s.wait_ge(z_in, 16)
            for t in range(NT):
                s.activation(z[:, t, :], z[:, t, :], ACT.Silu).then_inc(gated, 1)
            for c in (*decayed, *squared):
                c.begin(s)

            def body(t, b):
                for q in groups:
                    s.wait_ge(seged[q].sem, seged[q].done(t))
                    s.activation(seg[q][:, :, :], seg[q][:, :, :], ACT.Exp).then_inc(decayed[q].sem, 1)
                for q in groups:
                    s.drain()
                    s.wait_ge(gates[q].sem, gates[q].done(t))
                    s.activation(junk[:, :], z[:, bass.ds(t, 1), cols(q)].rearrange("p o c -> p (o c)"), ACT.Square,
                                 accum_out=ss[:, 0, bass.ds(2 * t + q, 1)]).then_inc(squared[q].sem, 1)

            pairs_of_tiles(s, body)
            s.wait_ge(mean, 1)
            s.activation(ss[:, 2, :], ss[:, 1, :], ACT.Sqrt).then_inc(root, 1)

        @blk.vector
        def _(ve):
            tt, ts, stt = ve.tensor_tensor, ve.tensor_scalar, ve.scalar_tensor_tensor
            ve.memset(S[:, :, :], 0.0)
            ve.drain()
            ve.wait_ge(const_in, 128)
            v, av, e, zz, z2, pl, tmp, na = (w8[:, i, :] for i in range(8))
            dtf = dt[:, :, :].rearrange("p t h -> p (t h)")
            tt(v.rearrange("p (t h) -> p t h", h=SH), dt[:, :, :], over(rows[:, 0, :], NT), ALU.add)
            ve.drain()
            stt(av, v, -1.0, v, ALU.mult, ALU.max).then_inc(pre_d.sem, pre_d.step("biased"))
            ve.drain()
            ve.wait_ge(pre_a.sem, 1)
            ts(tmp, e, 2.0, None, ALU.add)
            ve.drain()
            ve.reciprocal(pl, tmp)
            ve.drain()
            tt(zz, e, pl, ALU.mult)
            ve.drain()
            tt(z2, zz, zz, ALU.mult)
            ve.drain()
            ts(pl, z2, 1.0 / 17, 1.0 / 15, ALU.mult, ALU.add)
            for n in (13, 11, 9, 7, 5, 3, 1):
                ve.drain()
                tt(pl, pl, z2, ALU.mult)
                ve.drain()
                ts(pl, pl, 1.0 / n, None, ALU.add)
            ve.drain()
            tt(pl, pl, zz, ALU.mult)
            ts(v, v, 0.0, None, ALU.max)
            ve.drain()
            stt(dtf, pl, 2.0, v, ALU.mult, ALU.add)
            ve.drain()
            tt(tmp.rearrange("p (t h) -> p t h", h=SH), dt[:, :, :], over(na[:, 0:SH], NT), ALU.mult)
            ve.drain()
            ts(tmp, tmp, -1.0, None, ALU.mult).then_inc(pre_d.sem, pre_d.step("dta"))
            ve.drain()
            ve.wait_ge(pre_p.sem, 1)
            acf = acum[:, :, :].rearrange("p t h -> p (t h)")
            ve.tensor_copy(acf, ps[:, 0, 0:P]).then_inc(pre_d.sem, pre_d.step("acum"))
            ve.drain()
            ve.wait_ge(pre_p.sem, 2)
            ve.tensor_copy(zz, ps[:, 1, 0:P])
            ve.drain()
            tt(v, zz, acf, ALU.subtract)
            ve.drain()
            ve.wait_ge(pre_p.sem, 3)
            ve.tensor_copy(aT[:, :], ps[0:SH, 6:8, :].rearrange("p b c -> p (b c)"))
            ts(v, v, 0.0, None, ALU.min).then_inc(pre_d.sem, pre_d.step("diffs"))
            ve.drain()
            ve.wait_ge(pre_a.sem, 2)
            conv.begin(ve)
            for k in range(NX):
                c, x = cF[k % 2], xF[k % 2]
                ve.drain()
                ve.wait_ge(tap.sem, tap.done(k))
                for j in range(1, TAPS):
                    ve.drain()
                    ins = stt(c[:, :], x[:, j:j + SEQ], cw[:, j, k:k + 1], c[:, :], ALU.mult, ALU.add)
                ins.then_inc(conv.sem, 1)
            for c in (*seged, *masked, *stated, *outed, *gates):
                c.begin(ve)
            ve.drain()
            ve.wait_ge(gated, NT)
            h64 = lambda b: ps[:, b, :].rearrange("p (h d) -> p h d", d=SP_)

            def body(t, b):
                one = bass.ds(t, 1)
                row = lambda s, q: s[:, one, heads(q)].rearrange("p o h -> p (o h)")
                ve.drain()
                ve.tensor_copy(a1[:, :], acum[:, one, :].rearrange("p o h -> p (o h)"))
                for q in groups:
                    ve.drain()
                    ve.wait_ge(rowed[q].sem, rowed[q].done(t))
                    for i in range(HG):
                        h = HG * q + i
                        ins = ts(seg[q][:, i, :], block_of(ps, 4 * q, i), a1[:, h:h + 1], 0.0, ALU.subtract, ALU.min)
                    ins.then_inc(seged[q].sem, 1)
                    tt(sm[q][:, :], ps[:, 4 * q + 2, 0:P], cum, ALU.mult)
                for q in groups:
                    ve.drain()
                    ve.wait_ge(decayed[q].sem, decayed[q].done(t))
                    tt(seg[q][:, :, :], seg[q][:, :, :], over(sm[q][:, :], HG), ALU.mult).then_inc(masked[q].sem, 1)
                for q in groups:
                    ve.drain()
                    ve.wait_ge(summed[q].sem, summed[q].done(t))
                    tt(S[:, heads(q), :], S[:, heads(q), :], bcast(row(cdec, q), SP_), ALU.mult)
                    tt(y[q][:, :, :], h64(4 * q + 1), bcast(row(eac, q), SP_), ALU.mult)
                    ve.drain()
                    tt(S[:, heads(q), :], S[:, heads(q), :], h64(4 * q + 3), ALU.add).then_inc(stated[q].sem, 1)
                    tt(y[q][:, :, :], y[q][:, :, :], h64(4 * q), ALU.add)
                    ve.drain()
                    tt(y[q][:, :, :], y[q][:, :, :], xd[b][:, heads(q), :], ALU.add).then_inc(outed[q].sem, 1)
                    ve.drain()
                    zq = z[:, one, cols(q)].rearrange("p o c -> p (o c)")
                    tt(zq, y[q][:, :, :].rearrange("p h d -> p (h d)"), zq, ALU.mult).then_inc(gates[q].sem, 1)

            pairs_of_tiles(ve, body)
            ve.drain()
            ve.wait_ge(squared[0].sem, squared[0].done(NT - 1))
            ve.wait_ge(squared[1].sem, squared[1].done(NT - 1))
            ts(ss[:, 1, :], ss[:, 0, :], 1.0 / 512, EPS, ALU.mult, ALU.add).then_inc(mean, 1)
            ve.drain()
            ve.wait_ge(root, 1)
            ve.reciprocal(ss[:, 3, :], ss[:, 2, :])
            ve.drain()
            for t in range(NT):
                for q in groups:
                    ins = stt(z[:, t, cols(q)], z[:, t, cols(q)], ss[:, 3, 2 * t + q:2 * t + q + 1], nw[:, cols(q)],
                              ALU.mult, ALU.mult)
                ins.then_inc(normed, 1)

        @blk.tensor
        def _(te):
            te.wait_ge(const_in, 128)
            te.wait_ge(pre_d.sem, 2)
            te.matmul(ps[:, 0, 0:P], cum, w8[:, 6, :], start=True, stop=True).then_inc(pre_p.sem, pre_p.step("acum"))
            te.wait_ge(pre_d.sem, 3)
            te.matmul(ps[:, 1, 0:P], last_row, acum[:, :, :].rearrange("p t h -> p (t h)"), start=True, stop=True)\
                .then_inc(pre_p.sem, pre_p.step("last"))
            for t in range(NT):
                mm = te.transpose(ps[0:SH, 6 + t // 4, (t % 4) * P:(t % 4 + 1) * P], acum[:, t, :], ident)
            mm.then_inc(pre_p.sem, pre_p.step("aT"))
            te.wait_ge(pre_d.sem, 4)
            for c in (turned, back):
                c.begin(te)
            te.wait_ge(x_in, 16)
            for k in range(NX + 1):
                if k < NX:
                    te.wait_ge(held.sem, held.done(k - 2))
                    for t in range(NT):
                        mm = te.transpose(block_of(ps, 2 * (k % 2), t), xbc[:, t, k * P:(k + 1) * P], ident)
                    mm.then_inc(turned.sem, 1)
                if 1 <= k <= NB:
                    i = k - 1
                    te.wait_ge(silu.sem, silu.done(i))
                    te.wait_ge(put.sem, put.done(i - 2))
                    src = BC[:, i - 8, :] if i >= 8 else sF[i % 2][:, :]
                    for t in range(NT):
                        mm = te.transpose(block_of(ps, 4 + 2 * (i % 2), t), src[:, t * P:(t + 1) * P], ident)
                    mm.then_inc(back.sem, 1)
            te.wait_ge(put.sem, put.done(NB - 1))
            for c in (*rowed, *summed):
                c.begin(te)

            def body(t, b):
                te.wait_ge(prepared.sem, prepared.done(t))
                te.sem_inc(passed, 1)
                for q in groups:
                    te.wait_ge(outed[q].sem, outed[q].done(t - 1))
                    te.matmul(ps[:, 4 * q + 2, 0:P], cur[b][:, q, :], cur[b][:, 2 + q, :], start=True, stop=True)
                    for i in range(HG):
                        h = HG * q + i
                        mm = te.matmul(block_of(ps, 4 * q, i), sel[:, h * P:(h + 1) * P], aT[:, bass.ds(t * P, P)],
                                       start=True, stop=True)
                    mm.then_inc(rowed[q].sem, 1)
                for q in groups:
                    te.wait_ge(masked[q].sem, masked[q].done(t))
                    te.wait_ge(stated[q].sem, stated[q].done(t - 1))
                    for i in range(HG):
                        te.matmul(ps[:, 4 * q, i * SP_:(i + 1) * SP_], seg[q][:, i, :], xdt[b][:, HG * q + i, :],
                                  start=True, stop=True)
                    te.matmul(ps[:, 4 * q + 1, :], cur[b][:, 2 + q, :], S[:, heads(q), :].rearrange("p h d -> p (h d)"),
                              start=True, stop=True)
                    te.matmul(ps[:, 4 * q + 3, :], Bt[b][:, q, :], xdd[b][:, heads(q), :].rearrange("p h d -> p (h d)"),
                              start=True, stop=True).then_inc(summed[q].sem, 1)

            pairs_of_tiles(te, body)


HH, HD = 4, 128


def hgrn_masks():
    t, l = np.arange(P)[:, None], np.arange(P)[None, :]
    same = lambda n: (t // n) == (l // n)
    b16 = l // 32 * 32 + 16
    lev = same(32) & np.where(l >= b16, (t >= b16) & (t <= l), (t > l) & (t < b16))
    b8 = l // 16 * 16 + 8
    mid = np.where(same(16) & (l >= b8) & (t >= b8) & (t <= l), 1, 0) - np.where(same(16) & (l < b8) & (t > l) & (t < b8), 1, 0)
    cum = same(32) & (t <= l)
    suf = same(32) & (t > l)
    cross = same(32) & ~same(16) & (t < l)
    diag = same(16) & (t <= l)
    return np.concatenate([a.astype(np.float32) for a in (t == l, lev, mid, cum, suf, cross, diag)], axis=1)


def hgrn(nc, proj, out, masks_d, g):
    W = HH * HD
    HW = W // 2
    LIM = 85.0
    with Phase(nc, "hgrn") as ph:
        masks = ph.sb("masks", [P, 7 * P])
        ident, lev, mid, cum, suf, cross, diag = (masks[:, i * P:(i + 1) * P] for i in range(7))
        ind = ph.sb("ind", [P, 4])
        nw = ph.sb("nw", [P, W])
        Q = ph.sb("Q", [P, NT, W])
        LF = ph.sb("LF", [P, NT, W])
        V = ph.sb("V", [P, NT, W])
        G = ph.sb("G", [P, NT, W])
        K = ph.sb("K", [P, NT, W])
        sp0 = ph.sb("sp0", [P, NT, W])
        two = lambda n, shape: [ph.sb(f"{n}{q}", shape) for q in range(2)]
        vc = two("vc", [P, W])
        e1, e2c, e2, e2n = (two(n, [P, HW]) for n in ("e1_", "e2c", "e2_", "e2n"))
        e34 = two("e34_", [P, 2, HW])
        qk = two("qk", [P, 4, HW])
        q3, k4 = two("q3_", [P, HW]), two("k4_", [P, HW])
        T12, T34 = two("T12_", [P, 4, P]), two("T34_", [P, 4, P])
        T5 = two("T5_", [P, 2, P])
        at = two("at", [P, 2, P])
        a2 = two("a2_", [P, 2, P])
        dec = ph.sb("dec", [P, NT, HH, 4])
        S = two("S", [P, 5, HW])
        junk = ph.sb("junk", [P, HD])
        ss = ph.sb("ss", [P, 4, NT * HH])
        yo = two("yo", [P, W])
        ps = ph.psum()
        const_in, y_st, passed = (ph.sem(n) for n in ("const_in", "y_st", "passed"))
        f_in, q_in, v_in, g_in = (ph.sem(n) for n in ("f_in", "q_in", "v_in", "g_in"))
        gates = ph.marks("gates", "ln q g keys")
        lf_ok, decays, dec_ok, g_ok = (ph.sem(n) for n in ("lf_ok", "decays", "dec_ok", "g_ok"))
        valued = ph.count("valued")
        sums, exps, clamped, small, scaled, side, turned, copy1, copy2, scored, masked, outs, states, final, kept = (
            [ph.count(f"{n}{q}") for q in range(2)]
            for n in ("sums", "exps", "clamped", "small", "scaled", "side", "turned", "copy1", "copy2", "scored",
                      "masked", "outs", "states", "final", "kept"))
        mean, root, inverse, normed, stored = (ph.sem(n) for n in ("mean", "root", "inverse", "normed", "stored"))
        blk = ph.block()
        groups = range(2)
        cols = lambda q: slice(HW * q, HW * (q + 1))
        tile_of = lambda z, t, q: z[:, bass.ds(t, 1), cols(q)].rearrange("p o c -> p (o c)")
        whole = lambda z: z[:, :, :].rearrange("p t c -> p (t c)")
        half = lambda b, i: ps[:, b, i * HW:(i + 1) * HW]

        def pairs_of_tiles(eng, body):
            with eng.Fori(0, NT // 2) as j:
                for b in range(2):
                    body(2 * j + b, b)

        @blk.sync
        def _(sp):
            def load(dst, col, sem):
                sp.dma_start(dst[:, :, :], proj[:, col:col + W].rearrange("(t p) c -> p t c", p=P)).then_inc(sem, 16)

            load(LF, COL_F, f_in)
            for dst, src in ((masks[:, :], masks_d), (ind[:, :], g["ind32"]), (nw[:, :], g["hgrn_norm_w_2"].partition_broadcast(P))):
                sp.dma_start(dst, src).then_inc(const_in, 16)
            load(Q, COL_Q, q_in)
            load(V, COL_I, v_in)
            load(G, COL_G, g_in)
            for t in range(NT):
                sp.wait_ge(normed, t + 1)
                sp.dma_start(out[t * P:(t + 1) * P, :], Q[:, t, :]).then_inc(y_st, 16)
            sp.wait_ge(y_st, 16 * NT)

        @blk.gpsimd
        def _(po):
            po.wait_ge(v_in, 16)
            po.wait_ge(gates.sem, 4)
            for c in (valued, *side):
                c.begin(po)

            def body(t, b):
                po.drain()
                po.wait_ge(states[1].sem, states[1].done(t - 2))
                po.sem_inc(passed, 1)
                po.tensor_copy(vc[b][:, :], V[:, bass.ds(t, 1), :].rearrange("p o c -> p (o c)")).then_inc(valued.sem, 1)
                for q in groups:
                    po.wait_ge(exps[q].sem, exps[q].done(t))
                    po.sem_inc(passed, 1)
                    po.tensor_tensor(q3[q][:, :], tile_of(Q, t, q), e34[q][:, 0, :], ALU.mult)
                    po.tensor_tensor(k4[q][:, :], tile_of(K, t, q), e34[q][:, 1, :], ALU.mult).then_inc(side[q].sem, 1)

            pairs_of_tiles(po, body)

        @blk.scalar
        def _(s):
            s.wait_ge(f_in, 16)
            s.activation(whole(sp0), whole(LF), ACT.Abs)
            s.drain()
            s.activation(whole(sp0), whole(sp0), ACT.Exp, scale=-1.0)
            s.drain()
            s.activation(whole(K), whole(LF), ACT.Sigmoid, scale=-1.0)
            s.activation(whole(sp0), whole(sp0), ACT.Ln, bias=1.0).then_inc(gates.sem, gates.step("ln"))
            s.wait_ge(q_in, 16)
            s.activation(whole(Q), whole(Q), ACT.Silu).then_inc(gates.sem, gates.step("q"))
            s.wait_ge(g_in, 16)
            s.activation(whole(G), whole(G), ACT.Silu).then_inc(gates.sem, gates.step("g"))
            s.wait_ge(decays, 1)
            s.activation(dec[:, :, :, :].rearrange("p t h c -> p (t h c)"), ps[:, 7, 0:NT * HH * 4], ACT.Exp)\
                .then_inc(gates.sem, gates.step("keys"))
            for c in (*exps, *small, *copy2, *kept):
                c.begin(s)

            def body(t, b):
                for q in groups:
                    s.wait_ge(sums[q].sem, sums[q].done(t))
                    s.activation(e34[q][:, :, :].rearrange("p a c -> p (a c)"), ps[:, 4 * q + 1, :], ACT.Exp)
                    s.activation(e1[q][:, :], half(4 * q, 0), ACT.Exp).then_inc(exps[q].sem, 1)
                    s.wait_ge(clamped[q].sem, clamped[q].done(t))
                    s.activation(e2[q][:, :], e2c[q][:, :], ACT.Exp)
                    s.activation(e2n[q][:, :], e2c[q][:, :], ACT.Exp, scale=-1.0).then_inc(small[q].sem, 1)
                for q in groups:
                    s.wait_ge(turned[q].sem, turned[q].done(t))
                    s.activation(T34[q][:, :, :], blocks(ps, 4 * q + 1, 4), ACT.Copy)
                    s.activation(T5[q][:, :, :], blocks(ps, 4 * q + 3, 2), ACT.Copy).then_inc(copy2[q].sem, 1)
                for q in groups:
                    s.drain()
                    s.wait_ge(final[q].sem, final[q].done(t))
                    s.activation(tile_of(Q, t, q), half(4 * q + 3, 1), ACT.Copy)
                    for i in range(2):
                        ins = s.activation(junk[:, :], ps[:, 4 * q + 3, HW + i * HD:HW + (i + 1) * HD], ACT.Square,
                                           accum_out=ss[:, 0, bass.ds(HH * t + 2 * q + i, 1)])
                        if not i:
                            s.drain()
                    ins.then_inc(kept[q].sem, 1)

            pairs_of_tiles(s, body)
            s.wait_ge(mean, 1)
            s.activation(ss[:, 2, :], ss[:, 1, :], ACT.Sqrt).then_inc(root, 1)

        @blk.vector
        def _(ve):
            tt, ts, stt = ve.tensor_tensor, ve.tensor_scalar, ve.scalar_tensor_tensor
            for q in groups:
                ve.memset(S[q][:, :, :], 0.0)
                ve.memset(a2[q][:, :, :], 0.0)
            ve.drain()
            ve.wait_ge(const_in, 48)
            ve.wait_ge(gates.sem, 1)
            stt(whole(LF), whole(LF), 0.0, whole(sp0), ALU.min, ALU.subtract).then_inc(lf_ok, 1)
            for c in (*clamped, *scaled, *copy1, *masked, *states):
                c.begin(ve)
            ve.drain()
            ve.wait_ge(gates.sem, 4)
            tt(G[:, :, :], G[:, :, :], over(nw[:, :], NT), ALU.mult)

            def body(t, b):
                for q in groups:
                    ve.drain()
                    ve.wait_ge(sums[q].sem, sums[q].done(t))
                    ts(e2c[q][:, :], half(4 * q + 2, 0), LIM, -LIM, ALU.min, ALU.max).then_inc(clamped[q].sem, 1)
                    ve.tensor_copy(S[q][:, 0, :], S[q][:, 4, :])
                for q in groups:
                    ve.drain()
                    ve.wait_ge(exps[q].sem, exps[q].done(t))
                    tt(qk[q][:, 0, :], tile_of(Q, t, q), e1[q][:, :], ALU.mult)
                    tt(qk[q][:, 1, :], tile_of(K, t, q), e1[q][:, :], ALU.mult)
                    ve.drain()
                    ve.wait_ge(small[q].sem, small[q].done(t))
                    tt(qk[q][:, 2, :], tile_of(Q, t, q), e2[q][:, :], ALU.mult)
                    tt(qk[q][:, 3, :], tile_of(K, t, q), e2n[q][:, :], ALU.mult).then_inc(scaled[q].sem, 1)
                for q in groups:
                    ve.drain()
                    ve.wait_ge(turned[q].sem, turned[q].done(t))
                    ve.tensor_copy(T12[q][:, :, :], blocks(ps, 4 * q, 4)).then_inc(copy1[q].sem, 1)
                for q in groups:
                    ve.drain()
                    ve.wait_ge(scored[q].sem, scored[q].done(t))
                    tt(at[q][:, :, :], ps[:, 4 * q + 2, 0:HW].rearrange("p (h c) -> p h c", c=P), over(cross, 2), ALU.mult)
                    ve.copy_predicated(a2[q][:, :, :], over(diag.bitcast(U32), 2),
                                       ps[:, 4 * q + 2, HW:].rearrange("p (h c) -> p h c", c=P))
                    ve.drain()
                    tt(at[q][:, :, :], at[q][:, :, :], a2[q][:, :, :], ALU.add).then_inc(masked[q].sem, 1)
                for q in groups:
                    ve.drain()
                    ve.wait_ge(outs[q].sem, outs[q].done(t))
                    for c in range(4):
                        if c:
                            ve.drain()
                        for i in range(2):
                            hs = slice(i * HD, (i + 1) * HD)
                            ins = stt(S[q][:, c + 1, hs], S[q][:, c, hs],
                                      dec[:, bass.ds(t, 1), 2 * q + i, c:c + 1].rearrange("p o c -> p (o c)"),
                                      ps[:, 4 * q + c, hs], ALU.mult, ALU.add)
                    ins.then_inc(states[q].sem, 1)

            pairs_of_tiles(ve, body)
            ve.drain()
            ve.wait_ge(kept[0].sem, kept[0].done(NT - 1))
            ve.wait_ge(kept[1].sem, kept[1].done(NT - 1))
            ts(ss[:, 1, :], ss[:, 0, :], 1.0 / HD, EPS, ALU.mult, ALU.add).then_inc(mean, 1)
            ve.drain()
            ve.wait_ge(root, 1)
            ve.reciprocal(ss[:, 3, :], ss[:, 2, :])
            for t in range(NT):
                ve.drain()
                h4 = yo[t % 2][:, :].rearrange("p (h d) -> p h d", d=HD)
                tt(h4, Q[:, t, :].rearrange("p (h d) -> p h d", d=HD), bcast(ss[:, 3, HH * t:HH * (t + 1)], HD), ALU.mult)
                ve.drain()
                tt(Q[:, t, :], yo[t % 2][:, :], G[:, t, :], ALU.mult).then_inc(normed, 1)

        @blk.tensor
        def _(te):
            te.wait_ge(const_in, 48)
            te.wait_ge(lf_ok, 1)
            for t in range(NT):
                for h in range(HH):
                    n = 4 * (HH * t + h)
                    mm = te.matmul(ps[:, 7, n:n + 4], LF[:, t, h * HD:(h + 1) * HD], ind[:, :], start=True, stop=True)
            mm.then_inc(decays, 1)
            te.wait_ge(gates.sem, 4)
            for c in (*sums, *turned, *scored, *outs, *final):
                c.begin(te)

            def body(t, b):
                for q in groups:
                    for at_b, i, m in ((0, 0, lev), (1, 0, cum), (1, 1, suf), (2, 0, mid)):
                        mm = te.matmul(half(4 * q + at_b, i), m, tile_of(LF, t, q), start=True, stop=True)
                    mm.then_inc(sums[q].sem, 1)
                for q in groups:
                    te.wait_ge(scaled[q].sem, scaled[q].done(t))
                    for n in range(8):
                        te.transpose(block_of(ps, 4 * q, n), qk[q][:, n // 2, (n % 2) * HD:(n % 2 + 1) * HD], ident)
                    te.wait_ge(side[q].sem, side[q].done(t))
                    te.wait_ge(kept[q].sem, kept[q].done(t - 1))
                    for i in range(2):
                        mm = te.transpose(block_of(ps, 4 * q + 3, i), q3[q][:, i * HD:(i + 1) * HD], ident)
                    mm.then_inc(turned[q].sem, 1)
                for q in groups:
                    te.wait_ge(copy1[q].sem, copy1[q].done(t))
                    for i in range(2):
                        te.matmul(block_of(ps, 4 * q + 2, i), T12[q][:, 2 + i, :], T12[q][:, i, :], start=True, stop=True)
                    te.wait_ge(copy2[q].sem, copy2[q].done(t))
                    for i in range(2):
                        mm = te.matmul(block_of(ps, 4 * q + 2, 2 + i), T34[q][:, 2 + i, :], T34[q][:, i, :],
                                       start=True, stop=True)
                    mm.then_inc(scored[q].sem, 1)
                te.wait_ge(valued.sem, valued.done(t))
                for q in groups:
                    te.wait_ge(masked[q].sem, masked[q].done(t))
                    v = vc[b][:, cols(q)]
                    for c in range(4):
                        o = slice(32 * c, 32 * c + 32)
                        for i in range(2):
                            hs = slice(i * HD, (i + 1) * HD)
                            mm = te.matmul(ps[:, 4 * q + c, hs], k4[q][o, hs], v[o, hs], start=True, stop=True)
                    mm.then_inc(outs[q].sem, 1)
                for q in groups:
                    te.wait_ge(states[q].sem, states[q].done(t))
                    te.sem_inc(passed, 1)
                    for i in range(2):
                        hs = slice(i * HD, (i + 1) * HD)
                        te.matmul(half(4 * q + 3, 1)[:, hs], at[q][:, i, :], vc[b][:, cols(q)][:, hs], start=True, stop=False)
                        for c in range(4):
                            o = slice(32 * c, 32 * c + 32)
                            mm = te.matmul(half(4 * q + 3, 1)[o, hs], T5[q][:, i, o], S[q][:, c, hs], start=False, stop=True)
                    mm.then_inc(final[q].sem, 1)

            pairs_of_tiles(te, body)


GH, GP, NG = 16, 64, 32
S5W = GH * NG
NJ = NG // 2
JQ = NJ // 4


def s5(nc, proj, out, g):
    L = 256
    TWO_PI_HI, TWO_PI_LO = 6.28125, 2 * math.pi - 6.28125
    with Phase(nc, "s5") as ph:
        ident = ph.sb("ident", [P, P])
        prm = ph.sb("prm", [P, 24, NJ])
        ki = ph.sb("ki", [P, 2, NJ], I32)
        bc = ph.sb("bc", [P, 2, NJ, GH])
        bb = ph.sb("bb", [P, 2, NJ, GH])
        bt = ph.sb("bt", [P, 2, NJ, GH])
        bpad = ph.sb("bpad", [P, 2, NJ, 2 * GH])
        cpad = ph.sb("cpad", [P, 2, JQ, P])
        bT = ph.sb("bT", [P, 2, JQ, P])
        cT = ph.sb("cT", [P, 2, JQ, P])
        dcol = ph.sb("dcol", [P, JQ])
        uT = ph.sb("uT", [P, JQ, SEQ])
        two = lambda n, shape: [ph.sb(f"{n}{b}", shape) for b in range(2)]
        bq = two("bq", [P, 2, P])
        cq = two("cq", [P, 3, P])
        uq = two("uq", [P, SEQ])
        pq = ph.sb("pq", [P, 3, 4])
        tab = ph.sb("tab", [P, 2, NJ, L])
        w = ph.sb("w", [P, 2, SEQ])
        wt = ph.sb("wt", [P, 2, SEQ])
        ini = ph.sb("ini", [P, 4])
        zz = ph.sb("z", [P, 2, 2, SEQ])
        z = [zz[:, b, :, :] for b in range(2)]
        ut = zz[:, :, :, :].rearrange("p b k (t c) -> p (b k t) c", c=S5W)
        pr = two("pr", [P, 4, SEQ])
        yT = ph.sb("yT", [P, JQ, SEQ])
        gluw = ph.sb("gluw", [P, JQ, 2 * S5W])
        glub = ph.sb("glub", [P, 2 * S5W])
        nw = ph.sb("nw", [P, S5W])
        gel = ph.sb("gel", [P, 3, JQ, P])
        ycur = two("ycur", [P, JQ, P])
        gate = two("gate", [P, S5W])
        hg = ph.sb("hg", [P, 2 * S5W])
        sig = ph.sb("sig", [P, S5W])
        ys = tab[:, 0, :, :].rearrange("p (t a) c -> p t (a c)", t=NT)
        ss = ph.sb("ss", [P, 4, NT])
        ps = ph.psum()
        const_in, c_in, pad_set, x_in, y_st, passed = (ph.sem(n) for n in (
            "const_in", "c_in", "pad_set", "x_in", "y_st", "passed"))
        g_in = [ph.sem(f"g_in{b}") for b in range(2)]
        pre_a = ph.marks("pre_act", "step mag sin bTcT")
        pre_d = ph.marks("pre_dve", "lr angles bpad")
        pre_p = ph.marks("pre_pe", "turned")
        uturned, ucopied = ph.count("uturned"), ph.count("ucopied")
        current, taken, tables = ph.count("current"), ph.count("taken"), ph.sem("tables")
        fed, read = ([ph.count(f"{n}{h}") for h in range(2)] for n in ("fed", "read"))
        scanned, products, summed = (ph.count(n) for n in ("scanned", "products", "summed"))
        cubic, gelu, activated, glu, biased, opened, joined, squared = (ph.count(n) for n in (
            "cubic", "gelu", "activated", "glu", "biased", "opened", "joined", "squared"))
        mean, root, normed = (ph.sem(n) for n in ("mean", "root", "normed"))
        blk = ph.block()
        C = lambda i: prm[:, i, :]

        def state_tiles(eng, body):
            with eng.Fori(0, JQ // 2) as j:
                for r in range(2):
                    for i in range(4):
                        body(j * 8 + (4 * r + i), i, 2 * j + r, r)

        def build_phases(eng, tiles):
            c, sn = (tab[:, k, tiles, :] for k in range(2))
            m = c.shape[1]
            t0, t1 = (pr[k][:, :, :].rearrange("p a c -> p (a c)").rearrange("p (j n) -> p j n", n=L)[:, tiles, :]
                      for k in range(2))
            eng.tensor_copy(c[:, :, 0:1], prm[:, 9, tiles].unsqueeze(2))
            eng.tensor_copy(sn[:, :, 0:1], prm[:, 8, tiles].unsqueeze(2))
            n = 1
            while n < L:
                eng.drain()
                cn, sc = (z[:, :, n - 1:n].to_broadcast([P, m, n]) for z in (c, sn))
                new = slice(n, 2 * n)
                eng.tensor_tensor(t0[:, :, 0:n], sn[:, :, 0:n], sc, ALU.mult)
                eng.tensor_tensor(t1[:, :, 0:n], c[:, :, 0:n], sc, ALU.mult)
                eng.tensor_tensor(c[:, :, new], c[:, :, 0:n], cn, ALU.mult)
                eng.tensor_tensor(sn[:, :, new], sn[:, :, 0:n], cn, ALU.mult)
                eng.drain()
                eng.tensor_tensor(c[:, :, new], c[:, :, new], t0[:, :, 0:n], ALU.subtract)
                ins = eng.tensor_tensor(sn[:, :, new], sn[:, :, new], t1[:, :, 0:n], ALU.add)
                n *= 2
            ins.then_inc(tables, 1)

        DVE_TILES = 11

        @blk.sync
        def _(sp):
            ls = g["s5_log_step_2"].rearrange("(j g) -> g j", g=2)
            jobs = [(ident[:, :], g["ident"]),
                    (dcol[:, :], g["s5_d_2"].rearrange("(k p) -> p k", p=P)),
                    (gluw[:, :, :], g["s5_glu_w_2"].rearrange("(k p) n -> p k n", p=P)),
                    (glub[:, :], g["s5_glu_b_2"].partition_broadcast(P)),
                    (nw[:, :], g["s5_norm_w_2"].partition_broadcast(P))]
            for k in range(2):
                half = slice(64 * k, 64 * k + 64)
                jobs += [(prm[half, 2, :], ls[k, :].partition_broadcast(64)),
                         (prm[half, 0, :], g["s5_lambda_re_2"].rearrange("(j g) p -> g p j", g=2)[k]),
                         (prm[half, 1, :], g["s5_lambda_im_2"].rearrange("(j g) p -> g p j", g=2)[k]),
                         (bc[half, 0, :, :], g["s5_b_re_2"].rearrange("(j g) p h -> g p j h", g=2)[k]),
                         (bc[half, 1, :, :], g["s5_b_im_2"].rearrange("(j g) p h -> g p j h", g=2)[k])]
            assert len(jobs) == 15
            for dst, src in jobs:
                sp.dma_start(dst, src, allow_slow_non_contiguous=True).then_inc(const_in, 16)
            sp.wait_ge(pad_set, 1)
            for i, name in enumerate(("s5_c_re_2", "s5_c_im_2")):
                c_v = g[name].rearrange("(J j g) h p -> j g h J p", j=4, g=2)
                for jj in range(4):
                    for k in range(2):
                        r0 = 32 * jj + 16 * k
                        sp.dma_start(cpad[r0:r0 + 16, i, :, 64 * k:64 * k + 64], c_v[jj, k]).then_inc(c_in, 16)
            def load_gate(t, b):
                sp.dma_start(gate[b][:, :], proj[bass.ds(t * P, P), COL_SG:COL_SG + S5W]).then_inc(g_in[b], 16)

            for b in range(2):
                load_gate(b, b)
            with sp.Fori(0, NT // 2 - 1) as j:
                for b in range(2):
                    sp.wait_ge(joined.sem, joined.done(2 * j + b))
                    sp.sem_inc(passed, 1)
                    load_gate(2 * j + b + 2, b)
            for t in range(NT):
                sp.wait_ge(normed, t + 1)
                sp.dma_start(out[t * P:(t + 1) * P, :], ys[:, t, :]).then_inc(y_st, 16)
            sp.wait_ge(y_st, 16 * NT)

        @blk.gpsimd
        def _(pool):
            pool.memset(cpad[:, :, :, :], 0.0).then_inc(pad_set, 1)
            pool.dma_start(ut[:, :, :], proj[:, COL_U:COL_U + S5W].rearrange("(t p) c -> p t c", p=P)).then_inc(x_in, 16)
            tt = pool.tensor_tensor
            pool.wait_ge(pre_a.sem, 3)
            build_phases(pool, slice(DVE_TILES, NJ))
            pool.drain()
            pool.wait_ge(tables, 2)
            products.begin(pool)

            def body(T, i, R, r):
                b = i % 2
                phase = lambda k: tab[:, k, bass.ds(T, 1), :].rearrange("p o l -> p (o l)").unsqueeze(1)\
                    .to_broadcast([P, SEQ // L, L])
                pool.drain()
                pool.wait_ge(scanned.sem, scanned.done(T))
                pool.sem_inc(passed, 1)
                pool.wait_ge(summed.sem, summed.done(T - 2))
                pool.sem_inc(passed, 1)
                for k, (part, fn) in enumerate(((0, 0), (1, 1), (0, 1), (1, 0))):
                    ins = tt(pr[b][:, k, :].rearrange("p (a l) -> p a l", l=L),
                             z[b][:, part, :].rearrange("p (a l) -> p a l", l=L), phase(fn), ALU.mult)
                ins.then_inc(products.sem, 1)

            state_tiles(pool, body)

        @blk.scalar
        def _(a):
            a.wait_ge(const_in, 240)
            a.activation(C(3), C(2), ACT.Exp).then_inc(pre_a.sem, pre_a.step("step"))
            a.wait_ge(pre_d.sem, 1)
            a.activation(C(5), C(4), ACT.Exp).then_inc(pre_a.sem, pre_a.step("mag"))
            a.wait_ge(pre_d.sem, 2)
            a.activation(C(8), C(6), ACT.Sin)
            a.activation(C(9), C(7), ACT.Sin).then_inc(pre_a.sem, pre_a.step("sin"))
            a.wait_ge(pre_p.sem, 1)
            a.activation(bT[:, :, :, :].rearrange("p a j c -> p (a j) c"), blocks(ps, 0, 8), ACT.Copy)
            a.activation(cT[:, 0, :, :], blocks(ps, 2, 4), ACT.Copy)
            a.activation(cT[:, 1, :, :], blocks(ps, 3, 4), ACT.Copy, scale=-1.0).then_inc(pre_a.sem, pre_a.step("bTcT"))
            for c in (ucopied, current):
                c.begin(a)

            def copy_inputs(t, b, n):
                a.wait_ge(uturned.sem, uturned.done(t))
                a.activation(uT[:, :, bass.ds(t * P, P)], blocks(ps, 6 + b, 4), ACT.Copy).then_inc(ucopied.sem, 1)

            each_tile(a, copy_inputs)
            a.drain()

            def round_inputs(R, r):
                one = bass.ds(R, 1)
                block = lambda z: z.rearrange("p o c -> p (o c)")
                a.drain()
                a.wait_ge(summed.sem, summed.done(R * 4 - 5))
                a.wait_ge(taken.sem, taken.done(R - 2))
                for k in range(2):
                    a.activation(bq[r][:, k, :], block(bT[:, k, one, :]), ACT.Copy)
                    a.activation(cq[r][:, k, :], block(cT[:, k, one, :]), ACT.Copy)
                a.activation(cq[r][:, 2, :], block(cT[:, 0, one, :]), ACT.Copy, scale=-1.0)
                a.activation(uq[r][:, :], block(uT[:, one, :]), ACT.Copy).then_inc(current.sem, 1)

            for r in range(2):
                for k in range(2):
                    a.activation(bq[r][:, k, :], bT[:, k, r, :], ACT.Copy)
                    a.activation(cq[r][:, k, :], cT[:, k, r, :], ACT.Copy)
                a.activation(cq[r][:, 2, :], cT[:, 0, r, :], ACT.Copy, scale=-1.0)
                a.activation(uq[r][:, :], uT[:, r, :], ACT.Copy).then_inc(current.sem, 1)
            with a.Fori(1, JQ // 2) as j:
                for r in range(2):
                    round_inputs(2 * j + r, r)
            for c in (gelu, opened, squared):
                c.begin(a)

            def gelu_of(t):
                a.wait_ge(cubic.sem, cubic.done(t))
                a.activation(gel[:, 2, :, :], gel[:, 1, :, :], ACT.Sigmoid, scale=2 * math.sqrt(2 / math.pi))\
                    .then_inc(gelu.sem, 1)

            def gates_of(t, b, n):
                if not last(t):
                    gelu_of(t + 1)
                a.drain()
                a.wait_ge(biased.sem, biased.done(t))
                a.wait_ge(g_in[b], 16 * n + 16)
                a.activation(sig[:, :], hg[:, S5W:], ACT.Sigmoid)
                a.activation(gate[b][:, :], gate[b][:, :], ACT.Silu).then_inc(opened.sem, 1)
                a.drain()
                a.wait_ge(joined.sem, joined.done(t))
                y = ys[:, t, :] if isinstance(t, int) else ys[:, bass.ds(t, 1), :].rearrange("p o c -> p (o c)")
                a.activation(sig[:, :], y, ACT.Square, accum_out=ss[:, 0, t:t + 1] if isinstance(t, int)
                             else ss[:, 0, bass.ds(t, 1)]).then_inc(squared.sem, 1)

            gelu_of(0)
            each_tile(a, gates_of)
            a.wait_ge(mean, 1)
            a.activation(ss[:, 2, :], ss[:, 1, :], ACT.Sqrt).then_inc(root, 1)

        @blk.vector
        def _(ve):
            tt, ts, stt = ve.tensor_tensor, ve.tensor_scalar, ve.scalar_tensor_tensor
            ve.memset(bpad[:, :, :, :], 0.0)
            ve.drain()
            ve.wait_ge(pre_a.sem, 1)
            ts(C(10), C(0), -1e-4, None, ALU.min)
            ve.drain()
            tt(C(4), C(10), C(3), ALU.mult).then_inc(pre_d.sem, pre_d.step("lr"))
            tt(C(11), C(1), C(3), ALU.mult)
            ve.drain()
            ts(C(12), C(11), math.pi / 2, None, ALU.add)
            for k, src, dst in ((0, 11, 6), (1, 12, 7)):
                ve.drain()
                ts(C(13), C(src), 1 / (2 * math.pi), None, ALU.mult)
                ve.drain()
                ve.tensor_copy(ki[:, k, :], C(13))
                ve.drain()
                ve.tensor_copy(C(14), ki[:, k, :])
                ve.drain()
                stt(C(13), C(14), -TWO_PI_HI, C(src), ALU.mult, ALU.add)
                ve.drain()
                stt(C(15), C(14), -TWO_PI_LO, C(13), ALU.mult, ALU.add)
                for sign, cmp in ((-1, ALU.is_gt), (1, ALU.is_lt)):
                    ve.drain()
                    ts(C(16), C(15), -sign * math.pi, sign * 2 * math.pi, cmp, ALU.mult)
                    ve.drain()
                    tt(C(15), C(15), C(16), ALU.add)
                ve.drain()
                ins = ts(C(dst), C(15), math.pi, -math.pi, ALU.min, ALU.max)
            ins.then_inc(pre_d.sem, pre_d.step("angles"))
            ve.drain()
            ve.wait_ge(pre_a.sem, 3)
            sn, cs, mag, lr, li = C(8), C(9), C(5), C(10), C(1)
            tt(C(13), mag, cs, ALU.mult)
            tt(C(14), mag, sn, ALU.mult)
            tt(C(15), lr, lr, ALU.mult)
            tt(C(16), li, li, ALU.mult)
            ve.drain()
            ts(C(13), C(13), -1.0, None, ALU.add)
            tt(C(15), C(15), C(16), ALU.add)
            ve.drain()
            ve.reciprocal(C(16), C(15))
            tt(C(17), C(13), lr, ALU.mult)
            tt(C(18), C(14), li, ALU.mult)
            tt(C(19), C(14), lr, ALU.mult)
            tt(C(20), C(13), li, ALU.mult)
            ve.drain()
            tt(C(17), C(17), C(18), ALU.add)
            tt(C(19), C(19), C(20), ALU.subtract)
            ve.drain()
            tt(C(17), C(17), C(16), ALU.mult)
            tt(C(19), C(19), C(16), ALU.mult)
            ve.drain()
            for k, (i, j, op) in enumerate(((0, 1, ALU.subtract), (1, 0, ALU.add))):
                tt(bb[:, k, :, :], bc[:, i, :, :], bcast(C(17), GH), ALU.mult)
                tt(bt[:, k, :, :], bc[:, j, :, :], bcast(C(19), GH), ALU.mult)
                ve.drain()
                for q in range(2):
                    half = slice(64 * q, 64 * q + 64)
                    ins = tt(bpad[half, k, :, q * GH:(q + 1) * GH], bb[half, k, :, :], bt[half, k, :, :], op)
            ins.then_inc(pre_d.sem, pre_d.step("bpad"))
            ve.drain()
            build_phases(ve, slice(0, DVE_TILES))
            ve.drain()
            ve.wait_ge(tables, 2)
            for c in (*read, scanned, taken):
                c.begin(ve)

            def body(T, i, R, r):
                b = i % 2
                if i == 0:
                    four = bass.ds(R * 4, 4)
                    ve.drain()
                    ve.tensor_copy(pq[:, 0, :], prm[:, 5, four])
                    for k in range(2):
                        ve.tensor_copy(pq[:, 1 + k, :], tab[:, k, four, L - 1:L].rearrange("p j o -> p (j o)"))
                phase = lambda k: tab[:, k, bass.ds(T, 1), :].rearrange("p o l -> p (o l)").unsqueeze(1)\
                    .to_broadcast([P, 512 // L, L])
                chunks = lambda x: x.rearrange("p (a l) -> p a l", l=L)
                for h in range(2):
                    cols = slice(512 * h, 512 * (h + 1))
                    re, im = (chunks(ps[:, 2 * h + k, :]) for k in range(2))
                    ve.drain()
                    ve.wait_ge(fed[h].sem, fed[h].done(T))
                    tt(chunks(w[:, 0, cols]), re, phase(0), ALU.mult)
                    tt(chunks(wt[:, 0, cols]), im, phase(1), ALU.mult)
                    tt(chunks(w[:, 1, cols]), im, phase(0), ALU.mult)
                    tt(chunks(wt[:, 1, cols]), re, phase(1), ALU.mult).then_inc(read[h].sem, 1)
                ve.drain()
                tt(w[:, 0, :], w[:, 0, :], wt[:, 0, :], ALU.add)
                tt(w[:, 1, :], w[:, 1, :], wt[:, 1, :], ALU.subtract)
                ve.drain()
                ve.wait_ge(products.sem, products.done(T - 2))
                cl, sl = pq[:, 1, i:i + 1], pq[:, 2, i:i + 1]
                for q in range(SEQ // L):
                    if q:
                        zr, zi = (z[b][:, k, q * L - 1:q * L] for k in range(2))
                        ve.drain()
                        ts(ini[:, 2:3], zi, sl, None, ALU.mult)
                        ts(ini[:, 3:4], zr, sl, None, ALU.mult)
                        ve.drain()
                        stt(ini[:, 0:1], zr, cl, ini[:, 2:3], ALU.mult, ALU.subtract)
                        stt(ini[:, 1:2], zi, cl, ini[:, 3:4], ALU.mult, ALU.add)
                        ve.drain()
                    for k in range(2):
                        ins = ve.tensor_tensor_scan(z[b][:, k, q * L:(q + 1) * L], pq[:, 0, i:i + 1].to_broadcast([P, L]),
                                                    w[:, k, q * L:(q + 1) * L], ini[:, k:k + 1] if q else 0.0,
                                                    ALU.mult, ALU.add)
                ins.then_inc(scanned.sem, 1)

            def finish(R, r):
                one = bass.ds(R, 1)
                ve.drain()
                ve.wait_ge(summed.sem, summed.done(R * 4 + 3))
                stt(yT[:, one, :].rearrange("p o c -> p (o c)"), uq[r][:, :], dcol[:, one], banks(ps, 4 + 2 * r), ALU.mult, ALU.add)\
                    .then_inc(taken.sem, 1)

            with ve.Fori(0, JQ // 2) as j:
                for r in range(2):
                    for i in range(4):
                        body(j * 8 + (4 * r + i), i, 2 * j + r, r)
                    if r:
                        finish(2 * j, 0)
                finish(2 * j + 1, 1)
            for c in (cubic, activated, biased, joined):
                c.begin(ve)

            def gelu_of(t, b):
                x = yT[:, :, bass.ds(t * P, P)]
                ve.drain()
                tt(gel[:, 0, :, :], x, x, ALU.mult)
                ve.drain()
                ts(gel[:, 0, :, :], gel[:, 0, :, :], 0.044715, 1.0, ALU.mult, ALU.add)
                ve.drain()
                tt(gel[:, 1, :, :], gel[:, 0, :, :], x, ALU.mult).then_inc(cubic.sem, 1)
                ve.drain()
                ve.wait_ge(gelu.sem, gelu.done(t))
                tt(ycur[b][:, :, :], gel[:, 2, :, :], x, ALU.mult).then_inc(activated.sem, 1)

            def glu_of(t, b, n):
                if not last(t):
                    gelu_of(t + 1, 1 - b)
                ve.drain()
                ve.wait_ge(glu.sem, glu.done(t))
                tt(hg[:, :], banks(ps, 2 * b), glub[:, :], ALU.add).then_inc(biased.sem, 1)
                ve.drain()
                ve.wait_ge(opened.sem, opened.done(t))
                tt(hg[:, 0:S5W], hg[:, 0:S5W], sig[:, :], ALU.mult)
                ve.drain()
                y = ys[:, t, :] if isinstance(t, int) else ys[:, bass.ds(t, 1), :].rearrange("p o c -> p (o c)")
                tt(y, hg[:, 0:S5W], gate[b][:, :], ALU.mult).then_inc(joined.sem, 1)

            gelu_of(0, 0)
            each_tile(ve, glu_of)
            ve.drain()
            ve.wait_ge(squared.sem, squared.done(NT - 1))
            ts(ss[:, 1, :], ss[:, 0, :], 1.0 / S5W, EPS, ALU.mult, ALU.add).then_inc(mean, 1)
            ve.drain()
            ve.wait_ge(root, 1)
            ve.reciprocal(ss[:, 3, :], ss[:, 2, :])
            ve.drain()
            for t in range(NT):
                stt(ys[:, t, :], ys[:, t, :], ss[:, 3, t:t + 1], nw[:, :], ALU.mult, ALU.mult).then_inc(normed, 1)

        @blk.tensor
        def _(te):
            te.wait_ge(const_in, 240)
            te.wait_ge(pre_d.sem, 3)
            te.wait_ge(c_in, 256)
            for k in range(2):
                for j in range(JQ):
                    te.transpose(block_of(ps, k, j),
                                 bpad[:, k, 4 * j:4 * j + 4, :].rearrange("p j c -> p (j c)"), ident[:, :])
                    mm = te.transpose(block_of(ps, 2 + k, j), cpad[:, k, j, :], ident[:, :])
            mm.then_inc(pre_p.sem, pre_p.step("turned"))
            te.wait_ge(x_in, 16)
            for c in (uturned, *fed, summed):
                c.begin(te)
            for t in range(NT):
                te.wait_ge(ucopied.sem, ucopied.done(t - 2))
                for j in range(JQ):
                    mm = te.transpose(block_of(ps, 6 + t % 2, j), ut[:, t, j * P:(j + 1) * P], ident[:, :])
                mm.then_inc(uturned.sem, 1)

            def feed(T, i, R, r):
                rows = slice(32 * i, 32 * i + 32)
                if i == 0:
                    te.wait_ge(current.sem, current.done(R))
                for h in range(2):
                    te.wait_ge(read[h].sem, read[h].done(T - 1))
                    te.sem_inc(passed, 1)
                    for k in range(2):
                        mm = te.matmul(ps[:, 2 * h + k, :], bq[r][rows, k, :], uq[r][rows, h * 512:(h + 1) * 512],
                                       start=True, stop=True)
                    mm.then_inc(fed[h].sem, 1)

            def total(T, i, R, r):
                rows, b = slice(32 * i, 32 * i + 32), i % 2
                te.wait_ge(products.sem, products.done(T))
                te.sem_inc(passed, 1)
                for n in range(2):
                    for k, c in enumerate((0, 2, 1, 1)):
                        mm = te.matmul(ps[rows, 4 + 2 * r + n, :], cq[r][:, c, rows], pr[b][:, k, n * 512:(n + 1) * 512],
                                       start=(k == 0), stop=(k == 3))
                mm.then_inc(summed.sem, 1)

            te.wait_ge(pre_a.sem, 4)
            with te.Fori(0, JQ // 2) as j:
                steps = [(j * 8 + (4 * r + i), i, 2 * j + r, r) for r in range(2) for i in range(4)]
                feed(*steps[0])
                for n, step in enumerate(steps):
                    if n + 1 < len(steps):
                        feed(*steps[n + 1])
                    if n % 4 == 0:
                        te.wait_ge(taken.sem, taken.done(step[2] - 2))
                        te.sem_inc(passed, 1)
                    total(*step)
            for c in (glu,):
                c.begin(te)

            def product(t, b, n):
                te.wait_ge(activated.sem, activated.done(t))
                te.wait_ge(biased.sem, biased.done(t - 2))
                for h in range(2):
                    for k in range(JQ):
                        mm = te.matmul(ps[:, 2 * b + h, :], ycur[b][:, k, :], gluw[:, k, h * 512:(h + 1) * 512],
                                       start=(k == 0), stop=(k == JQ - 1))
                mm.then_inc(glu.sem, 1)

            each_tile(te, product)


NGRP, EPG = 4, 8
NE = NGRP * EPG
FF = 512
KF = FF // P
N_BLOCKS = (2 * SEQ + NE * P) // P
BIG = 1e30


def route_consts():
    t, l = np.arange(P)[:, None], np.arange(P)[None, :]
    io = np.broadcast_to(np.arange(EPG, dtype=np.float32), (P, EPG))
    return np.concatenate([(t == l).astype(np.float32), (t < l).astype(np.float32), np.ones((P, P), np.float32), io,
                           (t * P).astype(np.float32)], axis=1)


def token_ids():
    return (np.arange(NT)[None, :] * P + np.arange(P)[:, None]).astype(np.int32)


def route(nc, x, hbuf, buf_tok, ybuf, dests, weights, blk_e, n_pairs, consts_d, ids_d, g):
    with Phase(nc, "route") as ph:
        cst = ph.sb("cst", [P, 3 * P + EPG + 1])
        ident, strict, ones = (cst[:, i * P:(i + 1) * P] for i in range(3))
        iota, bcol = cst[:, 3 * P:3 * P + EPG], cst[:, 3 * P + EPG:]
        ids = ph.sb("ids", [P, NT], I32)
        gain = ph.sb("gain", [P, D])
        wr = ph.sb("wr", [P, KD, NGRP + NE])
        bias = ph.sb("bias", [P, NGRP + NE])
        xt = ph.sb("xt", [P, D])
        junk = ph.sb("junk", [P, D])
        ss = ph.sb("ss", [P, 4])
        h0 = ph.sb("h0", [P, D])
        h = ph.sb("h", [P, D])
        hT = ph.sb("hT", [P, KD, P])
        L = ph.sb("L", [P, NT, NGRP + NE])
        sc = ph.sb("sc", [P, 16, NT])
        og = ph.sb("og", [P, NT, NGRP])
        o8 = ph.sb("o8", [P, 2, NT, EPG])
        t8 = ph.sb("t8", [P, NT, EPG])
        t4 = ph.sb("t4", [P, NT, NGRP])
        es = ph.sb("es", [P, NT, EPG])
        e2 = ph.sb("e2", [P, NT, EPG])
        O = ph.sb("O", [P, 2, NT, NE])
        A = ph.sb("A", [P, NT, NE])
        pre = ph.sb("pre", [P, NT + 1, NE])
        Dst = ph.sb("Dst", [P, NT, NE])
        cnt = ph.sb("cnt", [P, 6, NE])
        cnti = ph.sb("cnti", [P, 2, NE], I32)
        di = ph.sb("di", [P, 2, NT], I32)
        wts = ph.sb("wts", [P, 2, NT])
        be = ph.sb("be", [P, 2])
        bei = ph.sb("bei", [P, 1], I32)
        npi = ph.sb("npi", [P, 2], I32)
        zero = ph.sb("zero", [P, N_BLOCKS + 2], I32)
        zrow = ph.sb("zrow", [P, D])
        ps = ph.psum()
        const_in, x_in, h_st, fill_st, tok_st, meta_st, passed = (ph.sem(n) for n in (
            "const_in", "x_in", "h_st", "fill_st", "tok_st", "meta_st", "passed"))
        act = ph.steps("act", "square root")
        dve = ph.steps("dve", "mean normed hT logits")
        pe = ph.steps("pe", "turned logits")
        d2 = ph.marks("dve2", "shifted diff counted rows")
        a2 = ph.marks("act2", "gexp eexp")
        p2 = ph.marks("pe2", "counts")
        blk = ph.block()

        @blk.sync
        def _(sp):
            for dst, src in ((cst[:, :], consts_d), (ids[:, :], ids_d), (gain[:, :], g["norm_ffn"].partition_broadcast(P)),
                             (wr[:, :, 0:NGRP], g["w_group"].rearrange("(k p) n -> p k n", p=P)),
                             (wr[:, :, NGRP:], g["w_expert_router"].rearrange("(k p) n -> p k n", p=P)),
                             (bias[:, 0:NGRP], g["b_group"].partition_broadcast(P)),
                             (bias[:, NGRP:], g["b_expert_router"].partition_broadcast(P))):
                sp.dma_start(dst, src, allow_slow_non_contiguous=True).then_inc(const_in, 16)
            sp.sem_inc(h_st, 16)
            with sp.Fori(0, NT) as t:
                sp.wait_ge(dve.sem, dve.start(t))
                sp.dma_start(xt[:, :], x[bass.ds(t * P, P), :]).then_inc(x_in, 16)
                sp.wait_ge(dve.sem, dve.at("normed", t))
                sp.sem_inc(passed, 1)
                sp.dma_start(hbuf[bass.ds(t * P, P), :], h[:, :]).then_inc(h_st, 16)
            sp.wait_ge(h_st, 16 * (NT + 1))
            sp.wait_ge(d2.sem, 4)
            sp.dma_start(dests, di[:, :, :]).then_inc(meta_st, 16)
            sp.dma_start(weights, wts[:, :, :]).then_inc(meta_st, 16)
            sp.dma_start(blk_e, bei[0:N_BLOCKS, :]).then_inc(meta_st, 16)
            sp.dma_start(n_pairs, npi[0:1, 1:2]).then_inc(meta_st, 16)
            sp.wait_ge(meta_st, 64)

        @blk.gpsimd
        def _(pool):
            pool.memset(zero[:, :], 0)
            pool.memset(zrow[:, :], 0.0)
            pool.drain()
            pool.dma_start(buf_tok.rearrange("(p b) o -> p (b o)", p=P), zero[:, :]).then_inc(fill_st, 16)
            full = 2 * SEQ // P
            pool.dma_start(ybuf[full * P:, :].rearrange("(b p) d -> p b d", p=P), over(zrow[:, :], N_BLOCKS - full))\
                .then_inc(fill_st, 16)
            pool.wait_ge(fill_st, 32)
            pool.wait_ge(d2.sem, 4)
            for k in range(2):
                for t in range(NT):
                    pool.indirect_dma_start(out=buf_tok, out_offset=bass.IndirectOffsetOnAxis(
                        ap=di[:, k, t:t + 1].bitcast(U32), axis=0), in_=ids[:, t:t + 1], in_offset=None).then_inc(tok_st, 16)
            pool.wait_ge(tok_st, 16 * 2 * NT)

        @blk.scalar
        def _(s):
            act.begin(s)
            with s.Fori(0, NT) as t:
                s.wait_ge(x_in, 16 * t + 16)
                s.activation(junk[:, :], xt[:, :], ACT.Square, accum_out=ss[:, 0:1]).then_inc(act.sem, act.step("square"))
                s.wait_ge(dve.sem, dve.at("mean", t))
                s.activation(ss[:, 2:3], ss[:, 1:2], ACT.Sqrt).then_inc(act.sem, act.step("root"))
            s.wait_ge(d2.sem, 1)
            s.activation(t4[:, :, :], t4[:, :, :], ACT.Exp).then_inc(a2.sem, a2.step("gexp"))
            s.wait_ge(d2.sem, 2)
            s.activation(sc[:, 9, :], sc[:, 8, :], ACT.Exp).then_inc(a2.sem, a2.step("eexp"))

        @blk.vector
        def _(ve):
            tt, ts, stt = ve.tensor_tensor, ve.tensor_scalar, ve.scalar_tensor_tensor
            ve.drain()
            ve.wait_ge(const_in, 112)
            dve.begin(ve)
            with ve.Fori(0, NT) as t:
                ve.wait_ge(act.sem, act.at("square", t))
                ts(ss[:, 1:2], ss[:, 0:1], 1.0 / D, EPS, ALU.mult, ALU.add).then_inc(dve.sem, dve.step("mean"))
                ve.drain()
                ve.wait_ge(act.sem, act.at("root", t))
                ve.reciprocal(ss[:, 3:4], ss[:, 2:3])
                ve.drain()
                ve.wait_ge(h_st, 16 * t + 16)
                stt(h[:, :], xt[:, :], ss[:, 3:4], gain[:, :], ALU.mult, ALU.mult).then_inc(dve.sem, dve.step("normed"))
                ve.drain()
                ve.wait_ge(pe.sem, pe.at("turned", t))
                ve.tensor_copy(hT[:, :, :], blocks(ps, 0, 8)).then_inc(dve.sem, dve.step("hT"))
                ve.drain()
                ve.wait_ge(pe.sem, pe.at("logits", t))
                tt(L[:, bass.ds(t, 1), :].rearrange("p o c -> p (o c)"), ps[:, 2, 0:NGRP + NE], bias[:, :], ALU.add)\
                    .then_inc(dve.sem, dve.step("logits"))
                ve.drain()

            def first_max(onehot, values, top, n, tmp):
                ve.tensor_reduce(top, values, AX, ALU.max)
                ve.drain()
                tt(tmp, values, bcast(top, n), ALU.is_lt)
                ve.drain()
                stt(tmp, tmp, BIG, iota[:, 0:n].unsqueeze(1).to_broadcast([P, NT, n]), ALU.mult, ALU.add)
                ve.drain()
                ve.tensor_reduce(sc[:, 15, :], tmp, AX, ALU.min)
                ve.drain()
                tt(onehot, tmp, bcast(sc[:, 15, :], n), ALU.is_equal)

            G = L[:, :, 0:NGRP]
            E = L[:, :, NGRP:].rearrange("p t (g e) -> p t g e", g=NGRP)
            first_max(og[:, :, :], G, sc[:, 0, :], NGRP, t4[:, :, :])
            ve.drain()
            tt(t4[:, :, :], G, bcast(sc[:, 0, :], NGRP), ALU.subtract).then_inc(d2.sem, d2.step("shifted"))
            prod = A[:, :, :].rearrange("p t (g e) -> p t g e", g=NGRP)
            tt(prod, E, og[:, :, :].unsqueeze(3).to_broadcast([P, NT, NGRP, EPG]), ALU.mult)
            ve.drain()
            ve.tensor_reduce(es[:, :, :], prod.rearrange("p t g e -> p t e g"), AX, ALU.add)
            ve.drain()
            first_max(o8[:, 0, :, :], es[:, :, :], sc[:, 1, :], EPG, t8[:, :, :])
            ve.drain()
            stt(e2[:, :, :], o8[:, 0, :, :], -BIG, es[:, :, :], ALU.mult, ALU.add)
            ve.drain()
            first_max(o8[:, 1, :, :], e2[:, :, :], sc[:, 2, :], EPG, t8[:, :, :])
            ve.drain()
            tt(sc[:, 8, :], sc[:, 2, :], sc[:, 1, :], ALU.subtract).then_inc(d2.sem, d2.step("diff"))
            for k in range(2):
                tt(O[:, k, :, :].rearrange("p t (g e) -> p t g e", g=NGRP),
                   og[:, :, :].unsqueeze(3).to_broadcast([P, NT, NGRP, EPG]),
                   o8[:, k, :, :].unsqueeze(2).to_broadcast([P, NT, NGRP, EPG]), ALU.mult)
            ve.drain()
            tt(A[:, :, :], O[:, 0, :, :], O[:, 1, :, :], ALU.add)
            ve.memset(pre[:, 0, :], 0.0)
            for t in range(NT):
                ve.drain()
                last = tt(pre[:, t + 1, :], pre[:, t, :], A[:, t, :], ALU.add)
            last.then_inc(d2.sem, d2.step("counted"))
            ve.drain()
            ve.wait_ge(a2.sem, 2)
            ve.tensor_reduce(sc[:, 3, :], t4[:, :, :], AX, ALU.add)
            ts(sc[:, 4, :], sc[:, 9, :], 1.0, None, ALU.add)
            ve.drain()
            tt(sc[:, 5, :], sc[:, 3, :], sc[:, 4, :], ALU.mult)
            ve.drain()
            ve.reciprocal(wts[:, 0, :], sc[:, 5, :])
            ve.drain()
            tt(wts[:, 1, :], wts[:, 0, :], sc[:, 9, :], ALU.mult)
            ve.drain()
            ve.wait_ge(p2.sem, 1)
            c = lambda i: cnt[:, i, :]
            ts(c(0), ps[:, 1, 0:NE], float(P - 1), None, ALU.add)
            ve.memset(c(3), 1.0)
            ve.drain()
            ve.tensor_copy(cnti[:, 0, :], c(0))
            ve.drain()
            ts(cnti[:, 1, :], cnti[:, 0, :], 7, 7, ALU.logical_shift_right, ALU.logical_shift_left)
            ve.drain()
            ve.tensor_copy(c(1), cnti[:, 1, :])
            ve.drain()
            ve.tensor_tensor_scan(c(2), c(3), c(1), 0.0, ALU.mult, ALU.add)
            ve.drain()
            tt(c(4), c(2), c(1), ALU.subtract)
            ts(c(5), c(2), bcol, None, ALU.is_le)
            ve.drain()
            ve.tensor_reduce(be[:, 0:1], c(5), AX, ALU.add)
            tt(Dst[:, :, :], ps[:, 0, 0:NT * NE].rearrange("p (t e) -> p t e", e=NE), over(c(4), NT), ALU.add)
            ve.drain()
            ts(be[:, 1:2], be[:, 0:1], float(NE - 1), None, ALU.min)
            ve.drain()
            ve.tensor_copy(bei[:, :], be[:, 1:2])
            ts(npi[:, 0:1], cnt[:, 2, NE - 1:NE], float(P), None, ALU.add)
            ve.drain()
            ts(npi[:, 1:2], npi[:, 0:1], 8, None, ALU.logical_shift_right)
            for k in range(2):
                tt(A[:, :, :], O[:, k, :, :], Dst[:, :, :], ALU.mult)
                ve.drain()
                ve.tensor_reduce(sc[:, 10 + k, :], A[:, :, :], AX, ALU.add)
                ve.drain()
            ve.tensor_copy(di[:, :, :], sc[:, 10:12, :]).then_inc(d2.sem, d2.step("rows"))

        @blk.tensor
        def _(te):
            te.wait_ge(const_in, 112)
            pe.begin(te)
            with te.Fori(0, NT) as t:
                te.wait_ge(dve.sem, dve.at("normed", t))
                for j in range(8):
                    mm = te.transpose(block_of(ps, 0, j), h[:, j * P:(j + 1) * P], ident)
                mm.then_inc(pe.sem, pe.step("turned"))
                te.wait_ge(dve.sem, dve.at("hT", t))
                for k in range(KD):
                    mm = te.matmul(ps[:, 2, 0:NGRP + NE], hT[:, k, :], wr[:, k, :], start=(k == 0), stop=(k == KD - 1))
                mm.then_inc(pe.sem, pe.step("logits"))
            te.wait_ge(d2.sem, 3)
            te.matmul(ps[:, 0, 0:NT * NE], strict, A[:, :, :].rearrange("p t e -> p (t e)"), start=True, stop=False)
            te.matmul(ps[:, 0, 0:NT * NE], ones, pre[:, 0:NT, :].rearrange("p t e -> p (t e)"), start=False, stop=True)
            te.matmul(ps[:, 1, 0:NE], ones, pre[:, NT, :], start=True, stop=True).then_inc(p2.sem, p2.step("counts"))


def experts(nc, hbuf, buf_tok, blk_e, n_pairs, ybuf, ident_d, g):
    NB = N_BLOCKS
    with Phase(nc, "moe") as ph:
        ident = ph.sb("ident", [P, P])
        idx_all = ph.sb("idx_all", [P, NB + 2], I32)
        be = ph.sb("be", [1, NB + 1], I32)
        idx = [ph.sb(f"idx{b}", [P, 1], I32) for b in range(2)]
        xb = [ph.sb(f"xb{b}", [P, D]) for b in range(2)]
        wg = [ph.sb(f"wg{b}", [P, KD, FF]) for b in range(2)]
        wu = [ph.sb(f"wu{b}", [P, KD, FF]) for b in range(2)]
        wd = [ph.sb(f"wd{b}", [P, KF, D]) for b in range(2)]
        xT = [ph.sb(f"xT{b}", [P, KD, P]) for b in range(2)]
        sg = ph.sb("sg", [P, FF])
        a = ph.sb("a", [P, FF])
        aT = ph.sb("aT", [P, KF, P])
        yb = [ph.sb(f"yb{b}", [P, D]) for b in range(2)]
        ps = ph.psum()
        const_in = ph.sem("const_in")
        w_in = [ph.sem(f"w_in{b}") for b in range(2)]
        x_in = [ph.sem(f"x_in{b}") for b in range(2)]
        y_st = [ph.sem(f"y_st{b}") for b in range(2)]
        passed = ph.sem("passed")
        xt_ps = ph.sem("xt_ps")
        xt_sb = ph.sem("xt_sb")
        gu = ph.sem("gu")
        silu = ph.sem("silu")
        a_ok = ph.sem("a_ok")
        at_ps = ph.sem("at_ps")
        at_sb = ph.sem("at_sb")
        down = ph.sem("down")
        y_act = ph.sem("y_act")
        y_dve = ph.sem("y_dve")
        idx_ok = ph.sem("idx_ok")
        blk = ph.block()

        def turns_of(eng):
            eng.wait_ge(const_in, 64)
            return eng.value_load(be[0:1, NB:NB + 1], min_val=8, max_val=NB // 2)

        @blk.sync
        def _(sp):
            sp.dma_start(ident[:, :], ident_d).then_inc(const_in, 16)
            sp.dma_start(idx_all[:, :], buf_tok.rearrange("(b p) o -> p (b o)", p=P), allow_slow_non_contiguous=True)\
                .then_inc(const_in, 16)
            sp.dma_start(be[0:1, 0:NB], blk_e.rearrange("b o -> o b"), allow_slow_non_contiguous=True).then_inc(const_in, 16)
            sp.dma_start(be[0:1, NB:NB + 1], n_pairs).then_inc(const_in, 16)
            turns = turns_of(sp)
            with sp.Fori(0, turns) as j:
                for b in range(2):
                    e = sp.value_load(be[0:1, bass.ds(2 * j + b, 1)], min_val=0, max_val=NE - 1)
                    sp.wait_ge(down, 2 * j + b + 1)
                    sp.dma_start(wg[b][:, :, :], g["w_gate"][bass.ds(e, 1), :, :].rearrange("o (k p) f -> p (o k) f", p=P))\
                        .then_inc(w_in[b], 16)
                    sp.dma_start(wu[b][:, :, :], g["w_up"][bass.ds(e, 1), :, :].rearrange("o (k p) f -> p (o k) f", p=P))\
                        .then_inc(w_in[b], 16)
                    sp.dma_start(wd[b][:, :, :], g["w_down"][bass.ds(e, 1), :, :].rearrange("o (k p) f -> p (o k) f", p=P))\
                        .then_inc(w_in[b], 16)

        @blk.gpsimd
        def _(pool):
            def gather(n, b):
                pool.tensor_copy(idx[b][:, :], idx_all[:, bass.ds(n, 1)] if not isinstance(n, int) else idx_all[:, n:n + 1])
                pool.drain()
                pool.indirect_dma_start(out=xb[b][:, :], out_offset=None, in_=hbuf, in_offset=bass.IndirectOffsetOnAxis(
                    ap=idx[b][:, :].bitcast(U32), axis=0)).then_inc(x_in[b], 16)

            turns = turns_of(pool)
            gather(0, 0)
            gather(1, 1)
            with pool.Fori(0, turns) as j:
                for b in range(2):
                    pool.wait_ge(xt_ps, 2 * j + b + 1)
                    pool.sem_inc(passed, 1)
                    pool.wait_ge(x_in[b], 16 * j + 16)
                    gather(2 * j + b + 2, b)
            for b in range(2):
                pool.wait_ge(x_in[b], 16 * (turns + 1))

        @blk.scalar
        def _(s):
            turns = turns_of(s)
            s.wait_ge(xt_ps, 1)
            s.activation(xT[0][:, :, :], blocks(ps, 0, 8), ACT.Copy).then_inc(xt_sb, 1)
            s.sem_inc(y_act, 1)
            for b in range(2):
                s.sem_inc(y_st[b], 16)
            with s.Fori(0, turns) as j:
                for b in range(2):
                    n = 2 * j + b
                    s.wait_ge(gu, n + 1)
                    s.activation(sg[:, :], ps[:, 2, :], ACT.Silu).then_inc(silu, 1)
                    s.wait_ge(xt_ps, n + 2)
                    s.activation(xT[1 - b][:, :, :], blocks(ps, 0, 8), ACT.Copy).then_inc(xt_sb, 1)
                    s.wait_ge(y_st[b], 16 * j + 16)
                    s.wait_ge(down, n + 3)
                    s.activation(yb[b][:, 0:512], ps[:, 5, :], ACT.Copy).then_inc(y_act, 1)
                    s.wait_ge(y_act, n + 2)
                    s.wait_ge(y_dve, n + 2)
                    s.sem_inc(passed, 1)
                    s.dma_start(ybuf[bass.ds(n * P, P), :], yb[b][:, :]).then_inc(y_st[b], 16)
            for b in range(2):
                s.wait_ge(y_st[b], 16 * (turns + 1))
                s.sem_inc(passed, 1)

        @blk.vector
        def _(ve):
            turns = turns_of(ve)
            ve.sem_inc(a_ok, 1)
            ve.sem_inc(y_dve, 1)
            with ve.Fori(0, turns) as j:
                for b in range(2):
                    n = 2 * j + b
                    ve.drain()
                    ve.wait_ge(silu, n + 1)
                    ve.tensor_tensor(a[:, :], sg[:, :], ps[:, 3, :], ALU.mult).then_inc(a_ok, 1)
                    ve.drain()
                    ve.wait_ge(at_ps, n + 1)
                    ve.tensor_copy(aT[:, :, :], blocks(ps, 4, 4)).then_inc(at_sb, 1)
                    ve.drain()
                    ve.wait_ge(y_st[b], 16 * j + 16)
                    ve.wait_ge(down, n + 3)
                    ve.tensor_copy(yb[b][:, 512:], ps[:, 6, :]).then_inc(y_dve, 1)

        @blk.tensor
        def _(te):
            def turn(b):
                for k in range(KD):
                    mm = te.transpose(block_of(ps, 0, k), xb[b][:, k * P:(k + 1) * P], ident[:, :])
                mm.then_inc(xt_ps, 1)

            te.sem_inc(down, 2)
            turns = turns_of(te)
            te.wait_ge(x_in[0], 16)
            turn(0)
            with te.Fori(0, turns) as j:
                for b in range(2):
                    n = 2 * j + b
                    te.wait_ge(xt_sb, n + 1)
                    te.wait_ge(a_ok, n + 1)
                    te.wait_ge(w_in[b], 48 * j + 48)
                    for bank, w in ((2, wg), (3, wu)):
                        for k in range(KD):
                            mm = te.matmul(ps[:, bank, :], xT[b][:, k, :], w[b][:, k, :], start=(k == 0), stop=(k == KD - 1))
                    mm.then_inc(gu, 1)
                    te.wait_ge(x_in[1 - b], 16 * (j + b) + 16)
                    turn(1 - b)
                    te.wait_ge(a_ok, n + 2)
                    for k in range(KF):
                        mm = te.transpose(block_of(ps, 4, k), a[:, k * P:(k + 1) * P], ident[:, :])
                    mm.then_inc(at_ps, 1)
                    te.wait_ge(at_sb, n + 1)
                    te.wait_ge(y_act, n + 1)
                    te.wait_ge(y_dve, n + 1)
                    for m in range(2):
                        for k in range(KF):
                            mm = te.matmul(ps[:, 5 + m, :], aT[:, k, :], wd[b][:, k, m * 512:(m + 1) * 512],
                                           start=(k == 0), stop=(k == KF - 1))
                    mm.then_inc(down, 1)


def combine(nc, x, ybuf, dests, weights, out, g):
    with Phase(nc, "comb") as ph:
        di = ph.sb("di", [P, 2, NT], I32)
        wts = ph.sb("wts", [P, 2, NT])
        idx = ph.sb("idx", [P, 2], I32)
        xt = ph.sb("xt", [P, D])
        y = [ph.sb(f"y{k}", [P, D]) for k in range(2)]
        acc = ph.sb("acc", [P, D])
        o = ph.sb("o", [P, D])
        const_in, x_in, y_in, o_st, passed = (ph.sem(n) for n in ("const_in", "x_in", "y_in", "o_st", "passed"))
        dve = ph.steps("dve", "sum")
        blk = ph.block()

        @blk.sync
        def _(sp):
            sp.dma_start(di[:, :, :], dests).then_inc(const_in, 16)
            sp.dma_start(wts[:, :, :], weights).then_inc(const_in, 16)
            sp.sem_inc(o_st, 16)
            with sp.Fori(0, NT) as t:
                sp.wait_ge(dve.sem, dve.start(t))
                sp.dma_start(xt[:, :], x[bass.ds(t * P, P), :]).then_inc(x_in, 16)
                sp.wait_ge(dve.sem, dve.at("sum", t))
                sp.sem_inc(passed, 1)
                sp.dma_start(out[bass.ds(t * P, P), :], o[:, :]).then_inc(o_st, 16)
            sp.wait_ge(o_st, 16 * (NT + 1))

        @blk.gpsimd
        def _(pool):
            pool.wait_ge(const_in, 32)
            with pool.Fori(0, NT) as t:
                pool.wait_ge(dve.sem, dve.start(t))
                pool.tensor_copy(idx[:, :], di[:, :, bass.ds(t, 1)].rearrange("p k o -> p (k o)"))
                pool.drain()
                for k in range(2):
                    pool.indirect_dma_start(out=y[k][:, :], out_offset=None, in_=ybuf, in_offset=bass.IndirectOffsetOnAxis(
                        ap=idx[:, k:k + 1].bitcast(U32), axis=0)).then_inc(y_in, 16)
                pool.wait_ge(y_in, 32 * t + 32)

        @blk.vector
        def _(ve):
            ve.wait_ge(const_in, 32)
            dve.begin(ve)
            with ve.Fori(0, NT) as t:
                one = bass.ds(t, 1)
                ve.drain()
                ve.wait_ge(x_in, 16 * t + 16)
                ve.wait_ge(y_in, 32 * t + 32)
                ve.scalar_tensor_tensor(acc[:, :], y[0][:, :], wts[:, 0, one], xt[:, :], ALU.mult, ALU.add)
                ve.drain()
                ve.wait_ge(o_st, 16 * t + 16)
                ve.scalar_tensor_tensor(o[:, :], y[1][:, :], wts[:, 1, one], acc[:, :], ALU.mult, ALU.add)\
                    .then_inc(dve.sem, dve.step("sum"))
                ve.drain()


RWKV_IN, DIFF_IN = 0, RWKV_COLS
GATES_IN = RWKV_COLS + 3 * 512


def build_program(nc, g, out):
    def scratch(name, shape, dt=F32):
        return nc.dram_tensor(f"scratch_{name}", shape, dt).ap()

    x0 = g["x"]
    w_in, w_in2 = g["w_in"], g["w_in_2"]
    proj = scratch("proj", (1 + SEQ, w_in.shape[1]))
    norm_project(nc, "pin", x0, g["norm_mix"], w_in, 448, proj, 1, g["ident"])
    tokens = proj[1:, :]
    o_rwkv = scratch("o_rwkv", (SEQ, RW))
    o_diff = scratch("o_diff", (SEQ, AH * AV))
    rwkv(nc, proj, o_rwkv, g["rwkv_masks"], g)
    attention(nc, tokens, DIFF_IN, o_diff, g)
    x1 = scratch("x1", (SEQ, D))
    mix_branches(nc, x0, tokens, GATES_IN, o_rwkv, o_diff, x1, g)

    hbuf = scratch("hbuf", (SEQ, D))
    buf_tok = scratch("buf_tok", ((N_BLOCKS + 2) * P, 1), I32)
    dests = scratch("dests", (P, 2, NT), I32)
    weights = scratch("weights", (P, 2, NT))
    blk_e = scratch("blk_e", (N_BLOCKS, 1), I32)
    n_pairs = scratch("n_pairs", (1, 1), I32)
    ybuf = scratch("ybuf", (N_BLOCKS * P, D))
    x2 = scratch("x2", (SEQ, D))
    route(nc, x1, hbuf, buf_tok, ybuf, dests, weights, blk_e, n_pairs, g["route_consts"], g["token_ids"], g)
    experts(nc, hbuf, buf_tok, blk_e, n_pairs, ybuf, g["ident"], g)
    combine(nc, x1, ybuf, dests, weights, x2, g)
    x3 = scratch("x3", (SEQ, D))
    ple(nc, x2, g["p"], x3, g)

    proj2 = scratch("proj2", (SEQ, w_in2.shape[1]))
    norm_project(nc, "pin2", x3, g["pre_norm_w_2"], w_in2, 353, proj2, 0, g["ident"])
    y_ssd = scratch("y_ssd", (SEQ, SW))
    y_hgrn = scratch("y_hgrn", (SEQ, HH * HD))
    y_s5 = scratch("y_s5", (SEQ, S5W))
    ssd(nc, proj2, y_ssd, g["ssd_masks"], g)
    hgrn(nc, proj2, y_hgrn, g["hgrn_masks"], g)
    s5(nc, proj2, y_s5, g)
    mix_out(nc, x3, [y_ssd, y_hgrn, y_s5], out, g)


def constants():
    rows, cols = np.arange(P)[:, None], np.arange(P)[None, :]
    return {
        "ident": np.eye(P, dtype=np.float32),
        "causal": np.where(cols <= rows, 0, NEG).astype(np.float32),
        "rope": rope_consts(),
        "rwkv_masks": rwkv_masks()[1],
        "ind64": (rows // 64 == np.arange(2)).astype(np.float32),
        "ssd_masks": ssd_masks(),
        "hgrn_masks": hgrn_masks(),
        "ind32": (rows // 32 == np.arange(4)).astype(np.float32),
        "route_consts": route_consts(),
        "token_ids": token_ids(),
    }


def kernel(**inputs):
    import concourse.bacc as bacc
    from concourse.bass_utils import run_bass_kernel_spmd

    nc = bacc.Bacc("TRN2", target_bir_lowering=False, num_devices=1)
    arrays, g = {}, {}
    inputs = {n: a for n, a in inputs.items() if n != "hgrn_lower_bounds_2"}
    for source, own in ((inputs, False), (constants(), True)):
        for name, a in source.items():
            a = np.ascontiguousarray(a)
            if not own:
                a = a[0, 0] if name == "p" else a[0]
            key = f"in_{name}"
            arrays[key] = a
            g[name] = nc.dram_tensor(key, a.shape, mybir.dt.from_np(a.dtype), kind="ExternalInput").ap()
    out = nc.dram_tensor("out_0", (SEQ, D), F32, kind="ExternalOutput").ap()
    build_program(nc, g, out)
    r = run_bass_kernel_spmd(nc, [arrays], core_ids=[0])
    return r.results[0]["out_0"].reshape(1, SEQ, D)
```
